# Optimizing a Trainium2 kernel written in Bass

```python
import jax, jax.numpy as jnp
from jax import lax
import numpy as np
import math

D_MODEL = 1024
BATCH = 1
SEQ = 512
DEPTH = 1

MLA_HEADS = 8
MLA_NOPE = 64
MLA_ROPE = 32
MLA_V = 64
MLA_Q_LORA = 512
MLA_KV_LORA = 256
DIL_HEADS = 8
DIL_HEAD_DIM = 64
DIL_PATTERNS = ((128, 1), (512, 4), (2048, 16))
DIL_WIDTH = DIL_HEADS * DIL_HEAD_DIM
MIX_WIDTH = MLA_HEADS * MLA_V + DIL_WIDTH
IN_COLS = MLA_Q_LORA + MLA_KV_LORA + MLA_ROPE + 3 * DIL_WIDTH
SPLITS = (MLA_Q_LORA,
          MLA_Q_LORA + MLA_KV_LORA,
          MLA_Q_LORA + MLA_KV_LORA + MLA_ROPE,
          MLA_Q_LORA + MLA_KV_LORA + MLA_ROPE + DIL_WIDTH,
          MLA_Q_LORA + MLA_KV_LORA + MLA_ROPE + 2 * DIL_WIDTH)
D_FF = 2816
CONV_WIDTH = 3
ROPE_THETA = 10000.0
EPS = 1e-6
Q_BLOCK = 128
NEG_INF = -1e30


def rms_norm(x, g):
    xf = x.astype(jnp.float32)
    y = xf * lax.rsqrt(jnp.mean(xf * xf, axis=-1, keepdims=True) + EPS)
    return (y * g.astype(jnp.float32)).astype(x.dtype)

def rope(x, positions):
    d = x.shape[-1]
    half = d // 2
    inv_freq = jnp.power(ROPE_THETA, -2.0 * jnp.arange(half, dtype=jnp.float32) / d)
    ang = positions.astype(jnp.float32)[:, :, None, None] * inv_freq
    cos, sin = jnp.cos(ang), jnp.sin(ang)
    xf = x.astype(jnp.float32)
    x1, x2 = xf[..., :half], xf[..., half:]
    return jnp.concatenate([x1 * cos - x2 * sin, x1 * sin + x2 * cos], axis=-1).astype(x.dtype)

def causal_dense_attention(q, k, v, scale):
    B, S, H, Dk = q.shape
    Dv = v.shape[-1]
    nb = S // Q_BLOCK
    qb = q.reshape(B, nb, Q_BLOCK, H, Dk).transpose(1, 0, 2, 3, 4)
    kpos = jnp.arange(S)

    def one_block(args):
        qi, i = args
        s = jnp.einsum('bqhd,bkhd->bhqk', qi, k).astype(jnp.float32) * scale
        qpos = i * Q_BLOCK + jnp.arange(Q_BLOCK)
        mask = kpos[None, :] <= qpos[:, None]
        s = jnp.where(mask, s, NEG_INF)
        p = jax.nn.softmax(s, axis=-1).astype(v.dtype)
        return jnp.einsum('bhqk,bkhd->bqhd', p, v)

    out = lax.map(one_block, (qb, jnp.arange(nb)))
    return out.transpose(1, 0, 2, 3, 4).reshape(B, S, H, Dv)

def banded_causal_attention(q, k, v, span):
    N, L, H, D = q.shape
    blk = span
    nb = -(-L // blk)
    Lp = nb * blk
    pad = ((0, 0), (0, Lp - L), (0, 0), (0, 0))
    q, k, v = jnp.pad(q, pad), jnp.pad(k, pad), jnp.pad(v, pad)
    qb = q.reshape(N, nb, blk, H, D)

    def two_blocks(t):
        tb = jnp.pad(t, ((0, 0), (blk, 0), (0, 0), (0, 0))).reshape(N, nb + 1, blk, H, D)
        return jnp.concatenate([tb[:, :-1], tb[:, 1:]], axis=2)

    kb, vb = two_blocks(k), two_blocks(v)
    s = jnp.einsum('nbqhd,nbkhd->nbhqk', qb, kb).astype(jnp.float32) * (D ** -0.5)
    blk_idx = jnp.arange(nb)[:, None, None]
    qry_pos = blk_idx * blk + jnp.arange(blk)[None, :, None]
    key_pos = (blk_idx - 1) * blk + jnp.arange(2 * blk)[None, None, :]
    dist = qry_pos - key_pos
    mask = (dist >= 0) & (dist <= span) & (key_pos >= 0)
    s = jnp.where(mask[None, :, None], s, NEG_INF)
    m = jnp.max(s, axis=-1, keepdims=True)
    e = jnp.exp(s - m)
    denom = jnp.sum(e, axis=-1, keepdims=True)
    p = (e / denom).astype(v.dtype)
    o = jnp.einsum('nbhqk,nbkhd->nbqhd', p, vb).reshape(N, Lp, H, D)[:, :L]
    lse = (m + jnp.log(denom))[..., 0]
    lse = lse.transpose(0, 1, 3, 2).reshape(N, Lp, H)[:, :L]
    return o, lse

def to_strided(t, dil):
    B, S, H, D = t.shape
    return t.reshape(B, S // dil, dil, H, D).transpose(0, 2, 1, 3, 4).reshape(B * dil, S // dil, H, D)

def dilated_attention(q, k, v):
    B, S, H, D = q.shape
    outs, lses = [], []
    for window, dil in DIL_PATTERNS:
        L = S // dil
        o, lse = banded_causal_attention(to_strided(q, dil), to_strided(k, dil),
                                         to_strided(v, dil), window // dil)
        outs.append(o.reshape(B, dil, L, H, D).transpose(0, 2, 1, 3, 4).reshape(B, S, H, D))
        lses.append(lse.reshape(B, dil, L, H).transpose(0, 2, 1, 3).reshape(B, S, H))
    w = jax.nn.softmax(jnp.stack(lses, axis=0), axis=0)
    out = jnp.sum(w[..., None] * jnp.stack(outs, axis=0).astype(jnp.float32), axis=0)
    return out.astype(q.dtype)

def causal_depthwise_conv(u, w, b):
    K = w.shape[0]
    S = u.shape[1]
    up = jnp.pad(u, ((0, 0), (K - 1, 0), (0, 0)))
    y = b
    for kk in range(K):
        y = y + up[:, kk:kk + S] * w[kk]
    return y

def first_inputs(seed: int = 0) -> dict:
    key = jax.random.key(seed)
    ks = jax.random.split(key, 24)
    nrm = jax.random.normal
    L = DEPTH

    def gain(k, n):
        return 1.0 + 0.05 * nrm(k, (L, n), jnp.float32)

    x = nrm(ks[0], (BATCH, SEQ, D_MODEL), jnp.float32)
    c = nrm(ks[1], (BATCH, D_MODEL), jnp.float32)
    positions = (jnp.arange(SEQ, dtype=jnp.int32)[None, :]
                 + jax.random.randint(ks[2], (BATCH, 1), 0, 4096, dtype=jnp.int32))
    return {
        "x": x,
        "c": c,
        "positions": positions,
        "w_ada": nrm(ks[3], (L, D_MODEL, 6 * D_MODEL), jnp.float32) * (0.5 * D_MODEL ** -0.5),
        "b_ada": 0.02 * nrm(ks[4], (L, 6 * D_MODEL), jnp.float32),
        "g_mix_norm": gain(ks[5], D_MODEL),
        "w_in": nrm(ks[6], (L, D_MODEL, IN_COLS), jnp.float32) * D_MODEL ** -0.5,
        "g_q_lat": gain(ks[7], MLA_Q_LORA),
        "w_q_b": nrm(ks[8], (L, MLA_Q_LORA, MLA_HEADS * (MLA_NOPE + MLA_ROPE)), jnp.float32) * MLA_Q_LORA ** -0.5,
        "g_kv_lat": gain(ks[9], MLA_KV_LORA),
        "w_kv_b": nrm(ks[10], (L, MLA_KV_LORA, MLA_HEADS * (MLA_NOPE + MLA_V)), jnp.float32) * MLA_KV_LORA ** -0.5,
        "g_mla_q_nope": gain(ks[11], MLA_NOPE),
        "g_mla_q_pe": gain(ks[12], MLA_ROPE),
        "g_mla_k_nope": gain(ks[13], MLA_NOPE),
        "g_mla_k_pe": gain(ks[14], MLA_ROPE),
        "g_dil_q": gain(ks[15], DIL_HEAD_DIM),
        "g_dil_k": gain(ks[16], DIL_HEAD_DIM),
        "w_o": nrm(ks[17], (L, MIX_WIDTH, D_MODEL), jnp.float32) * MIX_WIDTH ** -0.5,
        "g_ffn_norm": gain(ks[18], D_MODEL),
        "w_up": nrm(ks[19], (L, D_MODEL, 2 * D_FF), jnp.float32) * D_MODEL ** -0.5,
        "w_conv": nrm(ks[20], (L, CONV_WIDTH, 2 * D_FF), jnp.float32) * CONV_WIDTH ** -0.5,
        "b_conv": 0.02 * nrm(ks[21], (L, 2 * D_FF), jnp.float32),
        "w_down": nrm(ks[22], (L, D_FF, D_MODEL), jnp.float32) * D_FF ** -0.5,
    }

def first_block(x, c, positions, w_ada, b_ada, g_mix_norm, w_in, g_q_lat, w_q_b, g_kv_lat, w_kv_b,
              g_mla_q_nope, g_mla_q_pe, g_mla_k_nope, g_mla_k_pe, g_dil_q, g_dil_k, w_o,
              g_ffn_norm, w_up, w_conv, b_conv, w_down):
    B, S, _ = x.shape
    for l in range(DEPTH):
        mod = jax.nn.silu(c) @ w_ada[l] + b_ada[l]
        sh1, sc1, g1, sh2, sc2, g2 = jnp.split(mod, 6, axis=-1)

        h = rms_norm(x, g_mix_norm[l]) * (1.0 + sc1[:, None]) + sh1[:, None]
        proj = h @ w_in[l]
        q_lat, kv_lat, k_pe, qd, kd, vd = jnp.split(proj, SPLITS, axis=-1)

        q = (rms_norm(q_lat, g_q_lat[l]) @ w_q_b[l]).reshape(B, S, MLA_HEADS, MLA_NOPE + MLA_ROPE)
        q_nope = rms_norm(q[..., :MLA_NOPE], g_mla_q_nope[l])
        q_pe = rope(rms_norm(q[..., MLA_NOPE:], g_mla_q_pe[l]), positions)
        kv = (rms_norm(kv_lat, g_kv_lat[l]) @ w_kv_b[l]).reshape(B, S, MLA_HEADS, MLA_NOPE + MLA_V)
        k_nope = rms_norm(kv[..., :MLA_NOPE], g_mla_k_nope[l])
        v_mla = kv[..., MLA_NOPE:]
        k_pe = rope(rms_norm(k_pe, g_mla_k_pe[l])[:, :, None, :], positions)
        k_mla = jnp.concatenate([k_nope, jnp.broadcast_to(k_pe, (B, S, MLA_HEADS, MLA_ROPE))], axis=-1)
        q_mla = jnp.concatenate([q_nope, q_pe], axis=-1)
        o_mla = causal_dense_attention(q_mla, k_mla, v_mla, (MLA_NOPE + MLA_ROPE) ** -0.5)

        qd = rope(rms_norm(qd.reshape(B, S, DIL_HEADS, DIL_HEAD_DIM), g_dil_q[l]), positions)
        kd = rope(rms_norm(kd.reshape(B, S, DIL_HEADS, DIL_HEAD_DIM), g_dil_k[l]), positions)
        vd = vd.reshape(B, S, DIL_HEADS, DIL_HEAD_DIM)
        o_dil = dilated_attention(qd, kd, vd)

        mix = jnp.concatenate([o_mla.reshape(B, S, MLA_HEADS * MLA_V),
                               o_dil.reshape(B, S, DIL_WIDTH)], axis=-1) @ w_o[l]
        x = x + g1[:, None] * mix

        h2 = rms_norm(x, g_ffn_norm[l]) * (1.0 + sc2[:, None]) + sh2[:, None]
        u = causal_depthwise_conv(h2 @ w_up[l], w_conv[l], b_conv[l])
        gate, val = jnp.split(u, 2, axis=-1)
        x = x + g2[:, None] * ((jax.nn.silu(gate) * val) @ w_down[l])
    return x


DEPTH_2 = 2

MIX_WIDTH_2 = D_MODEL
DA_WIDTH = MIX_WIDTH_2 // 2
SC_WIDTH = MIX_WIDTH_2 // 4
LRU_WIDTH = MIX_WIDTH_2 - DA_WIDTH - SC_WIDTH

DA_HEAD_DIM = 64
DA_HEADS = DA_WIDTH // (2 * DA_HEAD_DIM)
NUM_BUCKETS = 32
MAX_DISTANCE = 128
SUBLN_EPS = 1e-5

SC_KERNEL = 3

LRU_BLOCKS = 4
LRU_BLOCK = LRU_WIDTH // LRU_BLOCKS
LRU_CONV = 4
LRU_C = 8.0

RMS_EPS = 1e-6
NEG_INF_2 = -1e30

IN_SPLIT_WIDTHS = (DA_WIDTH, DA_WIDTH, DA_WIDTH,
                   SC_WIDTH, SC_WIDTH, SC_WIDTH,
                   LRU_WIDTH, LRU_WIDTH)
IN_WIDTH = sum(IN_SPLIT_WIDTHS)
IN_SPLIT_POINTS = tuple(int(v) for v in np.cumsum(IN_SPLIT_WIDTHS)[:-1])


def rms_norm_2(x, g, eps=RMS_EPS):
    xf = x.astype(jnp.float32)
    y = xf * lax.rsqrt(jnp.mean(xf * xf, axis=-1, keepdims=True) + eps)
    return (y * g.astype(jnp.float32)).astype(x.dtype)

def swiglu(x, w_gate, w_up, w_down):
    return (jax.nn.silu(x @ w_gate) * (x @ w_up)) @ w_down

def causal_dwconv(x, w):
    K = w.shape[0]
    S = x.shape[1]
    xp = jnp.pad(x, ((0, 0), (K - 1, 0), (0, 0)))
    return sum(xp[:, k:k + S] * w[k] for k in range(K))

def t5_bucket(n):
    max_exact = NUM_BUCKETS // 2
    nf = jnp.maximum(n, 1).astype(jnp.float32)
    large = max_exact + (jnp.log(nf / max_exact) / math.log(MAX_DISTANCE / max_exact)
                         * (NUM_BUCKETS - max_exact)).astype(jnp.int32)
    large = jnp.minimum(large, NUM_BUCKETS - 1)
    return jnp.where(n < max_exact, n, large)

def diff_attention(q, k, v, lq1, lk1, lq2, lk2, subln_g, rel_bias, lam_init):
    B, S, _ = q.shape
    nblk = S // Q_BLOCK
    q = q.reshape(B, S, DA_HEADS, 2, DA_HEAD_DIM) * (DA_HEAD_DIM ** -0.5)
    k = k.reshape(B, S, DA_HEADS, 2, DA_HEAD_DIM)
    v = v.reshape(B, S, DA_HEADS, 2 * DA_HEAD_DIM)
    f32 = jnp.float32
    lam = (jnp.exp(jnp.sum(lq1.astype(f32) * lk1.astype(f32)))
           - jnp.exp(jnp.sum(lq2.astype(f32) * lk2.astype(f32))) + lam_init)
    k_pos = jnp.arange(S)
    q_blocks = jnp.moveaxis(q.reshape(B, nblk, Q_BLOCK, DA_HEADS, 2, DA_HEAD_DIM), 1, 0)

    def block(args):
        qb, start = args
        q_pos = start + jnp.arange(Q_BLOCK)
        dist = q_pos[:, None] - k_pos[None, :]
        bias = rel_bias[t5_bucket(jnp.maximum(dist, 0))]
        bias = bias.reshape(Q_BLOCK, S, DA_HEADS, 2).transpose(2, 3, 0, 1).astype(f32)
        logits = jnp.einsum('bqhmd,bkhmd->bhmqk', qb, k).astype(f32) + bias
        logits = jnp.where(dist >= 0, logits, NEG_INF_2)
        p = jax.nn.softmax(logits, axis=-1)
        attn = p[:, :, 0] - lam * p[:, :, 1]
        return jnp.einsum('bhqk,bkhe->bqhe', attn.astype(v.dtype), v)

    starts = jnp.arange(nblk) * Q_BLOCK
    o = lax.map(block, (q_blocks, starts))
    o = jnp.moveaxis(o, 0, 1).reshape(B, S, DA_HEADS, 2 * DA_HEAD_DIM)
    o = rms_norm_2(o, subln_g, SUBLN_EPS) * (1.0 - lam_init)
    return o.reshape(B, S, DA_WIDTH)

def block_diag_linear(x, w, b):
    B, S, _ = x.shape
    xb = x.reshape(B, S, LRU_BLOCKS, LRU_BLOCK)
    y = jnp.einsum('bsni,nij->bsnj', xb, w) + b
    return y.reshape(B, S, LRU_WIDTH)

def rg_lru(x, wa, ba, wx, bx, lam):
    f32 = jnp.float32
    r = jax.nn.sigmoid(block_diag_linear(x, wa, ba)).astype(f32)
    i = jax.nn.sigmoid(block_diag_linear(x, wx, bx)).astype(f32)
    log_a = -LRU_C * r * jax.nn.softplus(-lam.astype(f32))
    a = jnp.exp(log_a)
    mult = jnp.sqrt(-jnp.expm1(2.0 * log_a))
    b = mult * (i * x.astype(f32))

    def combine(e, l):
        return (e[0] * l[0], l[0] * e[1] + l[1])

    _, h = lax.associative_scan(combine, (a, b), axis=1)
    return h.astype(x.dtype)

def second_inputs(seed: int = 0) -> dict:
    key = jax.random.key(seed)
    ks = iter(jax.random.split(key, 40))
    f32 = jnp.float32

    def nrm(shape, fan_in):
        return jax.random.normal(next(ks), shape, f32) * fan_in ** -0.5

    def gain(shape):
        return 1.0 + 0.02 * jax.random.normal(next(ks), shape, f32)

    def small(shape, s):
        return s * jax.random.normal(next(ks), shape, f32)

    u = jax.random.uniform(next(ks), (DEPTH_2, LRU_WIDTH), f32, minval=0.9, maxval=0.999)
    a0 = u ** (1.0 / LRU_C)
    lru_lambda = jnp.log(a0) - jnp.log1p(-a0)

    return {
        "x": jax.random.normal(next(ks), (BATCH, SEQ, D_MODEL), f32),
        "rel_bias": small((NUM_BUCKETS, 2 * DA_HEADS), 0.5),
        "ffn1_norm": gain((DEPTH_2, D_MODEL)),
        "ffn1_gate": nrm((DEPTH_2, D_MODEL, D_FF), D_MODEL),
        "ffn1_up": nrm((DEPTH_2, D_MODEL, D_FF), D_MODEL),
        "ffn1_down": nrm((DEPTH_2, D_FF, D_MODEL), D_FF),
        "mix_norm": gain((DEPTH_2, D_MODEL)),
        "w_in": nrm((DEPTH_2, D_MODEL, IN_WIDTH), D_MODEL),
        "w_out": nrm((DEPTH_2, MIX_WIDTH_2, D_MODEL), MIX_WIDTH_2),
        "lam_q1": small((DEPTH_2, DA_HEAD_DIM), 0.1),
        "lam_k1": small((DEPTH_2, DA_HEAD_DIM), 0.1),
        "lam_q2": small((DEPTH_2, DA_HEAD_DIM), 0.1),
        "lam_k2": small((DEPTH_2, DA_HEAD_DIM), 0.1),
        "subln_gain": gain((DEPTH_2, 2 * DA_HEAD_DIM)),
        "sc_conv_w": nrm((DEPTH_2, SC_KERNEL, SC_WIDTH), SC_KERNEL),
        "lru_conv_w": nrm((DEPTH_2, LRU_CONV, LRU_WIDTH), LRU_CONV),
        "lru_conv_b": small((DEPTH_2, LRU_WIDTH), 0.01),
        "lru_wa": nrm((DEPTH_2, LRU_BLOCKS, LRU_BLOCK, LRU_BLOCK), LRU_BLOCK),
        "lru_ba": small((DEPTH_2, LRU_BLOCKS, LRU_BLOCK), 0.01),
        "lru_wx": nrm((DEPTH_2, LRU_BLOCKS, LRU_BLOCK, LRU_BLOCK), LRU_BLOCK),
        "lru_bx": small((DEPTH_2, LRU_BLOCKS, LRU_BLOCK), 0.01),
        "lru_lambda": lru_lambda,
        "ffn2_norm": gain((DEPTH_2, D_MODEL)),
        "ffn2_gate": nrm((DEPTH_2, D_MODEL, D_FF), D_MODEL),
        "ffn2_up": nrm((DEPTH_2, D_MODEL, D_FF), D_MODEL),
        "ffn2_down": nrm((DEPTH_2, D_FF, D_MODEL), D_FF),
        "final_norm": gain((D_MODEL,)),
    }

def second_block(x, rel_bias, ffn1_norm, ffn1_gate, ffn1_up, ffn1_down, mix_norm, w_in, w_out,
              lam_q1, lam_k1, lam_q2, lam_k2, subln_gain, sc_conv_w, lru_conv_w, lru_conv_b,
              lru_wa, lru_ba, lru_wx, lru_bx, lru_lambda, ffn2_norm, ffn2_gate, ffn2_up,
              ffn2_down, final_norm):
    for l in range(DEPTH_2):
        h = x + 0.5 * swiglu(rms_norm_2(x, ffn1_norm[l]), ffn1_gate[l], ffn1_up[l], ffn1_down[l])

        u = rms_norm_2(h, mix_norm[l])
        z = u @ w_in[l]
        q, k, v, sc_b, sc_c, sc_x, lru_x, lru_g = jnp.split(z, IN_SPLIT_POINTS, axis=-1)

        lam_init = 0.8 - 0.6 * math.exp(-0.3 * l)
        y_da = diff_attention(q, k, v, lam_q1[l], lam_k1[l], lam_q2[l], lam_k2[l],
                              subln_gain[l], rel_bias, lam_init)
        y_sc = sc_b * causal_dwconv(sc_c * sc_x, sc_conv_w[l])
        xr = causal_dwconv(lru_x, lru_conv_w[l]) + lru_conv_b[l]
        y_lru = jax.nn.gelu(lru_g) * rg_lru(xr, lru_wa[l], lru_ba[l], lru_wx[l], lru_bx[l],
                                            lru_lambda[l])

        h = h + jnp.concatenate([y_da, y_sc, y_lru], axis=-1) @ w_out[l]

        x = h + 0.5 * swiglu(rms_norm_2(h, ffn2_norm[l]), ffn2_gate[l], ffn2_up[l], ffn2_down[l])
    return rms_norm_2(x, final_norm)


def setup_inputs(seed=0):
    out = dict(first_inputs(seed))
    for name, value in second_inputs(seed + 1).items():
        if name != "x":
            out[name + "_2"] = value
    return out


def reference(
    x, c, positions, w_ada, b_ada, g_mix_norm, w_in, g_q_lat, w_q_b, g_kv_lat, w_kv_b,
    g_mla_q_nope, g_mla_q_pe, g_mla_k_nope, g_mla_k_pe, g_dil_q, g_dil_k, w_o, g_ffn_norm, w_up,
    w_conv, b_conv, w_down, rel_bias_2, ffn1_norm_2, ffn1_gate_2, ffn1_up_2, ffn1_down_2,
    mix_norm_2, w_in_2, w_out_2, lam_q1_2, lam_k1_2, lam_q2_2, lam_k2_2, subln_gain_2,
    sc_conv_w_2, lru_conv_w_2, lru_conv_b_2, lru_wa_2, lru_ba_2, lru_wx_2, lru_bx_2,
    lru_lambda_2, ffn2_norm_2, ffn2_gate_2, ffn2_up_2, ffn2_down_2, final_norm_2,
):
    x = first_block(
        x, c, positions, w_ada, b_ada, g_mix_norm, w_in, g_q_lat, w_q_b, g_kv_lat, w_kv_b,
        g_mla_q_nope, g_mla_q_pe, g_mla_k_nope, g_mla_k_pe, g_dil_q, g_dil_k, w_o, g_ffn_norm,
        w_up, w_conv, b_conv, w_down,
    )
    return second_block(
        x, rel_bias_2, ffn1_norm_2, ffn1_gate_2, ffn1_up_2, ffn1_down_2, mix_norm_2, w_in_2,
        w_out_2, lam_q1_2, lam_k1_2, lam_q2_2, lam_k2_2, subln_gain_2, sc_conv_w_2,
        lru_conv_w_2, lru_conv_b_2, lru_wa_2, lru_ba_2, lru_wx_2, lru_bx_2, lru_lambda_2,
        ffn2_norm_2, ffn2_gate_2, ffn2_up_2, ffn2_down_2, final_norm_2,
    )


_drawn_inputs = setup_inputs


def setup_inputs(seed=0):
    import zlib

    import numpy as np

    out = dict(_drawn_inputs(seed))
    spreads = {}
    factors = {'g_mix_norm': 5.883,
     'g_q_lat': 8.0,
     'g_kv_lat': 3.434,
     'g_mla_q_nope': 8.0,
     'g_mla_q_pe': 8.0,
     'g_mla_k_nope': 8.0,
     'g_mla_k_pe': 8.0,
     'g_dil_q': 8.0,
     'g_dil_k': 8.0,
     'b_conv': 4.054,
     'ffn1_norm_2': 4.244,
     'lam_k1_2': 5.199,
     'lam_k2_2': 8.0,
     'subln_gain_2': 20.081,
     'lru_conv_b_2': 113.392,
     'lru_ba_2': 200.0,
     'lru_bx_2': 200.0,
     'ffn2_norm_2': 6.284,
     'final_norm_2': 20.871,
     'lru_wa_2': 28.008,
     'lru_lambda_2': 25.312,
     'lru_conv_w_2': 8.0,
     'lru_wx_2': 8.0}
    for name, (base, spread) in spreads.items():
        noise = np.random.default_rng([zlib.crc32(name.encode()), seed]).standard_normal(out[name].shape)
        drawn = base * np.exp(spread * noise) if base else spread * noise
        out[name] = __import__('jax').numpy.asarray(drawn.astype(out[name].dtype))
    for name, factor in factors.items():
        out[name] = (out[name] * factor).astype(out[name].dtype)
    return out
```

```python
from contextlib import ExitStack
import math

import numpy as np

import concourse.bass as bass
from concourse import mybir
from concourse.alu_op_type import AluOpType as ALU

ACT = mybir.ActivationFunctionType
F32 = mybir.dt.float32
F32R = mybir.dt.float32r
I32 = mybir.dt.int32
P = 128
S = 512
D = 1024
DT = D // P
FF = 2816
FT = FF // P
HALF = FT // 2
UB = 16
LAYERS = 2
NEG = -1e30
TILE = S * 4

U_ADA, U_IN1, U_QB, U_KVB, U_O = 24, 10, 2, 1, 4
U_PAIR, U_DOWN, U_IN2 = 2, 12, 12
U_LAYER = 2 * (U_PAIR * HALF + U_DOWN) + U_IN2 + U_O
U_FIRST = U_ADA + U_IN1 + U_QB + U_KVB + U_O + U_PAIR * HALF + U_DOWN
U_PAD = U_FIRST % 2
U_ALL = U_FIRST + U_PAD + LAYERS * U_LAYER + 2


def column_plan():
    at, n = {}, 0
    for name, w in (("c", 8), ("b_ada", 48), ("g_mix", 8), ("g_q_lat", 4), ("g_kv_lat", 2), ("g_q", 1),
                    ("g_k", 1), ("g_dq", 1), ("g_dk", 1), ("g_ffn", 8), ("w_conv0", 44), ("w_conv1", 44),
                    ("w_conv2", 44), ("b_conv", 44), ("final", 8), ("freq_dil", 1), ("freq_mla", 1)):
        at[name] = n
        n += w
    return at, n


def layer_plan():
    at, n = {}, 0
    for name, w in (("ffn1", 8), ("mix", 8), ("ffn2", 8), ("subln", 1), ("sc_w", 6), ("lru_w", 8),
                    ("lru_b", 2), ("lambda", 2), ("ba", 2), ("bx", 2), ("lam", 4), ("lam_init", 1),
                    ("sub_scale", 1)):
        at[name] = n
        n += w
    return at, n


COL, NCOL = column_plan()
LCOL, NLCOL = layer_plan()
CONST = {name: n * P for n, name in enumerate(("ident", "ones", "blk64", "blkq", "perm64", "permq"))}


class Token:

    def __init__(self, sem, value, loops, lag=None, units=0):
        self.sem, self.value, self.loops, self.lag, self.units = sem, value, loops, lag, units


class Loop:
    def __init__(self, n):
        self.n, self.i, self.open = n, None, True
        self.per, self.marks, self.used = {}, {}, set()


class Program:

    def __init__(self, nc, ctx):
        self.nc, self.ctx = nc, ctx
        self.eng = {"pe": nc.tensor, "act": nc.scalar, "dve": nc.vector, "pool": nc.gpsimd, "sp": nc.sync}
        self.sems, self.count, self.known = {}, {}, {}
        self.loops, self.scopes, self.dry = [], [{}], False

    def sem(self, name):
        if name not in self.sems:
            self.sems[name] = self.ctx.enter_context(self.nc.semaphore("s_" + name))
            self.count[name] = 0
        return self.sems[name]

    def value(self, t):
        v = t.value
        for L in t.loops:
            per = L.per.get("use", 0) * t.units if t.units else L.per.get(t.sem, 0)
            v = L.i * per + v if L.open and per else v + ((L.n - 1) * per if not L.open else 0)
            if t.lag is L:
                v = v - per
        return v

    def first_turn(self, t):
        v = t.value
        for L in t.loops:
            per = L.per.get("use", 0) * t.units if t.units else L.per.get(t.sem, 0)
            v += (L.n - 1) * per if not L.open else 0
            v -= per if t.lag is L else 0
        return v

    def resolve(self, name, engine):
        for depth in range(len(self.scopes) - 1, -1, -1):
            if name in self.scopes[depth]:
                return self.scopes[depth][name]
            if depth:
                L = self.loops[depth - 1]
                if self.dry:
                    L.used.add((engine, name))
                elif name in L.marks:
                    return [Token(t.sem, t.value, t.loops, L) for t in L.marks[name]]
        return []

    def wait(self, engine, *waits, apart=True):
        if self.dry:
            for w in waits:
                if not isinstance(w, Token):
                    self.resolve(w, engine)
            return
        e, latest = self.eng[engine], {}
        self.sem("spare_" + engine)
        for w in waits:
            for t in ([w] if isinstance(w, Token) else self.resolve(w, engine)):
                v = self.value(t)
                key = (t.sem, not isinstance(v, int), tuple(id(L) for L in t.loops if L.open))
                first = self.value(t) if isinstance(v, int) else self.first_turn(t)
                if key not in latest or latest[key][0] < first:
                    latest[key] = (first, v)
        by_register, waited = False, set()
        for (sem, register, _), (first, v) in sorted(latest.items(), key=lambda kv: kv[0][1]):
            if register:
                if sem in waited:
                    e.sem_inc(self.sem("spare_" + engine), 1)
                waited.add(sem)
                assert first > 0, (engine, sem, first)
                by_register = True
            elif v <= self.known.get((engine, sem), 0):
                continue
            else:
                self.known[engine, sem] = v
            e.wait_ge(self.sem(sem), v)
        if by_register and apart:
            e.sem_inc(self.sem("spare_" + engine), 1)

    def run(self, engine, make, *waits, sem=None, by=1, mark=None, apart=False):
        name = sem or engine
        self.sem(name)
        self.wait(engine, *waits, apart=apart or engine == "pool")
        if not self.dry:
            make(self.eng[engine]).then_inc(self.sems[name], by)
        self.count[name] += by
        t = Token(name, self.count[name], tuple(self.loops))
        if mark:
            self.mark(mark, t)
        return t

    def mark(self, name, *tokens):
        self.scopes[-1][name] = list(tokens)

    def pe(self, make, *waits, **kw):
        return self.run("pe", make, *waits, **kw)

    def act(self, make, *waits, **kw):
        return self.run("act", make, *waits, **kw)

    def dve(self, make, *waits, **kw):
        return self.run("dve", make, *waits, **kw)

    def pool(self, make, *waits, **kw):
        return self.run("pool", make, *waits, **kw)

    def dma(self, engine, sem, out, in_, *waits, **kw):
        return self.run(engine, lambda e: e.dma_start(out() if callable(out) else out, in_() if callable(in_) else in_),
                        *waits, sem=sem, by=16, **kw)

    def loop(self, n, body):
        L, start, dry = Loop(n), dict(self.count), self.dry
        for real in ((False,) if dry else (False, True)):
            self.loops.append(L)
            self.scopes.append({})
            if not real:
                self.dry, L.i = True, 0
                body(0)
                self.dry = dry
                L.per = {k: v - start.get(k, 0) for k, v in self.count.items() if v != start.get(k, 0)}
                L.marks = dict(self.scopes[-1])
                for k in self.count:
                    self.count[k] = start.get(k, 0)
            else:
                self.loops.pop()
                scope = self.scopes.pop()
                for engine in sorted({e for e, _ in L.used}):
                    self.wait(engine, *sorted(n for e, n in L.used if e == engine and n in L.marks))
                self.loops.append(L)
                self.scopes.append(scope)
                with self.nc.Fori(0, n) as i:
                    L.i = i
                    body(i)
            scope = self.scopes.pop()
            self.loops.pop()
            if not real and not dry:
                continue
        L.open = False
        for k, v in L.per.items():
            self.count[k] = start.get(k, 0) + n * v
        self.scopes[-1].update(scope)


def build(nc, wstream, x_in, pos_in, cols_in, layer_in, const_in, strip_in, bucket_in, rel_in, lru_in, y_out):
    scratch = nc.dram_tensor("bias_by_distance", (8, 640), F32, kind="Internal").ap()
    strips_dram = nc.dram_tensor("bias_strips", (8, P, S), F32, kind="Internal").ap()
    with ExitStack() as ctx:
        k = Program(nc, ctx)
        top = [-(-nc.sbuf_base // 64) * 64]

        def place(name, shape, dt=F32, at=None):
            if at is None:
                at = top[0]
                top[0] += -(-int(np.prod(shape[1:])) * 4 // 32) * 32
                assert top[0] <= nc.sbuf_usable_end, name
            return nc.alloc_sbuf_tensor_at(name, shape, dt, offset=at)

        raw = [place(f"raw{s}", [P, UB, P]) for s in range(2)]
        whi = [place(f"whi{s}", [P, UB, P], F32R) for s in range(2)]
        wlo = [place(f"wlo{s}", [P, UB, P], F32R) for s in range(2)]
        x = place("x", [P, DT, S])
        ahi = place("ahi", [P, DT, S], F32R)
        alo = place("alo", [P, DT, S], F32R)
        big = top[0]
        hhi = place("hhi", [P, FT, S], F32R)
        hlo = place("hlo", [P, FT, S], F32R)

        def region(name, tile, shape, dt=F32):
            return place(name, shape, dt, at=big + int(tile * TILE))

        const = place("const", [P, len(CONST) * P])
        cols = place("cols", [P, NCOL])
        lc = place("lc", [P, NLCOL])
        mod = place("mod", [P, 48])
        gcol = place("gcol", [P, 16])
        small = place("small", [P, 32])
        chi = place("chi", [P, DT, 2], F32R)
        clo = place("clo", [P, DT, 2], F32R)
        sq = [place(f"sq{s}", [P, S]) for s in range(2)]
        tmp = [place(f"tmp{s}", [P, S]) for s in range(4)]
        rstd = place("rstd", [P, S])
        ps = ctx.enter_context(nc.psum_tensor("ps", [P, 8, S], F32))

        def C(name, w=P):
            return const[:, CONST[name]:CONST[name] + w]

        def col(name, j=0):
            return cols[:, COL[name] + j:COL[name] + j + 1]

        def dcol(name, j):
            return cols[:, bass.ds(j + COL[name], 1)]

        def lcol(name, j=0):
            return lc[:, LCOL[name] + j:LCOL[name] + j + 1]

        EPS, SUB_EPS, HALF_PI, ZERO = (small[:, n:n + 1] for n in range(4))
        k.sem("start")
        k.run("pool", lambda e: e.memset(small[:, 0:1], 1e-6), sem="start")
        k.run("pool", lambda e: e.memset(small[:, 1:2], 1e-5))
        k.run("pool", lambda e: e.memset(small[:, 2:3], math.pi / 2))
        t_small = k.run("pool", lambda e: e.memset(small[:, 3:4], 0.0))
        for e in ("act", "dve", "pe", "sp", "pool"):
            k.wait(e, Token("start", 1, ()), t_small)
        t_cols = k.dma("act", "d_cols", cols[:], cols_in)
        t_const = k.dma("act", "d_const", const[:], const_in)
        t_x = k.dma("act", "d_x", x[:], x_in)

        for s in range(2):
            nc.sync.dma_start(raw[s][:], wstream[s]).then_inc(k.sem(f"ld{s}"), 16)
        k.sem("hi"), k.sem("lo"), k.sem("use")
        with nc.sync.Fori(0, (U_ALL - 2) // 2) as i:
            for s in range(2):
                nc.sync.wait_ge(k.sem("lo"), i * 2 + (s + 1))
                nc.sync.dma_start(raw[s][:], wstream[bass.ds(i * 2 + (2 + s), 1)].rearrange("a p b m -> (a p) b m"))\
                    .then_inc(k.sem(f"ld{s}"), 16)

        def units(sem, value, times=1):
            return Token(sem, value, tuple(k.loops), units=times)

        def split():
            v = k.count["hi"]
            s = v % 2
            waits = [units(f"ld{s}", 16 * (v // 2 + 1), 8)]
            if v >= 2:
                waits.append(units("use", v - 1))
            k.act(lambda e: e.activation(whi[s][:], raw[s][:], ACT.Copy), *waits, sem="hi")
            k.dve(lambda e: e.tensor_tensor(wlo[s][:], raw[s][:], whi[s][:].bitcast(F32), ALU.subtract),
                  units("hi", v + 1), sem="lo")

        def mm3(e, out, s, b, m, rhi, rlo, start, stop):
            wh, wl = whi[s][:, b, 0:m], wlo[s][:, b, 0:m]
            e.matmul(out, wh, rhi, start=start, stop=False)
            e.matmul(out, wl, rhi, start=False, stop=False)
            return e.matmul(out, wh, rlo, start=False, stop=stop)

        def product(blocks, first=(), inputs=None):
            u = k.count["use"]
            s = u % 2

            def make(e):
                ins, seen = None, {blocks[0][-1]}
                for b, out, m, rhi, rlo, start, stop, n in blocks:
                    if inputs and n not in seen:
                        seen.add(n)
                        k.wait("pe", inputs[n])
                    ins = mm3(e, out, s, b, m, rhi, rlo, start, stop)
                return ins
            if inputs:
                first = [*first, inputs[blocks[0][-1]]]
            k.pe(make, units("lo", u + 1), *first, sem="use")
            t = units("use", u + 1)
            split()
            return t

        def bank(b, m=P, n=S, lo=0):
            return ps[lo:lo + m, b, 0:n]

        def hilo(dst_hi, dst_lo, src, *waits, shift=None, mark=None):
            if shift is None:
                t1 = k.act(lambda e: e.activation(dst_hi(), src, ACT.Copy), *waits)
                t2 = k.dve(lambda e: e.tensor_tensor(dst_lo(), src, dst_hi().bitcast(F32), ALU.subtract), t1)
            else:
                t1 = k.act(lambda e: e.activation(dst_hi(), src, ACT.Identity, bias=shift), *waits)
                t2 = k.dve(lambda e: e.scalar_tensor_tensor(dst_lo(), src, shift, dst_hi().bitcast(F32),
                                                            ALU.add, ALU.subtract), t1)
            if mark:
                k.mark(mark, t1, t2)
            return t2

        def norm(src, n, width, gain, shift=None, dst=0, out=None, ready=(), clear=()):
            for j in range(n):
                t = k.act(lambda e: e.activation(sq[j % 2][:], src(j), ACT.Square), f"sq{j % 2}", *ready)
                k.pe(lambda e: e.matmul(bank(7), C("ones"), sq[j % 2][:], start=(j == 0), stop=(j == n - 1)),
                     t, "bank7", t_const, mark=f"sq{j % 2}")
            t = k.act(lambda e: e.activation(rstd[:], bank(7), ACT.Sqrt, bias=EPS, scale=1.0 / width),
                      f"sq{(n - 1) % 2}", "rstd", mark="bank7")
            t_r = k.dve(lambda e: e.reciprocal(rstd[:], rstd[:]), t)
            tokens = []
            for j in range(n):
                if out is not None:
                    t = k.dve(lambda e: e.scalar_tensor_tensor(out(j), src(j), gain(j), rstd[:], ALU.mult, ALU.mult),
                              t_r, *clear)
                    tokens.append(t)
                    continue
                b = j % 2
                t = k.dve(lambda e: e.scalar_tensor_tensor(tmp[b][:], src(j), gain(j), rstd[:], ALU.mult, ALU.mult),
                          t_r, f"tmp{b}")
                tokens.append(hilo(lambda: ahi[:, dst + j, :], lambda: alo[:, dst + j, :], tmp[b][:], t, *clear,
                                   shift=shift(j) if shift else None, mark=f"tmp{b}"))
            k.mark("rstd", t)
            return tokens

        def wide(tokens, n_units, evac):
            def chunk(c, i):
                banks = (2 * (c % 2), 2 * (c % 2) + 1)
                t = product([(kt * 2 + m, bank(banks[m]), P, ahi[:, kt, :], alo[:, kt, :], kt == 0, kt == DT - 1, kt)
                             for kt in range(DT) for m in range(2)],
                            [f"bank{b}" for b in banks], tokens)
                evac(i, c, banks, t)
            if n_units // 2:
                k.loop(n_units // 2, lambda i: [chunk(c, i) for c in range(2)])
            if n_units % 2:
                chunk(0, n_units // 2)

        def into(dst):
            def evac(i, c, banks, t):
                k.act(lambda e: e.activation(one(dst, i * 4 + 2 * c), bank(banks[0]), ACT.Copy), t,
                      mark=f"bank{banks[0]}")
                k.dve(lambda e: e.tensor_copy(one(dst, i * 4 + (2 * c + 1)), bank(banks[1])), t,
                      mark=f"bank{banks[1]}")
            return evac

        def one(dst, j, rows=P, lo=0):
            if isinstance(j, int):
                return dst[lo:lo + rows, j, :]
            return dst[lo:lo + rows, bass.ds(j, 1), :].rearrange("p a n -> p (a n)")

        def residual(scale):
            def evac(i, c, banks, t):
                for m in range(2):
                    k.dve(lambda e: e.scalar_tensor_tensor(one(x, i * 4 + (2 * c + m)), bank(banks[m]),
                                                           scale(i * 4 + (2 * c + m)), one(x, i * 4 + (2 * c + m)),
                                                           ALU.mult, ALU.add), t, mark=f"bank{banks[m]}")
            return evac

        def down(scale):
            def body(i):
                for c in range(2):
                    banks = (2 * c, 2 * c + 1)
                    for part in range(3):
                        n = min(8, FT - 8 * part)
                        t = product([(kt * 2 + m, bank(banks[m]), P, hhi[:, 8 * part + kt, :], hlo[:, 8 * part + kt, :],
                                      part + kt == 0, 8 * part + kt == FT - 1, 0)
                                     for kt in range(n) for m in range(2)],
                                    [f"bank{b}" for b in banks] + ["hidden"])
                    residual(scale)(i, c, banks, t)
            k.loop(2, body)
            k.mark("x", Token("dve", k.count["dve"], ()))

        def last(engine):
            return Token(engine, k.count[engine], tuple(k.loops))

        def used():
            return units("use", k.count["use"])

        def plain_pair(i, tokens):
            def u(b0):
                return product([(kt * 2 + m, bank(b0 + m), P, ahi[:, kt, :], alo[:, kt, :], kt == 0, kt == DT - 1, kt)
                                for kt in range(DT) for m in range(2)], [f"bank{b0}", f"bank{b0 + 1}"], tokens)
            tg = u(0)
            ts = []
            for m in range(2):
                ts.append(k.act(lambda e: e.activation(tmp[m][:], bank(m), ACT.Silu), tg, f"tmp{m}", mark=f"bank{m}"))
            tv = u(2)
            for m in range(2):
                t = k.dve(lambda e: e.tensor_tensor(tmp[m][:], tmp[m][:], bank(2 + m), ALU.mult), tv, ts[m],
                          mark=f"bank{2 + m}")
                hilo(lambda: one(hhi, i * 2 + m),
                     lambda: one(hlo, i * 2 + m), tmp[m][:], t, mark=f"tmp{m}")

        def conv_pair(i, tokens):
            def u(b0):
                return product([(kt * 2 + m, bank(b0 + m), P, ahi[:, kt, :], alo[:, kt, :], kt == 0, kt == DT - 1, kt)
                                for kt in range(DT) for m in range(2)], [f"bank{b0}", f"bank{b0 + 1}"], tokens)

            def conv(b, dst, off, t, name):
                j = i * 2 + off
                t = k.act(lambda e: e.activation(dst[:], bank(b), ACT.Identity, bias=dcol("b_conv", j),
                                                 scale=dcol("w_conv2", j)), t, name)
                for d, w in ((1, "w_conv1"), (2, "w_conv0")):
                    t = k.dve(lambda e: e.scalar_tensor_tensor(dst[:, d:], bank(b, n=S - d), dcol(w, j), dst[:, d:],
                                                               ALU.mult, ALU.add), t)
                k.mark(f"bank{b}", t)
                return t
            tg = u(0)
            ts = []
            for m in range(2):
                t = conv(m, tmp[m], m, tg, f"tmp{m}")
                ts.append(k.act(lambda e: e.activation(tmp[m][:], tmp[m][:], ACT.Silu), t))
            tv = u(2)
            for m in range(2):
                t = conv(2 + m, tmp[2 + m], FT + m, tv, f"tmp{2 + m}")
                t = k.dve(lambda e: e.tensor_tensor(tmp[m][:], tmp[m][:], tmp[2 + m][:], ALU.mult), t, ts[m],
                          mark=f"tmp{2 + m}")
                hilo(lambda: one(hhi, i * 2 + m), lambda: one(hlo, i * 2 + m), tmp[m][:], t, mark=f"tmp{m}")

        def feed_forward(pair_of, gain, shift, scale):
            tokens = norm(lambda j: x[:, j, :], DT, D, gain, shift, ready=("x",), clear=(used(),))
            for e in ("act", "dve"):
                k.wait(e, last("pe"), last("pool"), last("act"), last("dve"))
            k.loop(HALF, lambda i: pair_of(i, tokens))
            k.mark("hidden", last("act"), last("dve"))
            down(scale)

        def head_norm(src, dst, rows, ones_name, gain, t_in, b, s, tables=None):
            t = k.act(lambda e: e.activation(sq[s][0:rows, :], src(), ACT.Square), f"sq{s}", *t_in)
            t = k.pe(lambda e: e.matmul(bank(b, rows), C(ones_name)[0:rows, 0:rows], sq[s][0:rows, :], start=True, stop=True),
                     t, f"bank{b}", mark=f"sq{s}", apart=True)
            t = k.act(lambda e: e.activation(sq[s][0:rows, :], bank(b, rows), ACT.Sqrt, bias=EPS[0:rows]), t)
            t = k.dve(lambda e: e.reciprocal(sq[s][0:rows, :], sq[s][0:rows, :]), t)
            y = tmp[s]
            if tables is None:
                t = k.dve(lambda e: e.scalar_tensor_tensor(dst(), src(), gain[0:rows], sq[s][0:rows, :], ALU.mult, ALU.mult), t)
                k.mark(f"sq{s}", t)
                k.mark(f"bank{b}", t)
                return t
            cos, sin, perm = tables
            ty = k.dve(lambda e: e.scalar_tensor_tensor(y[0:rows, :], src(), gain[0:rows], sq[s][0:rows, :], ALU.mult, ALU.mult),
                       t, f"tmp{s}")
            t = k.pe(lambda e: e.matmul(bank(b, rows), C(perm)[0:rows, 0:rows], y[0:rows, :], start=True, stop=True), ty)
            t2 = k.dve(lambda e: e.tensor_tensor(sq[s][0:rows, :], bank(b, rows), sin[0:rows, :], ALU.mult), t)
            t1 = k.pool(lambda e: e.tensor_tensor(y[0:rows, :], y[0:rows, :], cos[0:rows, :], ALU.mult), t)
            t = k.dve(lambda e: e.tensor_tensor(dst(), y[0:rows, :], sq[s][0:rows, :], ALU.add), t1, t2)
            for name in (f"sq{s}", f"bank{b}", f"tmp{s}"):
                k.mark(name, t)
            return t

        QAT = {3: (0, 0, 0), 2: (1, 0, 512), 0: (1, 384, 896), 1: (2, 0, 1024)}
        KAT = {0: (0, 0, 0), 1: (1, 0, 512), 3: (1, 384, 896), 2: (2, 0, 1024)}
        PACKED = 1280

        def scores(q, key, d, lo, strip, scale, E, stat, slot, ready, t_strip=()):
            done = {}
            for i in (3, 2, 0, 1):
                b, off, _ = QAT[i]
                done[i] = k.pe(lambda e: e.matmul(ps[:, b, off:off + P * (i + 1)], q[lo:lo + d, P * i:P * (i + 1)],
                                                  key[lo:lo + d, 0:P * (i + 1)], start=True, stop=True),
                               *ready, f"bank{b}")
            done[2] = done[0]
            for i in (3, 2, 0, 1):
                b, off, at = QAT[i]
                tm = k.dve(lambda e: e.tensor_tensor_reduce(
                    out=E[:, at:at + P * (i + 1)], in0=ps[:, b, off:off + P * (i + 1)],
                    in1=strip[:, S - P * (i + 1):S], scale=scale, scalar=-3e38, op0=ALU.add, op1=ALU.max,
                    accum_out=stat[:, i:i + 1]), done[i], f"E{slot}", *t_strip, mark=f"bank{b}", apart=True)
            t = k.dve(lambda e: e.tensor_scalar(stat[:, 4:8], stat[:, 0:4], -1.0, None, ALU.mult), tm)
            for i in (3, 2, 0, 1):
                at = QAT[i][2]
                te = k.act(lambda e: e.activation(E[:, at:at + P * (i + 1)], E[:, at:at + P * (i + 1)], ACT.Exp,
                                                  bias=stat[:, 4 + i:5 + i], accum_out=stat[:, 8 + i:9 + i]), t)
            return k.dve(lambda e: e.reciprocal(stat[:, 12:16], stat[:, 8:12]), te)

        def mix_values(E, t_e, PT, vtok, dv, lo, t_v):
            done = {}
            for j in (0, 1, 3, 2):
                b, off, _ = KAT[j]
                def make(e):
                    for i in range(j, 4):
                        at = QAT[i][2] + P * j
                        ins = e.transpose(ps[:, 3 + b, off + P * (i - j):off + P * (i - j + 1)], E[:, at:at + P], C("ident"))
                    return ins
                done[b] = k.pe(make, *t_e, f"bank{3 + b}")
            tt = done[2]
            tp = []
            for b, w, at in ((0, 512, 0), (1, 512, 512), (2, 256, 1024)):
                tp.append(k.act(lambda e: e.activation(PT[:, at:at + w], ps[:, 3 + b, 0:w], ACT.Copy), done[b], "PT",
                                mark=f"bank{3 + b}"))
            def make(e):
                for n, j in enumerate(range(4)):
                    at = KAT[j][2]
                    ins = e.matmul(ps[lo:lo + dv, 6, P * j:S], vtok[:, j, :], PT[:, at:at + S - P * j],
                                   start=(j == 0), stop=(j == 3))
                return ins
            t = k.pe(make, tp[-1], *t_v, "bank6")
            k.mark("PT", t)
            return tt, t

        z1 = region("z1", 0, [P, 19, S])
        qt = region("qt", 19, [P, 8, S])
        kvt = region("kvt", 27, [P, 8, S])
        tables = [region(f"table{n}", 35 + n, [P, S]) for n in range(4)]
        strip_causal = region("strip_causal", 40, [P, S])
        strip_dil = region("strip_dil", 41, [P, S])
        angle = region("angle", 0, [P, 4, S])
        pos_i = region("pos_i", 4, [1, S], I32)
        pos_f = region("pos_f", 5, [1, S])
        rel = region("rel", 6, [32, 8])
        onehot = region("onehot", 7, [P, 2 * 640])
        dist = region("dist", 10, [8, 640])
        hankel = region("hankel", 12, [P, 8, S])
        flip = region("flip", 20, [P, P])
        flipped = region("flipped", 21, [P, 8, S])

        t_pos = k.dma("act", "d_pos", pos_i[:], pos_in)
        t_strip = k.dma("act", "d_strip", strip_causal[:], strip_in[0])
        t_strip2 = k.dma("act", "d_strip2", strip_dil[:], strip_in[1])
        t_rel = k.dma("act", "d_rel", rel[:], rel_in)
        t_hot = k.dma("act", "d_hot", onehot[:], bucket_in[:, 0:1280])
        t_flip = k.dma("act", "d_flip", flip[:], bucket_in[:, 1280:1280 + P])

        for _ in range(2):
            split()

        t = k.act(lambda e: e.activation(small[:, 8:16], cols[:, COL["c"]:COL["c"] + 8], ACT.Silu), t_cols)
        t1 = k.act(lambda e: e.activation(chi[:, :, 0], small[:, 8:16], ACT.Copy), t)
        t1 = k.act(lambda e: e.activation(chi[:, :, 1], small[:, 8:16], ACT.Copy), t)
        for n in range(2):
            t_c = k.dve(lambda e: e.tensor_tensor(clo[:, :, n], small[:, 8:16], chi[:, :, n].bitcast(F32), ALU.subtract), t1)

        def make(e):
            e.matmul(ps[0:8, 4, :], rel[:], onehot[0:32, 0:512], start=True, stop=True)
            return e.matmul(ps[0:8, 5, 0:128], rel[:], onehot[0:32, 512:640], start=True, stop=True)
        t = k.pe(make, t_rel, t_hot)
        k.dve(lambda e: e.scalar_tensor_tensor(dist[:, 0:512], ps[0:8, 4, :], 8.0, onehot[0:8, 640:1152], ALU.mult, ALU.add), t, t_hot)
        t = k.dve(lambda e: e.scalar_tensor_tensor(dist[:, 512:640], ps[0:8, 5, 0:128], 8.0, onehot[0:8, 1152:1280], ALU.mult, ALU.add))
        t = k.dma("act", "d_scratch", scratch, dist[:], t)
        t = k.dma("act", "d_hankel", hankel[:], bass.AP(tensor=scratch.tensor, offset=0, ap=[[1, P], [640, 8], [1, S]]), t)
        tf = []
        for h in range(8):
            b = 4 + h % 2
            t1 = k.pe(lambda e: e.matmul(bank(b), flip[:], hankel[:, h, :], start=True, stop=True), t, t_flip, f"flip{h % 2}")
            tf.append(k.dve(lambda e: e.tensor_copy(flipped[:, h, :], bank(b)), t1, mark=f"flip{h % 2}"))
        t_strips = k.dma("act", "d_strips", strips_dram.rearrange("h p n -> p h n"), flipped[:], tf[-1])

        t = k.dve(lambda e: e.tensor_copy(pos_f[:], pos_i[:]), t_pos)
        t_p = k.pe(lambda e: e.matmul(bank(6), C("ones")[0:1, :], pos_f[:], start=True, stop=True), t, t_const)
        TWO_PI = 2 * math.pi
        C1 = 6.28125
        C2 = float(np.round((TWO_PI - C1) * 2 ** 22) / 2 ** 22)
        C3 = TWO_PI - C1 - C2
        MAGIC = 1.5 * 2 ** 23
        for n, f in enumerate(("freq_dil", "freq_mla")):
            a, m, r, q = (angle[:, j, :] for j in range(4))
            cos, sin = tables[2 * n], tables[2 * n + 1]
            t = k.dve(lambda e: e.tensor_scalar(a, bank(6), col(f), None, ALU.mult), t_p, t_cols, "angle")
            t = k.dve(lambda e: e.tensor_scalar(m, a, 1.0 / TWO_PI, MAGIC, ALU.mult, ALU.add), t)
            t = k.dve(lambda e: e.tensor_scalar(m, m, -MAGIC, None, ALU.add), t)
            for c in (C1, C2, C3):
                t = k.dve(lambda e: e.scalar_tensor_tensor(a, m, -c, a, ALU.mult, ALU.add), t)
            t = k.dve(lambda e: e.tensor_scalar(a, a, 3.1415925, -3.1415925, ALU.min, ALU.max), t)
            t1 = k.act(lambda e: e.activation(sin[:], a, ACT.Sin), t)
            t = k.act(lambda e: e.activation(r, a, ACT.Abs), t)
            t = k.act(lambda e: e.activation(cos[:], r, ACT.Sin, bias=HALF_PI, scale=-1.0), t, mark="angle")
        t_tab = t
        k.mark("bank6", t)
        k.mark("bank4", tf[-1])
        k.mark("bank5", tf[-1])

        def ada(i):
            for c in range(2):
                banks = (2 * c, 2 * c + 1)
                t = product([(kt * 2 + m, bank(banks[m], n=2), P, chi[:, kt, :], clo[:, kt, :], kt == 0, kt == DT - 1, 0)
                             for kt in range(DT) for m in range(2)], [f"bank{b}" for b in banks] + [t_c])
                for m in range(2):
                    j = i * 4 + (2 * c + m)
                    k.dve(lambda e: e.tensor_tensor(mod[:, bass.ds(j, 1)], bank(banks[m], n=1), dcol("b_ada", j), ALU.add),
                          t, mark=f"bank{banks[m]}")
        k.loop(U_ADA // 2, ada)
        t_mod = last("dve")
        for n, (g, c) in enumerate((("g_mix", 8), ("g_ffn", 32))):
            t = k.dve(lambda e: e.tensor_scalar(gcol[:, 8 * n:8 * n + 8], mod[:, c:c + 8], 1.0, None, ALU.add), t_mod)
            t = k.dve(lambda e: e.tensor_tensor(gcol[:, 8 * n:8 * n + 8], gcol[:, 8 * n:8 * n + 8],
                                                cols[:, COL[g]:COL[g] + 8], ALU.mult), t)
        t_g = t

        tokens = norm(lambda j: x[:, j, :], DT, D, lambda j: gcol[:, j:j + 1], lambda j: mod[:, j:j + 1],
                      ready=(t_x,), clear=(t_g,))
        k.wait("act", t_strips, t_g)
        k.wait("dve", t_strips)

        wide(tokens, U_IN1 - 1, into(z1))
        t = product([(kt * 2, bank(2, 96), 96, ahi[:, kt, :], alo[:, kt, :], kt == 0, kt == DT - 1, kt)
                     for kt in range(DT)], ["bank2"])
        t_z = k.act(lambda e: e.activation(z1[0:96, 18, :], bank(2, 96), ACT.Copy), t, mark="bank2")
        t_zd = last("dve")

        tok_q = norm(lambda j: z1[:, j, :], 4, 512, lambda j: col("g_q_lat", j), ready=(t_z, t_zd), clear=(used(),))
        for u in range(U_QB):
            banks = range(4)
            t = product([(kt * 4 + h, bank(h, 96), 96, ahi[:, kt, :], alo[:, kt, :], kt == 0, kt == 3, kt)
                         for kt in range(4) for h in range(4)], [f"bank{b}" for b in banks], tok_q)
            for h in range(4):
                if h % 2:
                    k.act(lambda e: e.activation(qt[0:96, 4 * u + h, :], bank(h, 96), ACT.Copy), t, mark=f"bank{h}")
                else:
                    k.dve(lambda e: e.tensor_copy(qt[0:96, 4 * u + h, :], bank(h, 96)), t, mark=f"bank{h}")
        tok_kv = norm(lambda j: z1[:, 4 + j, :], 2, 256, lambda j: col("g_kv_lat", j), dst=4, ready=(t_z, t_zd),
                      clear=(t_z,))
        t = product([(kt * 8 + h, bank(h if h < 7 else 7), P, ahi[:, 4 + kt, :], alo[:, 4 + kt, :], kt == 0, kt == 1, kt)
                     for h in range(8) for kt in range(2)], [f"bank{b}" for b in range(8)], tok_kv)
        for h in range(8):
            if h % 2:
                k.act(lambda e: e.activation(kvt[:, h, :], bank(h), ACT.Copy), t, mark=f"bank{h}")
            else:
                k.dve(lambda e: e.tensor_copy(kvt[:, h, :], bank(h)), t, mark=f"bank{h}")
        t_a, t_d = last("act"), last("dve")

        rot_q = (tables[2], tables[3], "permq")
        rot_d = (tables[0], tables[1], "perm64")
        head_norm(lambda: z1[0:96, 18, :], lambda: z1[0:96, 18, :], 96, "blkq", col("g_k"), (t_a, t_d, t_tab), 4, 0, rot_q)

        def prep_mla(i):
            for s in range(2):
                head_norm(lambda: one(qt, i * 2 + s, 96), lambda: one(qt, i * 2 + s, 96), 96, "blkq", col("g_q"),
                          (t_a, t_d, t_tab), 4 + s, s, rot_q)
                head_norm(lambda: one(kvt, i * 2 + s, 64), lambda: one(kvt, i * 2 + s, 64), 64, "blk64", col("g_k"),
                          (), 4 + s, s)
        k.loop(4, prep_mla)

        def prep_dil(i):
            for s, (base, g) in enumerate(((6, "g_dq"), (10, "g_dk"))):
                head_norm(lambda: one(z1, i + base), lambda: one(z1, i + base), P, "blk64", col(g), (), 4 + s, s, rot_d)
        k.loop(4, prep_dil)
        t_prep = (last("dve"), last("act"), last("pe"), last("pool"))

        E = [region(f"E{s}", 2.5 * s, [P, PACKED]) for s in range(2)]
        PT = region("PT", 35, [P, PACKED])
        vtok = region("vtok", 5, [P, 4, P])
        qs = [region("qs0", 37.5, [P, S]), region("qs1", 38.5, [P, S])]
        ks = [region("ks0", 42, [P, S]), region("ks1", 43, [P, S])]
        stat = [place(f"stat{s}", [P, 16]) for s in range(2)]

        for e in ("act", "dve", "pool", "pe"):
            k.wait(e, *t_prep)
        for s in range(2):
            t_kpe = k.dve(lambda e: e.tensor_copy(ks[s][64:96, :], z1[64:96, 18, :]))

        def attend_heads(heads, strip, scale, i, dst):
            st = []
            for s, (q, key, d, lo, t_qk, V, olo) in enumerate(heads):
                t = scores(q, key, d, lo, strip, scale, E[s], stat[s], s, t_qk, (t_strip, t_strip2))
                k.mark(f"QK{s}", last("pe"))
                for b in (3, 2, 0, 1):
                    at = QAT[b][2]
                    t2 = k.dve(lambda e: e.tensor_scalar(E[s][:, at:at + P * (b + 1)], E[s][:, at:at + P * (b + 1)],
                                                         stat[s][:, 12 + b:13 + b], None, ALU.mult), t)
                st.append(t2)
            for s, (q, key, d, lo, t_qk, V, olo) in enumerate(heads):
                t_v, v = V(s)
                t_tr, t_o = mix_values(E[s], (st[s],), PT, v, 64, olo, (t_v,))
                k.mark(f"E{s}", t_tr)
                k.mark("vtok", t_o)
                o = ps[olo:olo + 64, 6, :]
                hilo(lambda: one(ahi, dst(i), 64, olo), lambda: one(alo, dst(i), 64, olo), o, t_o, mark="bank6")

        def mla(i):
            heads = []
            for s in range(2):
                t1 = k.pool(lambda e: e.tensor_copy(qs[s][0:96, :], one(qt, i * 2 + s, 96)), f"QK{s}")
                t2 = k.pool(lambda e: e.tensor_copy(ks[s][0:64, :], one(kvt, i * 2 + s, 64)))
                t3 = k.pool(lambda e: e.tensor_copy(sq[s][:], one(kvt, i * 2 + s)), f"V{s}")

                def values(s, t3=t3):
                    def make(e):
                        for j in range(4):
                            ins = e.transpose(ps[:, 7, P * j:P * (j + 1)], sq[s][:, P * j:P * (j + 1)], C("ident"))
                        return ins
                    t = k.pe(make, t3, "bank7", mark=f"V{s}")
                    t = k.act(lambda e: e.activation(vtok[:, :, 64 * s:64 * s + 64],
                                                     ps[:, 7, :].rearrange("p (j d) -> p j d", j=4)[:, :, 64:128], ACT.Copy),
                              t, f"vtok", mark="bank7")
                    return t, vtok[:, :, 64 * s:64 * s + 64]
                heads.append((qs[s], ks[s], 96, 0, (t2, t_kpe), values, 64 * s))
            attend_heads(heads, strip_causal, (96.0) ** -0.5, i, lambda i: i)
        k.loop(4, mla)

        def dil(i):
            t1 = k.pool(lambda e: e.tensor_copy(qs[0][:], one(z1, i + 6)), "QK0", "QK1")
            t2 = k.pool(lambda e: e.tensor_copy(ks[0][:], one(z1, i + 10)))
            t3 = k.pool(lambda e: e.tensor_copy(sq[0][:], one(z1, i + 14)), "V0")

            def values(s):
                if s == 0:
                    def make(e):
                        for j in range(4):
                            ins = e.transpose(ps[:, 7, P * j:P * (j + 1)], sq[0][:, P * j:P * (j + 1)], C("ident"))
                        return ins
                    t = k.pe(make, t3, "bank7", mark="V0")
                    values.t = k.act(lambda e: e.activation(vtok[:], ps[:, 7, :].rearrange("p (j d) -> p j d", j=4), ACT.Copy),
                                     t, "vtok", mark="bank7")
                return values.t, vtok[:, :, 64 * s:64 * s + 64]
            heads = [(qs[0], ks[0], 64, 64 * s, (t2,), values, 64 * s) for s in range(2)]
            attend_heads(heads, strip_dil, 64.0 ** -0.5, i, lambda i: i + 4)
        k.loop(4, dil)
        tok_mix = [last("dve")] * DT
        k.wait("pe", last("dve"), last("act"))

        wide(tok_mix, U_O, residual(lambda j: mod[:, bass.ds(j + 16, 1)]))
        k.mark("x", last("dve"))
        feed_forward(conv_pair, lambda j: gcol[:, 8 + j:9 + j], lambda j: mod[:, 24 + j:25 + j],
                     lambda j: mod[:, bass.ds(j + 40, 1)])
        k.mark("x", last("dve"))
        def skip():
            product([(0, bank(0), P, ahi[:, 0, :], alo[:, 0, :], True, True, 0)], ["bank0"])
        for _ in range(U_PAD):
            skip()

        z2 = region("z2", 0, [P, FT, S])
        strip2 = [region(f"strip{m}", 22 + m, [P, S]) for m in range(2)]
        E4 = [region(f"EE{s}", 24 + 2.5 * s, [P, PACKED]) for s in range(4)]
        PT2 = region("PTT", 34, [P, PACKED])
        vtok2 = region("vtok2", 36.5, [P, 4, P])
        stage = [region(f"stage{n}", 37.5 + n, [P, S]) for n in range(3)]
        stat4 = stat + [place(f"stat{s}", [P, 16]) for s in range(2, 4)]
        bd = place("bd", [P, 4, P])
        W = [region(f"W{n}", 24 + n, [P, S]) for n in range(8)]

        def layer(l):
            t_lc = k.dma("pool", "d_lc", lc[:], lambda: layer_in[bass.ds(l, 1)].rearrange("a p n -> (a p) n"),
                         last("act"), last("dve"), last("pe"))
            t_bd = k.dma("pool", "d_bd", bd[:], lambda: lru_in[bass.ds(l, 1)].rearrange("a p b n -> (a p) b n"))
            for e in ("act", "dve"):
                k.wait(e, t_lc)
            feed_forward(plain_pair, lambda j: lcol("ffn1", j), None, lambda j: 0.5)
            k.mark("x", last("dve"))
            tokens = norm(lambda j: x[:, j, :], DT, D, lambda j: lcol("mix", j), ready=("x",), clear=(used(),))
            for e in ("act", "dve", "pool"):
                k.wait(e, last("pe"), used())
            wide(tokens, 11, into(z2))
            skip()
            t_a, t_d = last("act"), last("dve")
            t_u = used()
            for e in ("act", "dve", "pool", "pe"):
                k.wait(e, t_a, t_d, t_u)

            for n in range(2):
                t = k.dve(lambda e: e.tensor_tensor(small[0:64, 16 + n:17 + n], lc[0:64, LCOL["lam"] + 2 * n:LCOL["lam"] + 2 * n + 1],
                                                    lc[0:64, LCOL["lam"] + 2 * n + 1:LCOL["lam"] + 2 * n + 2], ALU.mult))
            t = k.pe(lambda e: e.matmul(ps[:, 7, 0:2], C("ones")[0:64, :], small[0:64, 16:18], start=True, stop=True), t, "bank7")
            t = k.act(lambda e: e.activation(small[:, 18:20], ps[:, 7, 0:2], ACT.Exp), t, mark="bank7")
            t = k.dve(lambda e: e.tensor_tensor(small[:, 20:21], small[:, 18:19], small[:, 19:20], ALU.subtract), t)
            t = k.dve(lambda e: e.tensor_tensor(small[:, 20:21], small[:, 20:21], lcol("lam_init"), ALU.add), t)
            t = k.dve(lambda e: e.tensor_scalar(small[:, 21:22], small[:, 20:21], -1.0, None, ALU.mult), t)
            t_lam = t
            t_sub = k.dve(lambda e: e.tensor_tensor(small[:, 22:23], lcol("subln"), lcol("sub_scale"), ALU.mult))

            def head(h):
                ts = []
                for m in range(2):
                    ts.append(k.dma("pool", f"d_st{m}", strip2[m][:],
                                    lambda: strips_dram[bass.ds(h * 2 + m, 1)].rearrange("a p n -> (a p) n"), f"strip{m}"))
                for n in range(3):
                    tz = k.pool(lambda e: e.tensor_copy(stage[n][:], one(z2, h + 4 * n)), f"stage{n}")
                st = []
                for m in range(2):
                    t = scores(stage[0], stage[1], 64, 64 * m, strip2[m], 0.125, E4[m], stat4[m], m, (tz,), (ts[m],))
                    k.mark(f"strip{m}", last("dve"))
                    st.append(t)
                k.mark("stage0", last("pe"))
                k.mark("stage1", last("pe"))
                t = k.dve(lambda e: e.tensor_scalar(stat4[1][:, 12:16], stat4[1][:, 12:16], small[:, 21:22], None, ALU.mult),
                          st[1], t_lam)
                for i in (3, 2, 0, 1):
                    at, w = QAT[i][2], P * (i + 1)
                    t1 = k.dve(lambda e: e.tensor_scalar(E4[1][:, at:at + w], E4[1][:, at:at + w], stat4[1][:, 12 + i:13 + i],
                                                         None, ALU.mult), t)
                for i in (3, 2, 0, 1):
                    at, w = QAT[i][2], P * (i + 1)
                    t2 = k.dve(lambda e: e.scalar_tensor_tensor(E4[0][:, at:at + w], E4[0][:, at:at + w],
                                                                stat4[0][:, 12 + i:13 + i], E4[1][:, at:at + w],
                                                                ALU.mult, ALU.add), t1)
                k.mark("E1", t2)

                def make(e):
                    for j in range(4):
                        ins = e.transpose(ps[:, 7, P * j:P * (j + 1)], stage[2][:, P * j:P * (j + 1)], C("ident"))
                    return ins
                t = k.pe(make, tz, "bank7", mark="stage2")
                t_v = k.act(lambda e: e.activation(vtok2[:], ps[:, 7, :].rearrange("p (j d) -> p j d", j=4), ACT.Copy),
                            t, "vtok", mark="bank7")
                t_tr, t_o = mix_values(E4[0], (t2,), PT2, vtok2, P, 0, (t_v,))
                k.mark("E0", t_tr)
                k.mark("vtok", t_o)
                t = k.act(lambda e: e.activation(sq[0][:], bank(6), ACT.Square), t_o, "sq0")
                t = k.pe(lambda e: e.matmul(bank(7), C("ones"), sq[0][:], start=True, stop=True), t, "bank7", mark="sq0")
                t = k.act(lambda e: e.activation(rstd[:], bank(7), ACT.Sqrt, bias=SUB_EPS, scale=1.0 / P), t, "rstd", mark="bank7")
                t = k.dve(lambda e: e.reciprocal(rstd[:], rstd[:]), t)
                t = k.dve(lambda e: e.scalar_tensor_tensor(tmp[0][:], bank(6), small[:, 22:23], rstd[:], ALU.mult, ALU.mult),
                          t, t_sub, "tmp0", mark="bank6")
                k.mark("rstd", t)
                hilo(lambda: one(ahi, h), lambda: one(alo, h), tmp[0][:], t, mark="tmp0")
            k.loop(4, head)
            for e in ("act", "dve", "pool", "pe"):
                k.wait(e, last("act"), last("dve"), last("pe"))

            def shifted(dst, src, taps, t, *bias):
                if bias:
                    t = k.act(lambda e: e.activation(dst, src, ACT.Identity, bias=bias[0], scale=taps[0]), t)
                else:
                    t = k.act(lambda e: e.activation(dst, src, ACT.Copy, scale=taps[0]), t)
                for d in range(1, len(taps)):
                    t = k.dve(lambda e: e.scalar_tensor_tensor(dst[:, d:], src[:, 0:S - d], taps[d], dst[:, d:],
                                                               ALU.mult, ALU.add), t)
                return t
            for f in range(2):
                t = k.dve(lambda e: e.tensor_tensor(W[0][:], z2[:, 14 + f, :], z2[:, 16 + f, :], ALU.mult), "W0")
                t = shifted(W[1][:], W[0][:], [lcol("sc_w", 2 * n + f) for n in (2, 1, 0)], t)
                t = k.dve(lambda e: e.tensor_tensor(W[2][:], W[1][:], z2[:, 12 + f, :], ALU.mult), t, "W2", mark="W0")
                hilo(lambda: ahi[:, 4 + f, :], lambda: alo[:, 4 + f, :], W[2][:], t, mark="W2")

            n2 = slice(LCOL["lambda"], LCOL["lambda"] + 2)
            sc = [small[:, 4 + 2 * n:6 + 2 * n] for n in range(2)] + [small[:, 24 + 2 * n:26 + 2 * n] for n in range(4)]
            t = k.act(lambda e: e.activation(sc[0], lc[:, n2], ACT.Abs))
            t = k.act(lambda e: e.activation(sc[0], sc[0], ACT.Exp, scale=-1.0), t)
            t = k.dve(lambda e: e.tensor_scalar(sc[1], sc[0], 1.0, None, ALU.add), t)
            t1 = k.act(lambda e: e.activation(sc[2], sc[1], ACT.Ln), t)
            t = k.dve(lambda e: e.tensor_scalar(sc[3], sc[1], -1.0, None, ALU.add), t)
            t = k.dve(lambda e: e.tensor_scalar(sc[4], sc[3], 0.0, None, ALU.is_equal), t)
            t = k.dve(lambda e: e.tensor_tensor(sc[3], sc[3], sc[4], ALU.add), t)
            t = k.dve(lambda e: e.reciprocal(sc[3], sc[3]), t)
            t = k.dve(lambda e: e.tensor_tensor(sc[2], sc[2], sc[4], ALU.add), t, t1)
            t = k.dve(lambda e: e.tensor_tensor(sc[2], sc[2], sc[3], ALU.mult), t)
            t = k.dve(lambda e: e.tensor_tensor(sc[2], sc[2], sc[0], ALU.mult), t)
            t = k.dve(lambda e: e.tensor_scalar(sc[5], lc[:, n2], 0.0, None, ALU.min), t)
            t = k.dve(lambda e: e.tensor_tensor(sc[2], sc[2], sc[5], ALU.subtract), t)
            t_sp = k.dve(lambda e: e.tensor_scalar(sc[2], sc[2], -8.0, None, ALU.mult), t)
            for f in range(2):
                nsp = small[:, 24 + f:25 + f]
                xr, r, g, a, th = (W[3 + n][:] for n in range(5))
                for e in ("act", "dve", "pe"):
                    k.wait(e, last("act"), last("dve"), last("pe"))
                t_xr = shifted(xr, z2[:, 18 + f, :], [lcol("lru_w", 2 * n + f) for n in (3, 2, 1, 0)], t_sp, lcol("lru_b", f))
                t_g1 = k.pe(lambda e: e.matmul(bank(0), bd[:, f, :], xr, start=True, stop=True), t_xr, "bank0", t_bd)
                t_g2 = k.pe(lambda e: e.matmul(bank(1), bd[:, 2 + f, :], xr, start=True, stop=True), "bank1")
                t_r = k.act(lambda e: e.activation(r, bank(0), ACT.Sigmoid, bias=lcol("ba", f)), t_g1, mark="bank0")
                t_i = k.act(lambda e: e.activation(g, bank(1), ACT.Sigmoid, bias=lcol("bx", f)), t_g2, mark="bank1")
                t_a = k.act(lambda e: e.activation(a, r, ACT.Exp, scale=nsp), t_r)
                t_t = k.act(lambda e: e.activation(th, r, ACT.Tanh, scale=nsp), t_r)
                t = k.dve(lambda e: e.tensor_scalar(r, th, -1.0, None, ALU.add), t_t, t_a)
                t = k.dve(lambda e: e.reciprocal(r, r), t)
                t = k.dve(lambda e: e.scalar_tensor_tensor(th, th, 2.0, r, ALU.mult, ALU.mult), t)
                t = k.dve(lambda e: e.tensor_scalar(th, th, 2.0 ** -116, None, ALU.max), t)
                t = k.act(lambda e: e.activation(th, th, ACT.Sqrt), t)
                t1 = k.dve(lambda e: e.tensor_tensor(g, g, xr, ALU.mult), t_i)
                t = k.dve(lambda e: e.tensor_tensor(g, g, th, ALU.mult), t, t1)
                t = k.dve(lambda e: e.tensor_tensor_scan(r, a, g, 0.0, ALU.mult, ALU.add), t)
                t1 = k.act(lambda e: e.activation(xr, z2[:, 20 + f, :], ACT.Gelu_apprx_tanh), t)
                t = k.dve(lambda e: e.tensor_tensor(xr, xr, r, ALU.mult), t1)
                hilo(lambda: ahi[:, 6 + f, :], lambda: alo[:, 6 + f, :], xr, t)
            k.wait("pe", last("dve"), last("act"))

            wide([last("dve")] * DT, U_O, residual(lambda j: 1.0))
            k.mark("x", last("dve"))
            feed_forward(plain_pair, lambda j: lcol("ffn2", j), None, lambda j: 0.5)
            k.mark("x", last("dve"))
        k.loop(LAYERS, layer)

        norm(lambda j: x[:, j, :], DT, D, lambda j: col("final", j), out=lambda j: x[:, j, :], ready=("x",))
        k.dma("sp", "d_out", y_out, x[:], last("dve"))
        nc.sync.wait_ge(k.sem("d_out"), 16)
        for s in range(2):
            nc.sync.wait_ge(k.sem(f"ld{s}"), 16 * (U_ALL // 2))


def blocks_of(w, order):
    out = np.zeros((len(order), P, P), w.dtype)
    for n, b in enumerate(order):
        if b is not None:
            kt, c, width = b
            out[n, :, :width] = w[kt * P:(kt + 1) * P, c:c + width]
    return out


def wide_order(n, first=0):
    return [(kt, first + 256 * u + P * m, P) for u in range(n) for kt in range(DT) for m in range(2)]


def down_order():
    order = []
    for pair in range(4):
        for part in range(3):
            blocks = [(8 * part + kt, 256 * pair + P * m, P) for kt in range(min(8, FT - 8 * part)) for m in range(2)]
            order += blocks + [None] * (UB - len(blocks))
    return order


def stream_of(v):
    parts = [blocks_of(v["w_ada"][0], wide_order(U_ADA))]
    w = v["w_in"][0]
    in1 = wide_order(3)
    in1 += [(kt, 800 + 256 * u + P * m, P) for u in range(6) for kt in range(DT) for m in range(2)]
    for kt in range(DT):
        in1 += [(kt, 704, 96), None]
    parts.append(blocks_of(w, in1))
    parts.append(blocks_of(v["w_q_b"][0], [(kt, 96 * (4 * u + h), 96) for u in range(2) for kt in range(4) for h in range(4)]))
    parts.append(blocks_of(v["w_kv_b"][0], [(kt, P * h, P) for kt in range(2) for h in range(8)]))
    parts.append(blocks_of(v["w_o"][0], wide_order(4)))

    def pairs(a, b, off):
        for j in range(HALF):
            order = [(kt, 256 * j + P * m, P) for kt in range(DT) for m in range(2)]
            parts.append(blocks_of(a, order))
            parts.append(blocks_of(b, [(kt, c + off, w) for kt, c, w in order]))
    pairs(v["w_up"][0], v["w_up"][0], FF)
    parts.append(blocks_of(v["w_down"][0], down_order()))
    parts.append(np.zeros((U_PAD * UB, P, P), np.float32))
    for l in range(LAYERS):
        for n in (1, 2):
            if n == 2:
                parts.append(blocks_of(v["w_in_2"][l], wide_order(11) + [None] * UB))
                parts.append(blocks_of(v["w_out_2"][l], wide_order(4)))
            pairs(v[f"ffn{n}_gate_2"][l], v[f"ffn{n}_up_2"][l], 0)
            parts.append(blocks_of(v[f"ffn{n}_down_2"][l], down_order()))
    parts.append(np.zeros((2 * UB, P, P), np.float32))
    s = np.concatenate(parts).reshape(-1, UB, P, P)
    assert len(s) == U_ALL
    return np.ascontiguousarray(s.transpose(0, 2, 1, 3))


def columns_of(plan, n, vectors):
    out = np.zeros((P, n), np.float32)
    for name, a in vectors.items():
        a = np.asarray(a).reshape(-1)
        w = -(-a.size // P)
        full = np.zeros(w * P, a.dtype)
        full[:a.size] = a
        out[:, plan[name]:plan[name] + w] = full.reshape(w, P).T
    return out


def constants():
    ident = np.eye(P)
    ones = np.ones((P, P))
    blk64 = np.kron(np.eye(2), np.ones((64, 64)) / 64)
    blkq = np.zeros((P, P))
    blkq[:64, :64] = 1 / 64
    blkq[64:96, 64:96] = 1 / 32
    def swap(m, at, half):
        for j in range(half):
            m[at + half + j, at + j] = -1
            m[at + j, at + half + j] = 1
    perm64, permq = np.zeros((P, P)), np.zeros((P, P))
    swap(perm64, 0, 32)
    swap(perm64, 64, 32)
    swap(permq, 64, 16)
    const = np.concatenate([ident, ones, blk64, blkq, perm64, permq], 1).astype(np.float32)
    dist = np.arange(P)[:, None] - np.arange(S)[None] + 384
    causal = np.where(dist >= 0, 0.0, NEG)
    times = ((dist >= 0) & (dist <= 128)).astype(int) + ((dist >= 0) & (dist % 4 == 0)) + ((dist >= 0) & (dist % 16 == 0))
    dil = np.where(times > 0, 8.0 * np.log(np.maximum(times, 1)), NEG)
    strips = np.stack([causal, dil]).astype(np.float32)
    d = 511 - np.arange(640)
    n = np.maximum(d, 0)
    nf = np.maximum(n, 1).astype(np.float32)
    large = 16 + (np.log(nf / np.float32(16)) / np.float32(math.log(8)) * np.float32(16)).astype(np.int32)
    bucket = np.where(n < 16, n, np.minimum(large, 31))
    table = np.zeros((P, 1280 + P), np.float32)
    table[:32, :640] = bucket[None] == np.arange(32)[:, None]
    table[:8, 640:1280] = np.where(d >= 0, 0.0, NEG)[None]
    table[:, 1280:] = np.eye(P)[::-1]
    return const, strips, table


def kernel(**inputs):
    import concourse.bacc as _bacc
    from concourse.bass_utils import run_bass_kernel_spmd as _run

    v = {name: np.asarray(a) for name, a in inputs.items()}
    const, strips, table = constants()
    freq = {d: (10000.0 ** (-2.0 * np.arange(d // 2) / d)).astype(np.float32) for d in (32, 64)}
    freq_mla = np.zeros(P, np.float32)
    freq_mla[64:96] = np.tile(freq[32], 2)
    cols = columns_of(COL, NCOL, {
        "c": v["c"], "b_ada": v["b_ada"], "g_mix": v["g_mix_norm"], "g_q_lat": v["g_q_lat"], "g_kv_lat": v["g_kv_lat"],
        "g_q": np.concatenate([v["g_mla_q_nope"][0], v["g_mla_q_pe"][0]]),
        "g_k": np.concatenate([v["g_mla_k_nope"][0], v["g_mla_k_pe"][0]]),
        "g_dq": np.tile(v["g_dil_q"][0], 2), "g_dk": np.tile(v["g_dil_k"][0], 2), "g_ffn": v["g_ffn_norm"],
        "w_conv0": v["w_conv"][0, 0], "w_conv1": v["w_conv"][0, 1], "w_conv2": v["w_conv"][0, 2], "b_conv": v["b_conv"],
        "final": v["final_norm_2"], "freq_dil": np.tile(freq[64], 4), "freq_mla": freq_mla})
    layers = []
    lru = np.zeros((LAYERS, P, 4, P), np.float32)
    for l in range(LAYERS):
        lam = np.zeros((4, P), np.float32)
        for n, name in enumerate(("lam_q1_2", "lam_k1_2", "lam_q2_2", "lam_k2_2")):
            lam[n, :64] = v[name][l]
        lam_init = 0.8 - 0.6 * math.exp(-0.3 * l)
        layers.append(columns_of(LCOL, NLCOL, {
            "ffn1": v["ffn1_norm_2"][l], "mix": v["mix_norm_2"][l], "ffn2": v["ffn2_norm_2"][l],
            "subln": v["subln_gain_2"][l], "sc_w": v["sc_conv_w_2"][l], "lru_w": v["lru_conv_w_2"][l],
            "lru_b": v["lru_conv_b_2"][l], "lambda": v["lru_lambda_2"][l], "ba": v["lru_ba_2"][l],
            "bx": v["lru_bx_2"][l], "lam": lam, "lam_init": np.full(P, lam_init), "sub_scale": np.full(P, 1.0 - lam_init)}))
        for n, name in enumerate(("lru_wa_2", "lru_wx_2")):
            for b in range(4):
                at = 64 * (b % 2)
                lru[l, at:at + 64, 2 * n + b // 2, at:at + 64] = v[name][l, b]
    arrays = {
        "wstream": stream_of(v),
        "x_in": np.ascontiguousarray(v["x"][0].T.reshape(DT, P, S).transpose(1, 0, 2)),
        "pos_in": v["positions"],
        "cols_in": cols,
        "layer_in": np.stack(layers),
        "const_in": const,
        "strip_in": strips,
        "bucket_in": table,
        "rel_in": v["rel_bias_2"],
        "lru_in": lru,
    }
    nc = _bacc.Bacc("TRN2", target_bir_lowering=False, num_devices=1)
    args = [nc.dram_tensor(name, a.shape, mybir.dt.from_np(a.dtype), kind="ExternalInput").ap() for name, a in arrays.items()]
    args.append(nc.dram_tensor("y_out", (P, DT, S), F32, kind="ExternalOutput").ap())
    build(nc, *args)
    r = _run(nc, [arrays], core_ids=[0])
    y = r.results[0]["y_out"]
    return np.ascontiguousarray(y.transpose(1, 0, 2).reshape(D, S).T)[None]
```

```python
from contextlib import ExitStack
import math

import numpy as np

import concourse.bass as bass
from concourse import mybir
from concourse.alu_op_type import AluOpType as ALU

ACT = mybir.ActivationFunctionType
F32 = mybir.dt.float32
F32R = mybir.dt.float32r
I32 = mybir.dt.int32
P = 128
S = 512
D = 1024
DT = D // P
FF = 2816
FT = FF // P
HALF = FT // 2
UB = 16
LAYERS = 2
NEG = -1e30
TILE = S * 4

U_ADA, U_IN1, U_QB, U_KVB, U_O = 24, 10, 2, 1, 4
U_PAIR, U_DOWN, U_IN2 = 2, 12, 12
U_LAYER = 2 * (U_PAIR * HALF + U_DOWN) + U_IN2 + U_O
U_FIRST = U_IN1 + U_QB + U_KVB + U_O + U_PAIR * HALF + U_DOWN
U_PAD = U_FIRST % 2
U_SPLIT = U_FIRST + U_PAD + LAYERS * U_LAYER + 2
U_ALL = U_ADA + U_SPLIT
ADA_EARLY = 8


def column_plan():
    at, n = {}, 0
    for name, w in (("c", 8), ("b_ada", 48), ("g_mix", 8), ("g_q_lat", 4), ("g_kv_lat", 2), ("g_q", 1),
                    ("g_k", 1), ("g_dq", 1), ("g_dk", 1), ("g_ffn", 8), ("w_conv0", 44), ("w_conv1", 44),
                    ("w_conv2", 44), ("b_conv", 44), ("final", 8), ("ffn1_0", 8), ("freq_dil", 1), ("freq_mla", 1)):
        at[name] = n
        n += w
    return at, n


def layer_plan():
    at, n = {}, 0
    for name, w in (("ffn1", 8), ("mix", 8), ("ffn2", 8), ("next", 8), ("subln", 1), ("sc_w", 6), ("lru_w", 8),
                    ("lru_b", 2), ("lambda", 2), ("ba", 2), ("bx", 2), ("lam", 4), ("lam_init", 1),
                    ("sub_scale", 1)):
        at[name] = n
        n += w
    return at, n


COL, NCOL = column_plan()
LCOL, NLCOL = layer_plan()
CONST = {name: n * P for n, name in enumerate(("ident", "ones", "blk64", "blkq", "perm64", "permq"))}


class Token:

    def __init__(self, sem, value, loops, lag=None, like=None):
        self.sem, self.value, self.loops, self.lag = sem, value, loops, lag
        self.counter, self.times = like or (sem, 1)

    def per(self, loop):
        return loop.per.get(self.counter, 0) * self.times


class Loop:
    def __init__(self, n):
        self.n, self.i, self.open = n, None, True
        self.per, self.marks, self.used = {}, {}, set()


class Program:

    def __init__(self, nc, ctx):
        self.nc, self.ctx = nc, ctx
        self.eng = {"pe": nc.tensor, "act": nc.scalar, "dve": nc.vector, "pool": nc.gpsimd, "sp": nc.sync}
        self.sems, self.count, self.known = {}, {}, {}
        self.loops, self.scopes, self.dry = [], [{}], False

    def sem(self, name):
        if name not in self.sems:
            self.sems[name] = self.ctx.enter_context(self.nc.semaphore("s_" + name))
            self.count[name] = 0
        return self.sems[name]

    def value(self, t):
        v = t.value
        for L in t.loops:
            per = t.per(L)
            v = L.i * per + v if L.open and per else v + ((L.n - 1) * per if not L.open else 0)
            if t.lag is L:
                v = v - per
        return v

    def first_turn(self, t):
        v = t.value
        for L in t.loops:
            per = t.per(L)
            v += (L.n - 1) * per if not L.open else 0
            v -= per if t.lag is L else 0
        return v

    def resolve(self, name, engine):
        for depth in range(len(self.scopes) - 1, -1, -1):
            if name in self.scopes[depth]:
                return self.scopes[depth][name]
            if depth:
                L = self.loops[depth - 1]
                if self.dry:
                    L.used.add((engine, name))
                elif name in L.marks:
                    return [Token(t.sem, t.value, t.loops, L) for t in L.marks[name]]
        return []

    def wait(self, engine, *waits, apart=True):
        if self.dry:
            for w in waits:
                if not isinstance(w, Token):
                    self.resolve(w, engine)
            return
        e, latest = self.eng[engine], {}
        self.sem("spare_" + engine)
        for w in waits:
            for t in ([w] if isinstance(w, Token) else self.resolve(w, engine)):
                v = self.value(t)
                key = (t.sem, not isinstance(v, int), tuple(id(L) for L in t.loops if L.open))
                first = self.value(t) if isinstance(v, int) else self.first_turn(t)
                if key not in latest or latest[key][0] < first:
                    latest[key] = (first, v)
        by_register, waited = False, set()
        for (sem, register, _), (first, v) in sorted(latest.items(), key=lambda kv: kv[0][1]):
            if register:
                if sem in waited:
                    e.sem_inc(self.sem("spare_" + engine), 1)
                waited.add(sem)
                assert first > 0, (engine, sem, first)
                by_register = True
            elif v <= self.known.get((engine, sem), 0):
                continue
            else:
                self.known[engine, sem] = v
            e.wait_ge(self.sem(sem), v)
        if by_register and apart:
            e.sem_inc(self.sem("spare_" + engine), 1)

    def run(self, engine, make, *waits, sem=None, by=1, mark=None, apart=False):
        name = sem or engine
        self.sem(name)
        self.wait(engine, *waits, apart=apart or engine == "pool")
        if not self.dry:
            make(self.eng[engine]).then_inc(self.sems[name], by)
        self.count[name] += by
        t = Token(name, self.count[name], tuple(self.loops))
        if mark:
            self.mark(mark, t)
        return t

    def mark(self, name, *tokens):
        self.scopes[-1][name] = list(tokens)

    def pe(self, make, *waits, **kw):
        return self.run("pe", make, *waits, **kw)

    def act(self, make, *waits, **kw):
        return self.run("act", make, *waits, **kw)

    def dve(self, make, *waits, **kw):
        return self.run("dve", make, *waits, **kw)

    def pool(self, make, *waits, **kw):
        return self.run("pool", make, *waits, **kw)

    def dma(self, engine, sem, out, in_, *waits, **kw):
        return self.run(engine, lambda e: e.dma_start(out() if callable(out) else out, in_() if callable(in_) else in_),
                        *waits, sem=sem, by=16, **kw)

    def loop(self, n, body):
        L, start, dry = Loop(n), dict(self.count), self.dry
        for real in ((False,) if dry else (False, True)):
            self.loops.append(L)
            self.scopes.append({})
            if not real:
                self.dry, L.i = True, 0
                body(0)
                self.dry = dry
                L.per = {k: v - start.get(k, 0) for k, v in self.count.items() if v != start.get(k, 0)}
                L.marks = dict(self.scopes[-1])
                for k in self.count:
                    self.count[k] = start.get(k, 0)
            else:
                self.loops.pop()
                scope = self.scopes.pop()
                for engine in sorted({e for e, _ in L.used}):
                    self.wait(engine, *sorted(n for e, n in L.used if e == engine and n in L.marks))
                self.loops.append(L)
                self.scopes.append(scope)
                with self.nc.Fori(0, n) as i:
                    L.i = i
                    body(i)
            scope = self.scopes.pop()
            self.loops.pop()
            if not real and not dry:
                continue
        L.open = False
        for k, v in L.per.items():
            self.count[k] = start.get(k, 0) + n * v
        self.scopes[-1].update(scope)


def build(nc, wstream, x_in, pos_in, cols_in, layer_in, const_in, strip_in, bucket_in, rel_in, lru_in, y_out):
    scratch = nc.dram_tensor("bias_by_distance", (8, 640), F32, kind="Internal").ap()
    strips_dram = nc.dram_tensor("bias_strips", (8, P, S), F32, kind="Internal").ap()
    with ExitStack() as ctx:
        k = Program(nc, ctx)
        top = [-(-nc.sbuf_base // 64) * 64]

        def place(name, shape, dt=F32, at=None):
            if at is None:
                at = top[0]
                top[0] += -(-int(np.prod(shape[1:])) * 4 // 32) * 32
                assert top[0] <= nc.sbuf_usable_end, name
            return nc.alloc_sbuf_tensor_at(name, shape, dt, offset=at)

        raw = [place(f"raw{s}", [P, UB, P]) for s in range(2)]
        whi = [place(f"whi{s}", [P, UB, P], F32R) for s in range(2)]
        wlo = [place(f"wlo{s}", [P, UB, P], F32R) for s in range(2)]
        x = place("x", [P, DT, S])
        ahi = place("ahi", [P, DT, S], F32R)
        alo = place("alo", [P, DT, S], F32R)
        big = top[0]
        hhi = place("hhi", [P, FT, S], F32R)
        hlo = place("hlo", [P, FT, S], F32R)

        def region(name, tile, shape, dt=F32):
            return place(name, shape, dt, at=big + int(tile * TILE))

        const = place("const", [P, len(CONST) * P])
        cols = place("cols", [P, NCOL])
        lc = place("lc", [P, NLCOL])
        mod = place("mod", [P, 48])
        gcol = place("gcol", [P, 16])
        small = place("small", [P, 32])
        ada_row = place("ada_row", [1, 2, 2 * P])
        sq = [place(f"sq{s}", [P, S]) for s in range(2)]
        tmp = [place(f"tmp{s}", [P, S]) for s in range(4)]
        rstd = place("rstd", [P, S])
        ps = ctx.enter_context(nc.psum_tensor("ps", [P, 8, S], F32))

        def C(name, w=P):
            return const[:, CONST[name]:CONST[name] + w]

        def col(name, j=0):
            return cols[:, COL[name] + j:COL[name] + j + 1]

        def dyn(t, j, n=1):
            return t[:, j:j + n] if isinstance(j, int) else t[:, bass.ds(j, n)]

        def lcol(name, j=0):
            return lc[:, LCOL[name] + j:LCOL[name] + j + 1]

        EPS, SUB_EPS, HALF_PI = (small[:, n:n + 1] for n in range(3))
        ONE = small[0:1, 3:4]
        k.sem("start")
        k.run("pool", lambda e: e.memset(small[:, 0:1], 1e-6), sem="start")
        k.run("pool", lambda e: e.memset(small[:, 1:2], 1e-5))
        k.run("pool", lambda e: e.memset(small[:, 2:3], math.pi / 2))
        t_small = k.run("pool", lambda e: e.memset(small[:, 3:4], 1.0))
        for e in ("act", "dve", "pe", "sp", "pool"):
            k.wait(e, Token("start", 1, ()), t_small)
        t_cols = k.dma("act", "d_cols", cols[:], cols_in)
        t_const = k.dma("act", "d_const", const[:], const_in)
        t_x = k.dma("act", "d_x", x[:], x_in)

        for s in range(2):
            nc.sync.dma_start(raw[s][:], wstream[s]).then_inc(k.sem(f"ld{s}"), 16)
            k.sem(f"free{s}")
        k.sem("hi"), k.sem("use")
        k.count["take"] = 0
        with nc.sync.Fori(0, (U_ALL - 2) // 2) as i:
            for s in range(2):
                nc.sync.wait_ge(k.sem(f"free{s}"), i + 1)
                nc.sync.dma_start(raw[s][:], wstream[bass.ds(i * 2 + (2 + s), 1)].rearrange("a p b m -> (a p) b m"))\
                    .then_inc(k.sem(f"ld{s}"), 16)

        ahead = [0, 0]
        ada_at = []

        def count(sem, value):
            return Token(sem, value, tuple(k.loops))

        def take():
            v = k.count["take"]
            k.count["take"] += 1
            s = v % 2
            return s, Token(f"ld{s}", 16 * (v // 2 + 1), tuple(k.loops), like=(f"free{s}", 16)), v

        def split():
            g = k.count["hi"]
            r, loaded, v = take()
            s = g % 2
            ahead[s] = v - g
            k.act(lambda e: e.activation(whi[s][:], raw[r][:], ACT.Copy), loaded,
                  *([count("use", g - 1)] if g >= 2 else []), sem="hi")
            k.dve(lambda e: e.tensor_tensor(wlo[s][:], raw[r][:], whi[s][:].bitcast(F32), ALU.subtract),
                  count("hi", g + 1), sem=f"free{r}")

        def mm3(e, out, s, b, m, rhi, rlo, start, stop):
            wh, wl = whi[s][:, b, 0:m], wlo[s][:, b, 0:m]
            e.matmul(out, wh, rhi, start=start, stop=False)
            e.matmul(out, wl, rhi, start=False, stop=False)
            return e.matmul(out, wh, rlo, start=False, stop=stop)

        def product(blocks, first=(), inputs=None, last_part=True):
            u = k.count["use"]
            s = u % 2
            v = u + ahead[s]
            if k.dry and inputs:
                k.wait("pe", *(inputs.values() if isinstance(inputs, dict) else inputs))

            def make(e):
                ins, seen = None, {blocks[0][-1]}
                for b, out, m, rhi, rlo, start, stop, n in blocks:
                    if inputs and n not in seen:
                        seen.add(n)
                        k.wait("pe", inputs[n])
                    ins = mm3(e, out, s, b, m, rhi, rlo, start, stop)
                return ins
            if inputs:
                first = [*first, inputs[blocks[0][-1]]]
            if last_part:
                k.pe(make, count(f"free{v % 2}", v // 2 + 1), *first, sem="use")
                split()
                return count("use", u + 1)
            k.pe(make, count(f"free{v % 2}", v // 2 + 1), *first)

        def bank(b, m=P, n=S, lo=0):
            return ps[lo:lo + m, b, 0:n]

        def hilo(dst_hi, dst_lo, src, *waits, shift=None, mark=None):
            if shift is None:
                t1 = k.act(lambda e: e.activation(dst_hi(), src, ACT.Copy), *waits)
                t2 = k.dve(lambda e: e.tensor_tensor(dst_lo(), src, dst_hi().bitcast(F32), ALU.subtract), t1)
            else:
                t1 = k.act(lambda e: e.activation(dst_hi(), src, ACT.Identity, bias=shift), *waits)
                t2 = k.dve(lambda e: e.scalar_tensor_tensor(dst_lo(), src, shift, dst_hi().bitcast(F32),
                                                            ALU.add, ALU.subtract), t1)
            if mark:
                k.mark(mark, t1, t2)
            return t2

        def norm(src, n, width, gain, shift=None, dst=0, out=None, ready=(), clear=()):
            for j in range(n):
                t = k.act(lambda e: e.activation(sq[j % 2][:], src(j), ACT.Square), f"sq{j % 2}", *ready)
                k.pe(lambda e: e.matmul(bank(7), C("ones"), sq[j % 2][:], start=(j == 0), stop=(j == n - 1)),
                     t, "bank7", t_const, mark=f"sq{j % 2}")
            t = k.act(lambda e: e.activation(rstd[:], bank(7), ACT.Sqrt, bias=EPS, scale=1.0 / width),
                      f"sq{(n - 1) % 2}", "rstd", mark="bank7")
            t_r = k.dve(lambda e: e.reciprocal(rstd[:], rstd[:]), t)
            tokens = []
            for j in range(n):
                if out is not None:
                    t = k.dve(lambda e: e.scalar_tensor_tensor(out(j), src(j), gain(j), rstd[:], ALU.mult, ALU.mult),
                              t_r, *clear)
                    tokens.append(t)
                    continue
                b = j % 2
                t = k.dve(lambda e: e.scalar_tensor_tensor(tmp[b][:], src(j), gain(j), rstd[:], ALU.mult, ALU.mult),
                          t_r, f"tmp{b}")
                tokens.append(hilo(lambda: ahi[:, dst + j, :], lambda: alo[:, dst + j, :], tmp[b][:], t, *clear,
                                   shift=shift(j) if shift else None, mark=f"tmp{b}"))
            k.mark("rstd", t)
            return tokens

        def unit_of(banks, tokens=None, half=None):
            kts = range(DT) if half is None else range(2 * half, 2 * half + 2)
            return product([(kt * 2 + m, bank(banks[m]), P, ahi[:, kt, :], alo[:, kt, :], kt == 0, kt == DT - 1, kt)
                            for kt in kts for m in range(2)], [f"bank{b}" for b in banks], tokens,
                           last_part=half in (None, 3))

        def wide(tokens, n_units, evac, after_first=None):
            def chunk(c, j, tokens=None):
                banks = (2 * (c % 2), 2 * (c % 2) + 1)
                t = unit_of(banks, tokens)
                if tokens and c == 0 and after_first:
                    after_first()
                evac(j, banks, t)
            for c in range(2):
                chunk(c, 2 * c, tokens)
            if n_units >= 4:
                k.loop(n_units // 2 - 1, lambda i: [chunk(c, i * 4 + (4 + 2 * c)) for c in range(2)])
            if n_units % 2:
                chunk(0, 2 * n_units - 2)

        def into(dst):
            def evac(j, banks, t):
                k.act(lambda e: e.activation(one(dst, j), bank(banks[0]), ACT.Copy), t, mark=f"bank{banks[0]}")
                k.dve(lambda e: e.tensor_copy(one(dst, j + 1), bank(banks[1])), t, mark=f"bank{banks[1]}")
            return evac

        def into_scaled(dst):
            def evac(j, banks, t):
                for m in range(2):
                    k.dve(lambda e: e.tensor_tensor(one(dst, j + m), bank(banks[m]), rstd[:], ALU.mult), t, "rstd",
                          mark=f"bank{banks[m]}")
            return evac

        def one(dst, j, rows=P, lo=0):
            if isinstance(j, int):
                return dst[lo:lo + rows, j, :]
            return dst[lo:lo + rows, bass.ds(j, 1), :].rearrange("p a n -> p (a n)")

        def clear_sum():
            k.dve(lambda e: e.memset(rstd[:], 0.0), "rstd", last("dve"), mark="sum")

        def residual(scale, gain=None):
            def evac(j, banks, t):
                for m in range(2):
                    tx = k.dve(lambda e: e.scalar_tensor_tensor(one(x, j + m), bank(banks[m]), scale(j + m), one(x, j + m),
                                                                ALU.mult, ALU.add), t, mark=f"bank{banks[m]}")
                    tq = k.act(lambda e: e.activation(sq[m][:], one(x, j + m), ACT.Square), tx, f"sq{m}")
                    if gain:
                        split_input(j + m, gain, tx, m)
                    ts = k.dve(lambda e: e.tensor_tensor(rstd[:], rstd[:], sq[m][:], ALU.add), tq, "sum", mark="sum")
                    k.mark(f"sq{m}", ts)
            return evac

        def split_input(j, gain, t, m):
            t = k.dve(lambda e: e.tensor_scalar(tmp[m][:], one(x, j), gain(j), None, ALU.mult), t, f"tmp{m}")
            return hilo(lambda: one(ahi, j), lambda: one(alo, j), tmp[m][:], t, "ahi_read", mark=f"tmp{m}")

        def root(extra=None):
            t = k.pe(lambda e: e.matmul(bank(5), C("ones"), rstd[:], start=True, stop=True), "sum", "bank5")
            t = k.act(lambda e: e.activation(rstd[:], bank(5), ACT.Sqrt, bias=EPS, scale=1.0 / D), t, mark="bank5")
            k.dve(lambda e: e.reciprocal(rstd[:], rstd[:]), t, mark="rstd")

        def down(scale, gain):
            clear_sum()

            def body(i):
                for c in range(2):
                    banks = (2 * c, 2 * c + 1)
                    for part in range(3):
                        n = min(8, FT - 8 * part)
                        t = product([(kt * 2 + m, bank(banks[m]), P, hhi[:, 8 * part + kt, :], hlo[:, 8 * part + kt, :],
                                      part + kt == 0, 8 * part + kt == FT - 1, 0)
                                     for kt in range(n) for m in range(2)],
                                    [f"bank{b}" for b in banks] + ["hidden"])
                    evac = residual(scale, gain)
                    evac(i * 4 + 2 * c, banks, t)
                    k.mark(f"a{c}", last("dve"))
            k.loop(2, body)

        def down_inputs():
            return ["a0"] * 6 + ["a1"] * 2

        def last(engine):
            return Token(engine, k.count[engine], tuple(k.loops))

        def used():
            return count("use", k.count["use"])

        def plain_pair(i, tokens=None, after_first=None):
            tg = unit_of((0, 1), tokens)
            if after_first:
                after_first()
            ts = []
            for m in range(2):
                t = k.dve(lambda e: e.tensor_tensor(tmp[m][:], bank(m), rstd[:], ALU.mult), tg, f"tmp{m}", "rstd", mark=f"bank{m}")
                ts.append(k.act(lambda e: e.activation(tmp[m][:], tmp[m][:], ACT.Silu), t))
                ts[m] = k.pool(lambda e: e.tensor_tensor(tmp[m][:], tmp[m][:], rstd[:], ALU.mult), ts[m])
            tv = unit_of((2, 3), tokens)
            for m in range(2):
                t = k.dve(lambda e: e.tensor_tensor(tmp[m][:], tmp[m][:], bank(2 + m), ALU.mult), tv, ts[m],
                          mark=f"bank{2 + m}")
                hilo(lambda: one(hhi, i * 2 + m), lambda: one(hlo, i * 2 + m), tmp[m][:], t, mark=f"tmp{m}")

        def conv_pair(i, tokens=None, after_first=None):
            def conv(b, dst, off, t, name):
                j = i * 2 + off
                t = k.act(lambda e: e.activation(dst[:], bank(b), ACT.Identity, bias=dyn(cols, j + COL["b_conv"]),
                                                 scale=dyn(cols, j + COL["w_conv2"])), t, name)
                for d, w in ((1, "w_conv1"), (2, "w_conv0")):
                    t = k.dve(lambda e: e.scalar_tensor_tensor(dst[:, d:], bank(b, n=S - d), dyn(cols, j + COL[w]), dst[:, d:],
                                                               ALU.mult, ALU.add), t)
                k.mark(f"bank{b}", t)
                return t
            tg = unit_of((0, 1), tokens)
            ts = []
            for m in range(2):
                t = conv(m, tmp[m], m, tg, f"tmp{m}")
                ts.append(k.act(lambda e: e.activation(tmp[m][:], tmp[m][:], ACT.Silu), t))
            tv = unit_of((2, 3), tokens)
            for m in range(2):
                t = conv(2 + m, tmp[2 + m], FT + m, tv, f"tmp{2 + m}")
                t = k.dve(lambda e: e.tensor_tensor(tmp[m][:], tmp[m][:], tmp[2 + m][:], ALU.mult), t, ts[m],
                          mark=f"tmp{2 + m}")
                hilo(lambda: one(hhi, i * 2 + m), lambda: one(hlo, i * 2 + m), tmp[m][:], t, mark=f"tmp{m}")

        def feed_forward(pair_of, tokens, scale, gain, after_first=None):
            pair_of(0, tokens, after_first)
            k.loop(HALF - 1, lambda i: pair_of(i + 1))
            k.mark("hidden", last("act"), last("dve"))
            k.mark("ahi_read", used())
            for e in ("act", "dve"):
                k.wait(e, "lc")
            down(scale, gain)

        def head_norm(src, dst, rows, ones_name, gain, t_in, b, s, tables=None):
            t = k.act(lambda e: e.activation(sq[s][0:rows, :], src(), ACT.Square), f"sq{s}", *t_in)
            t = k.pe(lambda e: e.matmul(bank(b, rows), C(ones_name)[0:rows, 0:rows], sq[s][0:rows, :], start=True, stop=True),
                     t, f"bank{b}", mark=f"sq{s}", apart=True)
            t = k.act(lambda e: e.activation(sq[s][0:rows, :], bank(b, rows), ACT.Sqrt, bias=EPS[0:rows]), t)
            t = k.dve(lambda e: e.reciprocal(sq[s][0:rows, :], sq[s][0:rows, :]), t)
            y = tmp[s]
            if tables is None:
                t = k.dve(lambda e: e.scalar_tensor_tensor(dst(), src(), gain[0:rows], sq[s][0:rows, :], ALU.mult, ALU.mult), t)
                k.mark(f"sq{s}", t)
                k.mark(f"bank{b}", t)
                return t
            cos, sin, perm = tables
            ty = k.dve(lambda e: e.scalar_tensor_tensor(y[0:rows, :], src(), gain[0:rows], sq[s][0:rows, :], ALU.mult, ALU.mult),
                       t, f"tmp{s}")
            t = k.pe(lambda e: e.matmul(bank(b, rows), C(perm)[0:rows, 0:rows], y[0:rows, :], start=True, stop=True), ty)
            t2 = k.dve(lambda e: e.tensor_tensor(sq[s][0:rows, :], bank(b, rows), sin[0:rows, :], ALU.mult), t)
            t1 = k.pool(lambda e: e.tensor_tensor(y[0:rows, :], y[0:rows, :], cos[0:rows, :], ALU.mult), t)
            t = k.dve(lambda e: e.tensor_tensor(dst(), y[0:rows, :], sq[s][0:rows, :], ALU.add), t1, t2)
            for name in (f"sq{s}", f"bank{b}", f"tmp{s}"):
                k.mark(name, t)
            return t

        QAT = {3: (0, 0, 0), 2: (1, 0, 512), 0: (1, 384, 896), 1: (2, 0, 1024)}
        KAT = {0: (0, 0, 0), 1: (1, 0, 512), 3: (1, 384, 896), 2: (2, 0, 1024)}
        PACKED = 1280

        def scores_steps(q, key, d, lo, strip, scale, E, stat, slot, ready, t_strip=()):
            done = {}
            for i in (3, 2, 0, 1):
                b, off, _ = QAT[i]
                done[i] = k.pe(lambda e: e.matmul(ps[:, b, off:off + P * (i + 1)], q[lo:lo + d, P * i:P * (i + 1)],
                                                  key[lo:lo + d, 0:P * (i + 1)], start=True, stop=True),
                               *ready, f"bank{b}")
            done[2] = done[0]
            for i in (3, 2, 0, 1):
                b, off, at = QAT[i]
                tm = k.dve(lambda e: e.tensor_tensor_reduce(
                    out=E[:, at:at + P * (i + 1)], in0=ps[:, b, off:off + P * (i + 1)],
                    in1=strip[:, S - P * (i + 1):S], scale=scale, scalar=-3e38, op0=ALU.add, op1=ALU.max,
                    accum_out=stat[:, i:i + 1]), done[i], f"E{slot}", *t_strip, mark=f"bank{b}", apart=True)
            t = k.dve(lambda e: e.tensor_scalar(stat[:, 4:8], stat[:, 0:4], -1.0, None, ALU.mult), tm)
            yield
            for i in (3, 2, 0, 1):
                at = QAT[i][2]
                te = k.act(lambda e: e.activation(E[:, at:at + P * (i + 1)], E[:, at:at + P * (i + 1)], ACT.Exp,
                                                  bias=stat[:, 4 + i:5 + i], accum_out=stat[:, 8 + i:9 + i]), t)
            yield k.dve(lambda e: e.reciprocal(stat[:, 12:16], stat[:, 8:12]), te)

        def scores(*args):
            return list(scores_steps(*args))[-1]

        def mix_values(E, t_e, PT, vtok, dv, lo, t_v):
            tp = []
            for b, w, at in ((0, 512, 0), (1, 512, 512), (2, 256, 1024)):
                tb = (3, 4, 3)[b]

                def make(e):
                    for j in range(4):
                        if KAT[j][0] == b:
                            for i in range(j, 4):
                                src = QAT[i][2] + P * j
                                to = KAT[j][1] + P * (i - j)
                                ins = e.transpose(ps[:, tb, to:to + P], E[:, src:src + P], C("ident"))
                    return ins
                tt = k.pe(make, *t_e, f"bank{tb}")
                tp.append(k.act(lambda e: e.activation(PT[:, at:at + w], ps[:, tb, 0:w], ACT.Copy), tt, "PT",
                                mark=f"bank{tb}"))
            yield tt

            def make(e):
                for j in range(4):
                    at = KAT[j][2]
                    ins = e.matmul(ps[lo:lo + dv, 5, P * j:S], vtok[:, j, :], PT[:, at:at + S - P * j],
                                   start=(j == 0), stop=(j == 3))
                return ins
            t = k.pe(make, tp[-1], *t_v, "bank5")
            k.mark("PT", t)
            yield t

        def weave(*plans):
            turn, live = 0, list(plans)
            while live:
                for plan in list(live):
                    if plan[0] <= turn and next(plan[1], "end") == "end":
                        live.remove(plan)
                turn += 1

        z1 = region("z1", 0, [P, 19, S])
        qt = region("qt", 19, [P, 8, S])
        kvt = region("kvt", 27, [P, 8, S])
        tables = [region(f"table{n}", 35 + n, [P, S]) for n in range(4)]
        strip_causal = region("strip_causal", 40, [P, S])
        strip_dil = region("strip_dil", 41, [P, S])
        angle = region("angle", 0, [P, 4, S])
        pos_i = region("pos_i", 4, [1, S], I32)
        pos_f = region("pos_f", 5, [1, S])
        rel = region("rel", 6, [32, 8])
        onehot = region("onehot", 7, [P, 2 * 640])
        dist = region("dist", 10, [8, 640])
        hankel = region("hankel", 12, [P, 8, S])
        flip = region("flip", 20, [P, P])
        flipped = region("flipped", 21, [P, 8, S])

        t_pos = k.dma("act", "d_pos", pos_i[:], pos_in)
        t_strip = k.dma("act", "d_strip", strip_causal[:], strip_in[0])
        t_strip2 = k.dma("act", "d_strip2", strip_dil[:], strip_in[1])
        t_rel = k.dma("act", "d_rel", rel[:], rel_in)
        t_hot = k.dma("act", "d_hot", onehot[:], bucket_in[:, 0:1280])
        t_flip = k.dma("act", "d_flip", flip[:], bucket_in[:, 1280:1280 + P])

        t_c = k.act(lambda e: e.activation(small[:, 8:16], cols[:, COL["c"]:COL["c"] + 8], ACT.Silu), t_cols)

        def make(e):
            e.matmul(ps[0:8, 4, :], rel[:], onehot[0:32, 0:512], start=True, stop=True)
            return e.matmul(ps[0:8, 5, 0:128], rel[:], onehot[0:32, 512:640], start=True, stop=True)
        t = k.pe(make, t_rel, t_hot)
        k.dve(lambda e: e.scalar_tensor_tensor(dist[:, 0:512], ps[0:8, 4, :], 8.0, onehot[0:8, 640:1152], ALU.mult, ALU.add), t, t_hot)
        t = k.dve(lambda e: e.scalar_tensor_tensor(dist[:, 512:640], ps[0:8, 5, 0:128], 8.0, onehot[0:8, 1152:1280], ALU.mult, ALU.add))
        t = k.dma("act", "d_scratch", scratch, dist[:], t)
        t = k.dma("act", "d_hankel", hankel[:], bass.AP(tensor=scratch.tensor, offset=0, ap=[[1, P], [640, 8], [1, S]]), t)
        tf = []
        for h in range(8):
            b = 4 + h % 2
            t1 = k.pe(lambda e: e.matmul(bank(b), flip[:], hankel[:, h, :], start=True, stop=True), t, t_flip, f"flip{h % 2}")
            tf.append(k.dve(lambda e: e.tensor_copy(flipped[:, h, :], bank(b)), t1, mark=f"flip{h % 2}"))
        t_strips = k.dma("act", "d_strips", strips_dram.rearrange("h p n -> p h n"), flipped[:], tf[-1])

        t = k.dve(lambda e: e.tensor_copy(pos_f[:], pos_i[:]), t_pos)
        t_p = k.pe(lambda e: e.matmul(bank(6), C("ones")[0:1, :], pos_f[:], start=True, stop=True), t, t_const)
        TWO_PI = 2 * math.pi
        C1 = 6.28125
        C2 = float(np.round((TWO_PI - C1) * 2 ** 22) / 2 ** 22)
        C3 = TWO_PI - C1 - C2
        MAGIC = 1.5 * 2 ** 23
        for n, f in enumerate(("freq_dil", "freq_mla")):
            a, m, r, q = (angle[:, j, :] for j in range(4))
            cos, sin = tables[2 * n], tables[2 * n + 1]
            t = k.dve(lambda e: e.tensor_scalar(a, bank(6), col(f), None, ALU.mult), t_p, t_cols, "angle")
            t = k.dve(lambda e: e.tensor_scalar(m, a, 1.0 / TWO_PI, MAGIC, ALU.mult, ALU.add), t)
            t = k.dve(lambda e: e.tensor_scalar(m, m, -MAGIC, None, ALU.add), t)
            for c in (C1, C2, C3):
                t = k.dve(lambda e: e.scalar_tensor_tensor(a, m, -c, a, ALU.mult, ALU.add), t)
            t = k.dve(lambda e: e.tensor_scalar(a, a, 3.1415925, -3.1415925, ALU.min, ALU.max), t)
            t1 = k.act(lambda e: e.activation(sin[:], a, ACT.Sin), t)
            t = k.act(lambda e: e.activation(r, a, ACT.Abs), t)
            t = k.act(lambda e: e.activation(cos[:], r, ACT.Sin, bias=HALF_PI, scale=-1.0), t, mark="angle")
        t_tab = t
        k.mark("bank6", t)
        k.mark("bank4", tf[-1])
        k.mark("bank5", tf[-1])

        def ada(j, bank_of):
            rows, turned = bank_of
            for m in range(2):
                r, loaded, v = take()
                if not k.dry:
                    L = k.loops[-1] if k.loops else None
                    ada_at.extend((j if isinstance(j, int) else n, v + n * (L.per["take"] if L else 0), m)
                                  for n in range(L.n if L else 1))

                def make(e):
                    for kt in range(DT):
                        ins = e.matmul(ps[0:1, rows[m], 0:2 * P], small[:, 8 + kt:9 + kt], raw[r][:, 2 * kt:2 * kt + 2, :],
                                       start=(kt == 0), stop=(kt == DT - 1))
                    return ins
                t = k.pe(make, loaded, t_c, f"bank{rows[m]}", sem=f"free{r}")
                t = count(f"free{r}", k.count[f"free{r}"])
                k.dve(lambda e: e.tensor_copy(ada_row[:, m, :], ps[0:1, rows[m], 0:2 * P]), t, "ada_row", mark=f"bank{rows[m]}")

            def make(e):
                for n in range(4):
                    ins = e.matmul(ps[:, turned, n:n + 1], ada_row[0:1, n // 2, P * (n % 2):P * (n % 2) + P], ONE,
                                   start=True, stop=True)
                return ins
            t = k.pe(make, last("dve"), f"bank{turned}", mark="ada_row")
            k.dve(lambda e: e.tensor_tensor(dyn(mod, j * 4, 4), ps[:, turned, 0:4], dyn(cols, j * 4 + COL["b_ada"], 4), ALU.add),
                  t, mark=f"bank{turned}")

        k.loop(ADA_EARLY // 2, lambda i: ada(i, ((0, 1), 2)))
        t_mod = last("dve")
        def scaled_gain(n, g, c):
            t = k.dve(lambda e: e.tensor_scalar(gcol[:, 8 * n:8 * n + 8], mod[:, c:c + 8], 1.0, None, ALU.add), last("dve"))
            return k.dve(lambda e: e.tensor_tensor(gcol[:, 8 * n:8 * n + 8], gcol[:, 8 * n:8 * n + 8],
                                                   cols[:, COL[g]:COL[g] + 8], ALU.mult), t)
        t_g = scaled_gain(0, "g_mix", 8)
        for _ in range(2):
            split()

        tokens = norm(lambda j: x[:, j, :], DT, D, lambda j: gcol[:, j:j + 1], lambda j: mod[:, j:j + 1],
                      ready=(t_x,), clear=(t_g,))
        k.wait("act", t_strips, t_g)
        k.wait("dve", t_strips)

        wide(dict(enumerate(tokens)), U_IN1 - 1, into(z1))
        t = product([(kt * 2, bank(2, 96), 96, ahi[:, kt, :], alo[:, kt, :], kt == 0, kt == DT - 1, kt)
                     for kt in range(DT)], ["bank2"])
        t_z = k.act(lambda e: e.activation(z1[0:96, 18, :], bank(2, 96), ACT.Copy), t, mark="bank2")
        t_zd = last("dve")

        tok_q = norm(lambda j: z1[:, j, :], 4, 512, lambda j: col("g_q_lat", j), ready=(t_z, t_zd), clear=(used(),))
        for u in range(U_QB):
            banks = range(4)
            t = product([(kt * 4 + h, bank(h, 96), 96, ahi[:, kt, :], alo[:, kt, :], kt == 0, kt == 3, kt)
                         for kt in range(4) for h in range(4)], [f"bank{b}" for b in banks], tok_q)
            for h in range(4):
                if h % 2:
                    k.act(lambda e: e.activation(qt[0:96, 4 * u + h, :], bank(h, 96), ACT.Copy), t, mark=f"bank{h}")
                else:
                    k.dve(lambda e: e.tensor_copy(qt[0:96, 4 * u + h, :], bank(h, 96)), t, mark=f"bank{h}")
        tok_kv = norm(lambda j: z1[:, 4 + j, :], 2, 256, lambda j: col("g_kv_lat", j), dst=4, ready=(t_z, t_zd),
                      clear=(t_z,))
        t = product([(kt * 8 + h, bank(h if h < 7 else 7), P, ahi[:, 4 + kt, :], alo[:, 4 + kt, :], kt == 0, kt == 1, kt)
                     for h in range(8) for kt in range(2)], [f"bank{b}" for b in range(8)], tok_kv)
        for h in range(8):
            if h % 2:
                k.act(lambda e: e.activation(kvt[:, h, :], bank(h), ACT.Copy), t, mark=f"bank{h}")
            else:
                k.dve(lambda e: e.tensor_copy(kvt[:, h, :], bank(h)), t, mark=f"bank{h}")
        t_a, t_d = last("act"), last("dve")

        rot_q = (tables[2], tables[3], "permq")
        rot_d = (tables[0], tables[1], "perm64")
        head_norm(lambda: z1[0:96, 18, :], lambda: z1[0:96, 18, :], 96, "blkq", col("g_k"), (t_a, t_d, t_tab), 4, 0, rot_q)

        def prep_mla(i):
            for s in range(2):
                head_norm(lambda: one(qt, i * 2 + s, 96), lambda: one(qt, i * 2 + s, 96), 96, "blkq", col("g_q"),
                          (t_a, t_d, t_tab), 4 + s, s, rot_q)
                head_norm(lambda: one(kvt, i * 2 + s, 64), lambda: one(kvt, i * 2 + s, 64), 64, "blk64", col("g_k"),
                          (), 4 + s, s)
        k.loop(4, prep_mla)

        def prep_dil(i):
            for s, (base, g) in enumerate(((6, "g_dq"), (10, "g_dk"))):
                head_norm(lambda: one(z1, i + base), lambda: one(z1, i + base), P, "blk64", col(g), (), 4 + s, s, rot_d)
        k.loop(4, prep_dil)
        t_prep = (last("dve"), last("act"), last("pe"), last("pool"))

        E = [region(f"E{s}", 2.5 * s, [P, PACKED]) for s in range(2)]
        PT = region("PT", 35, [P, PACKED])
        vtok = region("vtok", 5, [P, 4, P])
        qs = [region("qs0", 37.5, [P, S]), region("qs1", 38.5, [P, S])]
        ks = [region("ks0", 42, [P, S]), region("ks1", 43, [P, S])]
        stat = [place(f"stat{s}", [P, 16]) for s in range(2)]

        for e in ("act", "dve", "pool", "pe"):
            k.wait(e, *t_prep)
        for s in range(2):
            t_kpe = k.dve(lambda e: e.tensor_copy(ks[s][64:96, :], z1[64:96, 18, :]))

        def attend_heads(heads, strip, scale, i, dst, j_ada):
            st = []
            for s, (q, key, d, lo, t_qk, V, olo) in enumerate(heads):
                t = scores(q, key, d, lo, strip, scale, E[s], stat[s], s, t_qk, (t_strip, t_strip2))
                k.mark(f"QK{s}", last("pe"))
                for b in (3, 2, 0, 1):
                    at = QAT[b][2]
                    t2 = k.dve(lambda e: e.tensor_scalar(E[s][:, at:at + P * (b + 1)], E[s][:, at:at + P * (b + 1)],
                                                         stat[s][:, 12 + b:13 + b], None, ALU.mult), t)
                st.append(t2)
            for s, (q, key, d, lo, t_qk, V, olo) in enumerate(heads):
                t_v, v = V(s)
                t_tr, t_o = mix_values(E[s], (st[s],), PT, v, 64, olo, (t_v,))
                k.mark(f"E{s}", t_tr)
                k.mark("vtok", t_o)
                o = ps[olo:olo + 64, 5, :]
                hilo(lambda: one(ahi, dst(i), 64, olo), lambda: one(alo, dst(i), 64, olo), o, t_o, mark="bank5")
            ada(i + j_ada, ((6, 7), 6))

        def mla(i):
            heads = []
            for s in range(2):
                t1 = k.pool(lambda e: e.tensor_copy(qs[s][0:96, :], one(qt, i * 2 + s, 96)), f"QK{s}")
                t2 = k.pool(lambda e: e.tensor_copy(ks[s][0:64, :], one(kvt, i * 2 + s, 64)))
                t3 = k.pool(lambda e: e.tensor_copy(sq[s][:], one(kvt, i * 2 + s)), f"V{s}")

                def values(s, t3=t3):
                    def make(e):
                        for j in range(4):
                            ins = e.transpose(ps[:, 4, P * j:P * (j + 1)], sq[s][:, P * j:P * (j + 1)], C("ident"))
                        return ins
                    t = k.pe(make, t3, "bank4", mark=f"V{s}")
                    t = k.act(lambda e: e.activation(vtok[:, :, 64 * s:64 * s + 64],
                                                     ps[:, 4, :].rearrange("p (j d) -> p j d", j=4)[:, :, 64:128], ACT.Copy),
                              t, f"vtok", mark="bank4")
                    return t, vtok[:, :, 64 * s:64 * s + 64]
                heads.append((qs[s], ks[s], 96, 0, (t2, t_kpe), values, 64 * s))
            attend_heads(heads, strip_causal, (96.0) ** -0.5, i, lambda i: i, ADA_EARLY // 2)
        k.loop(4, mla)

        def dil(i):
            t1 = k.pool(lambda e: e.tensor_copy(qs[0][:], one(z1, i + 6)), "QK0", "QK1")
            t2 = k.pool(lambda e: e.tensor_copy(ks[0][:], one(z1, i + 10)))
            t3 = k.pool(lambda e: e.tensor_copy(sq[0][:], one(z1, i + 14)), "V0")

            def values(s):
                if s == 0:
                    def make(e):
                        for j in range(4):
                            ins = e.transpose(ps[:, 4, P * j:P * (j + 1)], sq[0][:, P * j:P * (j + 1)], C("ident"))
                        return ins
                    t = k.pe(make, t3, "bank4", mark="V0")
                    values.t = k.act(lambda e: e.activation(vtok[:], ps[:, 4, :].rearrange("p (j d) -> p j d", j=4), ACT.Copy),
                                     t, "vtok", mark="bank4")
                return values.t, vtok[:, :, 64 * s:64 * s + 64]
            heads = [(qs[0], ks[0], 64, 64 * s, (t2,), values, 64 * s) for s in range(2)]
            attend_heads(heads, strip_dil, 64.0 ** -0.5, i, lambda i: i + 4, ADA_EARLY // 2 + 4)
        k.loop(4, dil)
        tok_mix = [last("dve")] * DT
        t_g = scaled_gain(1, "g_ffn", 32)
        for e in ("pe", "act", "dve"):
            k.wait(e, last("dve"), last("act"), last("pe"))

        clear_sum()
        wide(tok_mix, U_O, residual(lambda j: dyn(mod, j + 16)))
        t_x, t_used = last("dve"), used()
        root()
        tokens = []
        for j in range(DT):
            b = j % 2
            t = k.dve(lambda e: e.scalar_tensor_tensor(tmp[b][:], x[:, j, :], gcol[:, 8 + j:9 + j], rstd[:], ALU.mult, ALU.mult),
                      "rstd", f"tmp{b}", t_x)
            tokens.append(hilo(lambda: ahi[:, j, :], lambda: alo[:, j, :], tmp[b][:], t, t_used,
                               shift=mod[:, 24 + j:25 + j], mark=f"tmp{b}"))
        feed_forward(conv_pair, tokens, lambda j: dyn(mod, j + 40), lambda j: dyn(cols, j + COL["ffn1_0"]))

        def skip():
            product([(0, bank(6), P, ahi[:, 0, :], alo[:, 0, :], True, True, 0)], ["bank6"])
            k.mark("bank6", used())
        for _ in range(U_PAD):
            skip()

        z2 = region("z2", 0, [P, FT, S])
        EE = [[region(f"EE{h}{m}", 22 + 5 * h + 2.5 * m, [P, PACKED]) for m in range(2)] for h in range(2)]
        PT2 = region("PTT", 32, [P, PACKED])
        vtok2 = region("vtok2", 34.5, [P, 4, P])
        strip2 = [[region(f"strip{h}{m}", 35.5 + 2 * h + m, [P, S]) for m in range(2)] for h in range(2)]
        W = [region(f"W{n}", 39.5 + n, [P, S]) for n in range(4)] + [tmp[3]]
        stat4 = [stat, [place(f"stat{s}", [P, 16]) for s in range(2, 4)]]
        bd = place("bd", [P, 4, P])

        def head(h):
            slot = h % 2
            E0, E1 = EE[slot]
            st = []
            for m in range(2):
                t_s = k.dma("pool", f"d_st{slot}{m}", strip2[slot][m][:], strips_dram[2 * h + m], f"strip{slot}{m}")
                E, stat = EE[slot][m], stat4[slot][m]
                t_r = None
                for part in scores_steps(z2[:, h, :], z2[:, 4 + h, :], 64, 64 * m, strip2[slot][m], 0.125, E, stat,
                                         f"{slot}{m}", (), (t_s,)):
                    t_r = part
                    yield
                k.mark(f"strip{slot}{m}", t_r)
                st.append(t_r)
                if m == 0:
                    def make(e):
                        for j in range(4):
                            ins = e.transpose(ps[:, 4, P * j:P * (j + 1)], z2[:, 8 + h, P * j:P * (j + 1)], C("ident"))
                        return ins
                    t = k.pe(make, "bank4")
                    t_v = k.act(lambda e: e.activation(vtok2[:], ps[:, 4, :].rearrange("p (j d) -> p j d", j=4), ACT.Copy),
                                t, "vtok", mark="bank4")
            stat0, stat1 = stat4[slot]
            t = k.dve(lambda e: e.tensor_scalar(stat1[:, 12:16], stat1[:, 12:16], small[:, 21:22], None, ALU.mult), st[1])
            for i in (3, 2, 0, 1):
                at, w = QAT[i][2], P * (i + 1)
                t1 = k.dve(lambda e: e.tensor_scalar(E1[:, at:at + w], E1[:, at:at + w], stat1[:, 12 + i:13 + i],
                                                     None, ALU.mult), t)
            for i in (3, 2, 0, 1):
                at, w = QAT[i][2], P * (i + 1)
                t2 = k.dve(lambda e: e.scalar_tensor_tensor(E0[:, at:at + w], E0[:, at:at + w], stat0[:, 12 + i:13 + i],
                                                            E1[:, at:at + w], ALU.mult, ALU.add), t1)
            k.mark(f"E{slot}1", t2)
            yield
            two = mix_values(E0, (t2,), PT2, vtok2, P, 0, (t_v,))
            k.mark(f"E{slot}0", next(two))
            yield
            t_o = next(two)
            k.mark("vtok", t_o)
            t = k.act(lambda e: e.activation(sq[0][:], bank(5), ACT.Square), t_o, "sq0")
            yield
            t = k.pe(lambda e: e.matmul(bank(4), C("ones"), sq[0][:], start=True, stop=True), t, "bank4")
            t = k.act(lambda e: e.activation(sq[0][:], bank(4), ACT.Sqrt, bias=SUB_EPS, scale=1.0 / P), t, mark="bank4")
            t = k.dve(lambda e: e.reciprocal(sq[0][:], sq[0][:]), t)
            mixed[h] = k.dve(lambda e: e.scalar_tensor_tensor(z2[:, h, :], bank(5), small[:, 22:23], sq[0][:],
                                                              ALU.mult, ALU.mult), t, mark="bank5")
            k.mark("sq0", mixed[h])

        def shifted(dst, src, taps, *waits, bias=None):
            if bias is not None:
                t = k.act(lambda e: e.activation(dst, src, ACT.Identity, bias=bias, scale=taps[0]), *waits)
            else:
                t = k.act(lambda e: e.activation(dst, src, ACT.Copy, scale=taps[0]), *waits)
            for d in range(1, len(taps)):
                t = k.dve(lambda e: e.scalar_tensor_tensor(dst[:, d:], src[:, 0:S - d], taps[d], dst[:, d:],
                                                           ALU.mult, ALU.add), t)
            return t

        def decay():
            n2 = slice(LCOL["lambda"], LCOL["lambda"] + 2)
            sc = [small[:, 4:6], small[:, 6:8]] + [small[:, 24 + 2 * n:26 + 2 * n] for n in range(4)]
            t = k.act(lambda e: e.activation(sc[0], lc[:, n2], ACT.Abs), "decay")
            t = k.act(lambda e: e.activation(sc[0], sc[0], ACT.Exp, scale=-1.0), t)
            t = k.dve(lambda e: e.tensor_scalar(sc[1], sc[0], 1.0, None, ALU.add), t)
            t1 = k.act(lambda e: e.activation(sc[2], sc[1], ACT.Ln), t)
            t = k.dve(lambda e: e.tensor_scalar(sc[3], sc[1], -1.0, None, ALU.add), t)
            t = k.dve(lambda e: e.tensor_scalar(sc[4], sc[3], 0.0, None, ALU.is_equal), t)
            t = k.dve(lambda e: e.tensor_tensor(sc[3], sc[3], sc[4], ALU.add), t)
            t = k.dve(lambda e: e.reciprocal(sc[3], sc[3]), t)
            t = k.dve(lambda e: e.tensor_tensor(sc[2], sc[2], sc[4], ALU.add), t, t1)
            t = k.dve(lambda e: e.tensor_tensor(sc[2], sc[2], sc[3], ALU.mult), t)
            t = k.dve(lambda e: e.tensor_tensor(sc[2], sc[2], sc[0], ALU.mult), t)
            t = k.dve(lambda e: e.tensor_scalar(sc[5], lc[:, n2], 0.0, None, ALU.min), t)
            t = k.dve(lambda e: e.tensor_tensor(sc[2], sc[2], sc[5], ALU.subtract), t)
            return k.dve(lambda e: e.tensor_scalar(sc[2], sc[2], -8.0, None, ALU.mult), t)

        def recurrence(f, t_sp, t_x, t_bd):
            nsp = small[:, 24 + f:25 + f]
            xr, r, g, a, th = (w[:] for w in W)
            t_xr = shifted(xr, z2[:, 12 + f, :], [lcol("lru_w", 2 * n + f) for n in (3, 2, 1, 0)], t_x, "W",
                           bias=lcol("lru_b", f))
            yield
            t_g1 = k.pe(lambda e: e.matmul(bank(3), bd[:, f, :], xr, start=True, stop=True), t_xr, "bank3", t_bd)
            t_r = k.act(lambda e: e.activation(r, bank(3), ACT.Sigmoid, bias=lcol("ba", f)), t_g1, mark="bank3")
            t_g2 = k.pe(lambda e: e.matmul(bank(4), bd[:, 2 + f, :], xr, start=True, stop=True), "bank4")
            t_i = k.act(lambda e: e.activation(g, bank(4), ACT.Sigmoid, bias=lcol("bx", f)), t_g2, mark="bank4")
            yield
            t_a = k.act(lambda e: e.activation(a, r, ACT.Exp, scale=nsp), t_r, t_sp)
            t_t = k.act(lambda e: e.activation(th, r, ACT.Tanh, scale=nsp), t_r)
            t1 = k.pool(lambda e: e.tensor_tensor(g, g, xr, ALU.mult), t_i)
            yield
            t = k.dve(lambda e: e.tensor_scalar(r, th, -1.0, None, ALU.add), t_t, t_a)
            t = k.dve(lambda e: e.reciprocal(r, r), t)
            t = k.dve(lambda e: e.scalar_tensor_tensor(th, th, 2.0, r, ALU.mult, ALU.mult), t)
            t = k.dve(lambda e: e.tensor_scalar(th, th, 2.0 ** -116, None, ALU.max), t)
            t = k.act(lambda e: e.activation(th, th, ACT.Sqrt), t)
            yield
            t = k.dve(lambda e: e.tensor_tensor(g, g, th, ALU.mult), t, t1)
            rec[f] = k.dve(lambda e: e.tensor_tensor_scan(z2[:, 12 + f, :], a, g, 0.0, ALU.mult, ALU.add), t, mark="W")

        def short_conv(f, t_x):
            p = z2[:, 18 + f, :]
            t = k.pool(lambda e: e.tensor_tensor(p, z2[:, 16 + f, :], p, ALU.mult), t_x)
            t = shifted(tmp[1][:], p, [lcol("sc_w", 2 * n + f) for n in (2, 1, 0)], t, "tmp1")
            yield
            mixed[4 + f] = k.dve(lambda e: e.tensor_tensor(z2[:, 14 + f, :], tmp[1][:], z2[:, 14 + f, :], ALU.mult), t,
                                 mark="tmp1")

        def gated(f, t_x):
            t = k.act(lambda e: e.activation(tmp[2][:], z2[:, 20 + f, :], ACT.Gelu_apprx_tanh), t_x, "tmp2")
            mixed[6 + f] = k.dve(lambda e: e.tensor_tensor(z2[:, 12 + f, :], tmp[2][:], z2[:, 12 + f, :], ALU.mult), t, rec[f],
                                 mark="tmp2")

        mixed, rec = {}, {}
        MIXED_AT = (0, 1, 2, 3, 14, 15, 12, 13)

        def split_mixed(n):
            src = z2[:, MIXED_AT[n], :]
            mixed[n] = hilo(lambda: ahi[:, n, :], lambda: alo[:, n, :], src, mixed[n], "ahi_read")

        def layer(l):
            t_lc = k.dma("pool", "d_lc", lc[:], lambda: layer_in[bass.ds(l, 1)].rearrange("a p n -> (a p) n"),
                         last("act"), last("dve"), last("pe"))
            t_bd = k.dma("pool", "d_bd", bd[:], lambda: lru_in[bass.ds(l, 1)].rearrange("a p b n -> (a p) b n"))
            k.mark("lc", t_lc)
            feed_forward(plain_pair, down_inputs(), lambda j: 0.5, lambda j: dyn(lc, j + LCOL["mix"]), root)

            for n in range(2):
                t = k.dve(lambda e: e.tensor_tensor(small[0:64, 16 + n:17 + n], lc[0:64, LCOL["lam"] + 2 * n:LCOL["lam"] + 2 * n + 1],
                                                    lc[0:64, LCOL["lam"] + 2 * n + 1:LCOL["lam"] + 2 * n + 2], ALU.mult), t_lc)
            t_l = t
            wide(down_inputs(), 6, into_scaled(z2), root)
            t_q = last("dve")
            t = k.pe(lambda e: e.matmul(ps[:, 5, 0:2], C("ones")[0:64, :], small[0:64, 16:18], start=True, stop=True), t_l, "bank5")
            t = k.act(lambda e: e.activation(small[:, 18:20], ps[:, 5, 0:2], ACT.Exp), t, mark="bank5")
            t = k.dve(lambda e: e.tensor_tensor(small[:, 20:21], small[:, 18:19], small[:, 19:20], ALU.subtract), t)
            t = k.dve(lambda e: e.tensor_tensor(small[:, 20:21], small[:, 20:21], lcol("lam_init"), ALU.add), t)
            t = k.dve(lambda e: e.tensor_scalar(small[:, 21:22], small[:, 20:21], -1.0, None, ALU.mult), t)
            k.dve(lambda e: e.tensor_tensor(small[:, 22:23], lcol("subln"), lcol("sub_scale"), ALU.mult))
            t_sp = decay()
            k.mark("decay", t_sp)
            for e in ("pe", "act", "dve", "pool"):
                k.wait(e, last("dve"), last("act"), last("pe"), used())

            ready = {}

            def projection():
                for u in range(6, 11):
                    for quarter in range(4):
                        t = unit_of((6, 7), half=quarter)
                        yield
                    for m in range(2):
                        ready[2 * u + m] = k.dve(lambda e: e.tensor_tensor(z2[:, 2 * u + m, :], bank(6 + m), rstd[:], ALU.mult),
                                                 t, mark=f"bank{6 + m}")
                skip()
                k.mark("ahi_read", used())

            def mixers():
                for f in range(2):
                    yield from recurrence(f, t_sp, ready[12 + f], t_bd)
                    yield
                yield
                for f in range(2):
                    yield from short_conv(f, ready[18 + f])

            def finish():
                for f in range(2):
                    gated(f, ready[20 + f])
                for n in (0, 1, 2, 4, 5, 6, 7):
                    yield
                    split_mixed(n)
            weave((0, projection()), (0, head(0)), (6, head(1)), (12, head(2)), (18, head(3)), (8, mixers()), (22, finish()))
            split_mixed(3)

            clear_sum()
            wide(mixed, U_O, residual(lambda j: 1.0))
            t_x = last("dve")
            k.mark("ahi_read", used())
            tokens = [split_input(j, lambda j: lcol("ffn2", j), t_x, j % 2) for j in range(DT)]
            feed_forward(plain_pair, tokens, lambda j: 0.5, lambda j: dyn(lc, j + LCOL["next"]), root)
        k.loop(LAYERS, layer)

        root()
        for j in range(DT):
            k.dve(lambda e: e.scalar_tensor_tensor(x[:, j, :], x[:, j, :], col("final", j), rstd[:], ALU.mult, ALU.mult),
                  "rstd", last("act"))
        k.dma("sp", "d_out", y_out, x[:], last("dve"))
        nc.sync.wait_ge(k.sem("d_out"), 16)
        for s in range(2):
            nc.sync.wait_ge(k.sem(f"ld{s}"), 16 * (U_ALL // 2))
    return sorted(v for _, v, _ in ada_at)


def blocks_of(w, order):
    out = np.zeros((len(order), P, P), w.dtype)
    for n, b in enumerate(order):
        if b is not None:
            kt, c, width = b
            out[n, :, :width] = w[kt * P:(kt + 1) * P, c:c + width]
    return out


def wide_order(n, first=0):
    return [(kt, first + 256 * u + P * m, P) for u in range(n) for kt in range(DT) for m in range(2)]


def down_order():
    order = []
    for pair in range(4):
        for part in range(3):
            blocks = [(8 * part + kt, 256 * pair + P * m, P) for kt in range(min(8, FT - 8 * part)) for m in range(2)]
            order += blocks + [None] * (UB - len(blocks))
    return order


def stream_of(v, ada_at):
    parts = []
    w = v["w_in"][0]
    in1 = wide_order(3)
    in1 += [(kt, 800 + 256 * u + P * m, P) for u in range(6) for kt in range(DT) for m in range(2)]
    for kt in range(DT):
        in1 += [(kt, 704, 96), None]
    parts.append(blocks_of(w, in1))
    parts.append(blocks_of(v["w_q_b"][0], [(kt, 96 * (4 * u + h), 96) for u in range(2) for kt in range(4) for h in range(4)]))
    parts.append(blocks_of(v["w_kv_b"][0], [(kt, P * h, P) for kt in range(2) for h in range(8)]))
    parts.append(blocks_of(v["w_o"][0], wide_order(4)))

    def pairs(a, b, off):
        for j in range(HALF):
            order = [(kt, 256 * j + P * m, P) for kt in range(DT) for m in range(2)]
            parts.append(blocks_of(a, order))
            parts.append(blocks_of(b, [(kt, c + off, w) for kt, c, w in order]))
    pairs(v["w_up"][0], v["w_up"][0], FF)
    parts.append(blocks_of(v["w_down"][0], down_order()))
    parts.append(np.zeros((U_PAD * UB, P, P), np.float32))
    tiles = list(range(12)) + [18, 19] + list(range(12, 18)) + [20, 21]
    in2 = [(kt, P * tiles[2 * u + m], P) for u in range(11) for kt in range(DT) for m in range(2)]
    for l in range(LAYERS):
        for n in (1, 2):
            if n == 2:
                parts.append(blocks_of(v["w_in_2"][l], in2 + [None] * UB))
                parts.append(blocks_of(v["w_out_2"][l], wide_order(4)))
            pairs(v[f"ffn{n}_gate_2"][l], v[f"ffn{n}_up_2"][l], 0)
            parts.append(blocks_of(v[f"ffn{n}_down_2"][l], down_order()))
    parts.append(np.zeros((2 * UB, P, P), np.float32))
    rest = np.concatenate(parts).reshape(-1, UB, P, P)
    ada = blocks_of(v["w_ada"][0], wide_order(U_ADA)).reshape(-1, UB, P, P)
    s = np.empty((U_ALL, UB, P, P), np.float32)
    s[ada_at] = ada
    s[np.setdiff1d(np.arange(U_ALL), ada_at)] = rest
    return np.ascontiguousarray(s.transpose(0, 2, 1, 3))


def columns_of(plan, n, vectors):
    out = np.zeros((P, n), np.float32)
    for name, a in vectors.items():
        a = np.asarray(a).reshape(-1)
        w = -(-a.size // P)
        full = np.zeros(w * P, a.dtype)
        full[:a.size] = a
        out[:, plan[name]:plan[name] + w] = full.reshape(w, P).T
    return out


def constants():
    ident = np.eye(P)
    ones = np.ones((P, P))
    blk64 = np.kron(np.eye(2), np.ones((64, 64)) / 64)
    blkq = np.zeros((P, P))
    blkq[:64, :64] = 1 / 64
    blkq[64:96, 64:96] = 1 / 32
    def swap(m, at, half):
        for j in range(half):
            m[at + half + j, at + j] = -1
            m[at + j, at + half + j] = 1
    perm64, permq = np.zeros((P, P)), np.zeros((P, P))
    swap(perm64, 0, 32)
    swap(perm64, 64, 32)
    swap(permq, 64, 16)
    const = np.concatenate([ident, ones, blk64, blkq, perm64, permq], 1).astype(np.float32)
    dist = np.arange(P)[:, None] - np.arange(S)[None] + 384
    causal = np.where(dist >= 0, 0.0, NEG)
    times = ((dist >= 0) & (dist <= 128)).astype(int) + ((dist >= 0) & (dist % 4 == 0)) + ((dist >= 0) & (dist % 16 == 0))
    dil = np.where(times > 0, 8.0 * np.log(np.maximum(times, 1)), NEG)
    strips = np.stack([causal, dil]).astype(np.float32)
    d = 511 - np.arange(640)
    n = np.maximum(d, 0)
    nf = np.maximum(n, 1).astype(np.float32)
    large = 16 + (np.log(nf / np.float32(16)) / np.float32(math.log(8)) * np.float32(16)).astype(np.int32)
    bucket = np.where(n < 16, n, np.minimum(large, 31))
    table = np.zeros((P, 1280 + P), np.float32)
    table[:32, :640] = bucket[None] == np.arange(32)[:, None]
    table[:8, 640:1280] = np.where(d >= 0, 0.0, NEG)[None]
    table[:, 1280:] = np.eye(P)[::-1]
    return const, strips, table


def kernel(**inputs):
    import concourse.bacc as _bacc
    from concourse.bass_utils import run_bass_kernel_spmd as _run

    v = {name: np.asarray(a) for name, a in inputs.items()}
    const, strips, table = constants()
    freq = {d: (10000.0 ** (-2.0 * np.arange(d // 2) / d)).astype(np.float32) for d in (32, 64)}
    freq_mla = np.zeros(P, np.float32)
    freq_mla[64:96] = np.tile(freq[32], 2)
    cols = columns_of(COL, NCOL, {
        "c": v["c"], "b_ada": v["b_ada"], "g_mix": v["g_mix_norm"], "g_q_lat": v["g_q_lat"], "g_kv_lat": v["g_kv_lat"],
        "g_q": np.concatenate([v["g_mla_q_nope"][0], v["g_mla_q_pe"][0]]),
        "g_k": np.concatenate([v["g_mla_k_nope"][0], v["g_mla_k_pe"][0]]),
        "g_dq": np.tile(v["g_dil_q"][0], 2), "g_dk": np.tile(v["g_dil_k"][0], 2), "g_ffn": v["g_ffn_norm"],
        "w_conv0": v["w_conv"][0, 0], "w_conv1": v["w_conv"][0, 1], "w_conv2": v["w_conv"][0, 2], "b_conv": v["b_conv"],
        "final": v["final_norm_2"], "ffn1_0": v["ffn1_norm_2"][0], "freq_dil": np.tile(freq[64], 4), "freq_mla": freq_mla})
    layers = []
    lru = np.zeros((LAYERS, P, 4, P), np.float32)
    for l in range(LAYERS):
        lam = np.zeros((4, P), np.float32)
        for n, name in enumerate(("lam_q1_2", "lam_k1_2", "lam_q2_2", "lam_k2_2")):
            lam[n, :64] = v[name][l]
        lam_init = 0.8 - 0.6 * math.exp(-0.3 * l)
        layers.append(columns_of(LCOL, NLCOL, {
            "ffn1": v["ffn1_norm_2"][l], "mix": v["mix_norm_2"][l], "ffn2": v["ffn2_norm_2"][l],
            "next": v["ffn1_norm_2"][l + 1] if l + 1 < LAYERS else v["final_norm_2"],
            "subln": v["subln_gain_2"][l], "sc_w": v["sc_conv_w_2"][l], "lru_w": v["lru_conv_w_2"][l],
            "lru_b": v["lru_conv_b_2"][l], "lambda": v["lru_lambda_2"][l], "ba": v["lru_ba_2"][l],
            "bx": v["lru_bx_2"][l], "lam": lam, "lam_init": np.full(P, lam_init), "sub_scale": np.full(P, 1.0 - lam_init)}))
        for n, name in enumerate(("lru_wa_2", "lru_wx_2")):
            for b in range(4):
                at = 64 * (b % 2)
                lru[l, at:at + 64, 2 * n + b // 2, at:at + 64] = v[name][l, b]
    arrays = {
        "wstream": np.zeros((1,), np.float32),
        "x_in": np.ascontiguousarray(v["x"][0].T.reshape(DT, P, S).transpose(1, 0, 2)),
        "pos_in": v["positions"],
        "cols_in": cols,
        "layer_in": np.stack(layers),
        "const_in": const,
        "strip_in": strips,
        "bucket_in": table,
        "rel_in": v["rel_bias_2"],
        "lru_in": lru,
    }
    nc = _bacc.Bacc("TRN2", target_bir_lowering=False, num_devices=1)
    shapes = {name: a.shape for name, a in arrays.items()}
    shapes["wstream"] = (U_ALL, P, UB, P)
    args = [nc.dram_tensor(name, shapes[name], mybir.dt.from_np(a.dtype), kind="ExternalInput").ap() for name, a in arrays.items()]
    args.append(nc.dram_tensor("y_out", (P, DT, S), F32, kind="ExternalOutput").ap())
    arrays["wstream"] = stream_of(v, build(nc, *args))
    r = _run(nc, [arrays], core_ids=[0])
    y = r.results[0]["y_out"]
    return np.ascontiguousarray(y.transpose(1, 0, 2).reshape(D, S).T)[None]
```

```python
from contextlib import ExitStack
import math

import numpy as np

import concourse.bass as bass
from concourse import mybir
from concourse.alu_op_type import AluOpType as ALU

ACT = mybir.ActivationFunctionType
F32 = mybir.dt.float32
F32R = mybir.dt.float32r
I32 = mybir.dt.int32
P = 128
S = 512
D = 1024
DT = D // P
FF = 2816
FT = FF // P
HALF = FT // 2
UB = 16
LAYERS = 2
NEG = -1e30
TILE = S * 4

U_ADA, U_IN1, U_QB, U_KVB, U_O = 24, 10, 2, 1, 4
U_PAIR, U_DOWN, U_IN2 = 2, 12, 12
U_LAYER = 2 * (U_PAIR * HALF + U_DOWN) + U_IN2 + U_O
U_FIRST = U_IN1 + U_QB + U_KVB + U_O + U_PAIR * HALF + U_DOWN
U_PAD = U_FIRST % 2
U_SPLIT = U_FIRST + U_PAD + LAYERS * U_LAYER + 2
ADA_EARLY = 8
U_ALL = U_ADA - ADA_EARLY + U_SPLIT


def column_plan():
    at, n = {}, 0
    for name, w in (("c", 8), ("b_ada", 48), ("g_mix", 8), ("g_q_lat", 4), ("g_kv_lat", 2), ("g_q", 1),
                    ("g_k", 1), ("g_dq", 1), ("g_dk", 1), ("g_ffn", 8), ("w_conv0", 44), ("w_conv1", 44),
                    ("w_conv2", 44), ("b_conv", 44), ("final", 8), ("ffn1_0", 8), ("freq_dil", 1), ("freq_mla", 1)):
        at[name] = n
        n += w
    return at, n


def layer_plan():
    at, n = {}, 0
    for name, w in (("ffn1", 8), ("mix", 8), ("ffn2", 8), ("next", 8), ("subln", 1), ("sc_w", 6), ("lru_w", 8),
                    ("lru_b", 2), ("lambda", 2), ("ba", 2), ("bx", 2), ("lam", 4), ("lam_init", 1),
                    ("sub_scale", 1)):
        at[name] = n
        n += w
    return at, n


COL, NCOL = column_plan()
LCOL, NLCOL = layer_plan()
CONST = {name: n * P for n, name in enumerate(("ident", "ones", "blk64", "blkq", "perm64", "permq"))}


class Token:

    def __init__(self, sem, value, loops, lag=None, like=None):
        self.sem, self.value, self.loops, self.lag = sem, value, loops, lag
        self.counter, self.times = like or (sem, 1)

    def per(self, loop):
        return loop.per.get(self.counter, 0) * self.times


class Loop:
    def __init__(self, n):
        self.n, self.i, self.open = n, None, True
        self.per, self.marks, self.used, self.late = {}, {}, set(), ()


class Program:

    def __init__(self, nc, ctx):
        self.nc, self.ctx = nc, ctx
        self.eng = {"pe": nc.tensor, "act": nc.scalar, "dve": nc.vector, "pool": nc.gpsimd, "sp": nc.sync}
        self.sems, self.count, self.known = {}, {}, {}
        self.loops, self.scopes, self.dry = [], [{}], False

    def sem(self, name):
        if name not in self.sems:
            self.sems[name] = self.ctx.enter_context(self.nc.semaphore("s_" + name))
            self.count[name] = 0
        return self.sems[name]

    def value(self, t):
        v = t.value
        for L in t.loops:
            per = t.per(L)
            v = L.i * per + v if L.open and per else v + ((L.n - 1) * per if not L.open else 0)
            if t.lag is L:
                v = v - per
        return v

    def first_turn(self, t):
        v = t.value
        for L in t.loops:
            per = t.per(L)
            v += (L.n - 1) * per if not L.open else 0
            v -= per if t.lag is L else 0
        return v

    def resolve(self, name, engine):
        return self.resolve_at(name, len(self.scopes) - 1, engine)

    def resolve_at(self, name, top, engine):
        for depth in range(top, -1, -1):
            if name in self.scopes[depth]:
                return self.scopes[depth][name]
            if depth:
                L = self.loops[depth - 1]
                if self.dry:
                    L.used.add((engine, name))
                elif name in L.marks:
                    ahead = self.resolve_at(name, depth - 1, engine) if (engine, name) in L.late else []
                    return [Token(t.sem, t.value, t.loops, L) for t in L.marks[name]] + ahead
        return []

    def covered(self, L, name, engine):
        turn = {}
        for t in L.marks[name]:
            v = self.first_turn(Token(t.sem, t.value, t.loops, L))
            turn[t.sem] = max(v, turn.get(t.sem, v))
        return all(t.sem in turn and self.first_turn(t) <= turn[t.sem] for t in self.resolve(name, engine))

    def wait(self, engine, *waits, apart=True):
        if self.dry:
            for w in waits:
                if not isinstance(w, Token):
                    self.resolve(w, engine)
            return
        e, latest = self.eng[engine], {}
        self.sem("spare_" + engine)
        for w in waits:
            for t in ([w] if isinstance(w, Token) else self.resolve(w, engine)):
                v = self.value(t)
                key = (t.sem, not isinstance(v, int), tuple(id(L) for L in t.loops if L.open))
                first = self.value(t) if isinstance(v, int) else self.first_turn(t)
                if key not in latest or latest[key][0] < first:
                    latest[key] = (first, v)
        by_register, waited = False, set()
        for (sem, register, _), (first, v) in sorted(latest.items(), key=lambda kv: kv[0][1]):
            if register:
                if sem in waited:
                    e.sem_inc(self.sem("spare_" + engine), 1)
                waited.add(sem)
                assert first > 0, (engine, sem, first)
                by_register = True
            elif v <= self.known.get((engine, sem), 0):
                continue
            else:
                self.known[engine, sem] = v
            e.wait_ge(self.sem(sem), v)
        if by_register and apart:
            e.sem_inc(self.sem("spare_" + engine), 1)

    def run(self, engine, make, *waits, sem=None, by=1, mark=None, apart=False):
        name = sem or engine
        self.sem(name)
        self.wait(engine, *waits, apart=apart or engine == "pool")
        if not self.dry:
            make(self.eng[engine]).then_inc(self.sems[name], by)
        self.count[name] += by
        t = Token(name, self.count[name], tuple(self.loops))
        if mark:
            self.mark(mark, t)
        return t

    def mark(self, name, *tokens):
        self.scopes[-1][name] = list(tokens)

    def pe(self, make, *waits, **kw):
        return self.run("pe", make, *waits, **kw)

    def act(self, make, *waits, **kw):
        return self.run("act", make, *waits, **kw)

    def dve(self, make, *waits, **kw):
        return self.run("dve", make, *waits, **kw)

    def pool(self, make, *waits, **kw):
        return self.run("pool", make, *waits, **kw)

    def dma(self, engine, sem, out, in_, *waits, **kw):
        return self.run(engine, lambda e: e.dma_start(out() if callable(out) else out, in_() if callable(in_) else in_),
                        *waits, sem=sem, by=16, **kw)

    def loop(self, n, body, late=()):
        L, start, dry = Loop(n), dict(self.count), self.dry
        for real in ((False,) if dry else (False, True)):
            self.loops.append(L)
            self.scopes.append({})
            if not real:
                self.dry, L.i = True, 0
                body(0)
                self.dry = dry
                L.per = {k: v - start.get(k, 0) for k, v in self.count.items() if v != start.get(k, 0)}
                L.marks = dict(self.scopes[-1])
                for k in self.count:
                    self.count[k] = start.get(k, 0)
            else:
                self.loops.pop()
                scope = self.scopes.pop()
                L.i = 0
                left = sorted((e, n) for e, n in L.used if n in L.marks and not self.covered(L, n, e))
                L.late = tuple(u for u in late if u in left)
                for engine in sorted({e for e, _ in left}):
                    self.wait(engine, *(n for e, n in left if e == engine and (e, n) not in L.late))
                self.loops.append(L)
                self.scopes.append(scope)
                with self.nc.Fori(0, n) as i:
                    L.i = i
                    body(i)
            scope = self.scopes.pop()
            self.loops.pop()
            if not real and not dry:
                continue
        L.open = False
        for k, v in L.per.items():
            self.count[k] = start.get(k, 0) + n * v
        self.scopes[-1].update(scope)


def build(nc, wstream, ada_in, x_in, pos_in, cols_in, layer_in, const_in, strip_in, bucket_in, rel_in, lru_in, y_out):
    scratch = nc.dram_tensor("bias_by_distance", (8, 640), F32, kind="Internal").ap()
    strips_dram = nc.dram_tensor("bias_strips", (8, P, S), F32, kind="Internal").ap()
    with ExitStack() as ctx:
        k = Program(nc, ctx)
        for engine in ("pe", "act", "dve", "pool"):
            k.sem(engine)
        top = [-(-nc.sbuf_base // 64) * 64]

        def place(name, shape, dt=F32, at=None):
            if at is None:
                at = top[0]
                top[0] += -(-int(np.prod(shape[1:])) * 4 // 32) * 32
                assert top[0] <= nc.sbuf_usable_end, name
            return nc.alloc_sbuf_tensor_at(name, shape, dt, offset=at)

        raw = [place(f"raw{s}", [P, UB, P]) for s in range(2)]
        whi = [place(f"whi{s}", [P, UB, P], F32R) for s in range(2)]
        wlo = [place(f"wlo{s}", [P, UB, P], F32R) for s in range(2)]
        x = place("x", [P, DT, S])
        ahi = place("ahi", [P, DT, S], F32R)
        alo = place("alo", [P, DT, S], F32R)
        big = top[0]
        hhi = place("hhi", [P, FT, S], F32R)
        hlo = place("hlo", [P, FT, S], F32R)

        def region(name, tile, shape, dt=F32):
            return place(name, shape, dt, at=big + int(tile * TILE))

        const = place("const", [P, len(CONST) * P])
        cols = place("cols", [P, NCOL])
        lc = place("lc", [P, NLCOL])
        mod = place("mod", [P, 48])
        gcol = place("gcol", [P, 16])
        small = place("small", [P, 32])
        ada_row = place("ada_row", [1, 2, 2 * P])
        sq = [place(f"sq{s}", [P, S]) for s in range(2)]
        tmp = [place(f"tmp{s}", [P, S]) for s in range(4)]
        rstd = place("rstd", [P, S])
        ps = ctx.enter_context(nc.psum_tensor("ps", [P, 8, S], F32))

        def C(name, w=P):
            return const[:, CONST[name]:CONST[name] + w]

        def col(name, j=0):
            return cols[:, COL[name] + j:COL[name] + j + 1]

        def dyn(t, j, n=1):
            return t[:, j:j + n] if isinstance(j, int) else t[:, bass.ds(j, n)]

        def lcol(name, j=0):
            return lc[:, LCOL[name] + j:LCOL[name] + j + 1]

        EPS, SUB_EPS, HALF_PI = (small[:, n:n + 1] for n in range(3))
        ONE = small[0:1, 3:4]
        k.sem("start")
        k.run("pool", lambda e: e.memset(small[:, 0:1], 1e-6), sem="start")
        k.run("pool", lambda e: e.memset(small[:, 1:2], 1e-5))
        k.run("pool", lambda e: e.memset(small[:, 2:3], math.pi / 2))
        t_small = k.run("pool", lambda e: e.memset(small[:, 3:4], 1.0))
        for e in ("act", "dve", "pe", "sp", "pool"):
            k.wait(e, Token("start", 1, ()), t_small)
        early = region("early", 0, [P, ADA_EARLY, UB, P])
        pos_i = region("pos_i", 39, [1, S], I32)
        strip_causal = region("strip_causal", 40, [P, S])
        strip_dil = region("strip_dil", 41, [P, S])
        t_cols = k.dma("act", "d_cols", cols[:], cols_in)
        t_pos = k.dma("act", "d_pos", pos_i[:], pos_in)
        t_const = k.dma("act", "d_const", const[:], const_in)
        t_x = k.dma("act", "d_x", x[:], x_in)
        t_early = [k.dma("sp", f"d_ada{n}", early[:, n], ada_in[n]) for n in range(ADA_EARLY)]

        for s in range(2):
            nc.sync.dma_start(raw[s][:], wstream[s]).then_inc(k.sem(f"ld{s}"), 16)
            k.sem(f"free{s}")
        k.sem("hi"), k.sem("use")
        k.count["take"] = 0
        with nc.sync.Fori(0, (U_ALL - 2) // 2) as i:
            for s in range(2):
                nc.sync.wait_ge(k.sem(f"free{s}"), i + 1)
                nc.sync.dma_start(raw[s][:], wstream[bass.ds(i * 2 + (2 + s), 1)].rearrange("a p b m -> (a p) b m"))\
                    .then_inc(k.sem(f"ld{s}"), 16)

        ahead = [0, 0]
        ada_at = []

        def count(sem, value):
            return Token(sem, value, tuple(k.loops))

        def take():
            v = k.count["take"]
            k.count["take"] += 1
            s = v % 2
            return s, Token(f"ld{s}", 16 * (v // 2 + 1), tuple(k.loops), like=(f"free{s}", 16)), v

        lo_engine = ["dve"]

        def split():
            g = k.count["hi"]
            r, loaded, v = take()
            s = g % 2
            ahead[s] = v - g
            k.act(lambda e: e.activation(whi[s][:], raw[r][:], ACT.Copy), loaded,
                  *([count("use", g - 1)] if g >= 2 else []), sem="hi")
            k.run(lo_engine[0], lambda e: e.tensor_tensor(wlo[s][:], raw[r][:], whi[s][:].bitcast(F32), ALU.subtract),
                  count("hi", g + 1), sem=f"free{r}")

        def mm3(e, out, s, b, m, rhi, rlo, start, stop):
            wh, wl = whi[s][:, b, 0:m], wlo[s][:, b, 0:m]
            e.matmul(out, wh, rhi, start=start, stop=False)
            e.matmul(out, wl, rhi, start=False, stop=False)
            return e.matmul(out, wh, rlo, start=False, stop=stop)

        def product(blocks, first=(), inputs=None, last_part=True, then=None):
            u = k.count["use"]
            s = u % 2
            v = u + ahead[s]
            if k.dry and inputs:
                k.wait("pe", *(inputs.values() if isinstance(inputs, dict) else inputs))

            def make(e):
                ins, seen = None, {blocks[0][-1]}
                for b, out, m, rhi, rlo, start, stop, n in blocks:
                    if inputs and n not in seen:
                        seen.add(n)
                        k.wait("pe", inputs[n])
                    ins = mm3(e, out, s, b, m, rhi, rlo, start, stop)
                return ins
            if inputs:
                first = [*first, inputs[blocks[0][-1]]]
            if last_part:
                k.pe(make, count(f"free{v % 2}", v // 2 + 1), *first, sem="use")
                if then:
                    then(count("use", u + 1))
                split()
                return count("use", u + 1)
            return k.pe(make, count(f"free{v % 2}", v // 2 + 1), *first)

        def bank(b, m=P, n=S, lo=0):
            return ps[lo:lo + m, b, 0:n]

        def hilo(dst_hi, dst_lo, src, *waits, shift=None, mark=None):
            if shift is None:
                t1 = k.act(lambda e: e.activation(dst_hi(), src, ACT.Copy), *waits)
                t2 = k.dve(lambda e: e.tensor_tensor(dst_lo(), src, dst_hi().bitcast(F32), ALU.subtract), t1)
            else:
                t1 = k.act(lambda e: e.activation(dst_hi(), src, ACT.Identity, bias=shift), *waits)
                t2 = k.dve(lambda e: e.scalar_tensor_tensor(dst_lo(), src, shift, dst_hi().bitcast(F32),
                                                            ALU.add, ALU.subtract), t1)
            if mark:
                k.mark(mark, t1, t2)
            return t2

        def unit_of(banks, tokens=None, parts=None, then=None, order=range(DT)):
            parts = parts or (lambda kt: (ahi[:, kt, :], alo[:, kt, :]))
            return product([(kt * 2 + m, bank(banks[m]), P, *parts(kt), kt == order[0], kt == order[-1], kt)
                            for kt in order for m in range(2)], [f"bank{b}" for b in banks], tokens, then=then)

        def quarter_of(n, bank_of):
            m, kts = n // 2, range(4 * (n % 2), 4 * (n % 2) + 4)
            return product([(kt * 2 + m, bank(bank_of[m]), P, ahi[:, kt, :], alo[:, kt, :], kt == 0, kt == DT - 1, kt)
                            for kt in kts], [f"bank{bank_of[m]}"], last_part=n == 3)

        def wide(tokens, n_units, evac, after_first=None, parts=None, urgent=False, order=range(DT)):
            def chunk(c, j, tokens=None):
                banks = (2 * (c % 2), 2 * (c % 2) + 1)
                if urgent:
                    unit_of(banks, tokens, parts, lambda t: evac(j, banks, t), order)
                    if tokens and after_first:
                        after_first()
                else:
                    t = unit_of(banks, tokens, parts, then=after_first if tokens else None)
                    evac(j, banks, t)
                k.mark(f"a{c}", last("dve"))
            for c in range(2):
                chunk(c, 2 * c, None if c else tokens)
            if n_units == 4:
                for c in range(2):
                    chunk(c, 4 + 2 * c)
            elif n_units >= 6:
                k.loop(n_units // 2 - 1, lambda i: [chunk(c, i * 4 + (4 + 2 * c)) for c in range(2)])
            if n_units % 2:
                chunk(0, 2 * n_units - 2)

        def into_scaled(dst):
            def evac(j, banks, t):
                for m in range(2):
                    k.dve(lambda e: e.tensor_tensor(one(dst, j + m), bank(banks[m]), rstd[:], ALU.mult), t, "rstd",
                          mark=f"bank{banks[m]}")
            return evac

        def one(dst, j, rows=P, lo=0):
            if isinstance(j, int):
                return dst[lo:lo + rows, j, :]
            return dst[lo:lo + rows, bass.ds(j, 1), :].rearrange("p a n -> p (a n)")

        def clear_sum():
            k.dve(lambda e: e.memset(rstd[:], 0.0), "rstd", last("dve"), mark="sum")

        def residual(scale, gain=None):
            def evac(j, banks, t):
                tx = [k.dve(lambda e: e.scalar_tensor_tensor(one(x, j + m), bank(banks[m]), scale(j + m), one(x, j + m),
                                                             ALU.mult, ALU.add), t, mark=f"bank{banks[m]}") for m in range(2)]
                if gain:
                    split_input(j, gain, tx)
                for m in range(2):
                    tq = k.act(lambda e: e.activation(sq[m][:], one(x, j + m), ACT.Square), tx[m], f"sq{m}", apart=True)
                    ts = k.dve(lambda e: e.tensor_tensor(rstd[:], rstd[:], sq[m][:], ALU.add), tq, "sum", mark="sum")
                    k.mark(f"sq{m}", ts)
            return evac

        def split_input(j, gain, tx):
            t = [k.act(lambda e: e.activation(one(ahi, j + m), one(x, j + m), ACT.Copy, scale=gain(j + m)), tx[m], "ahi_read",
                       apart=True) for m in range(2)]
            for m in range(2):
                k.dve(lambda e: e.scalar_tensor_tensor(one(alo, j + m), one(x, j + m), gain(j + m),
                                                       one(ahi, j + m).bitcast(F32), ALU.mult, ALU.subtract), t[m])

        def root(*_):
            t = k.pe(lambda e: e.matmul(bank(5), C("ones"), rstd[:], start=True, stop=True), "sum", "bank5")
            t = k.act(lambda e: e.activation(rstd[:], bank(5), ACT.Sqrt, bias=EPS, scale=1.0 / D), t, mark="bank5")
            k.dve(lambda e: e.reciprocal(rstd[:], rstd[:]), t, mark="rstd")

        def modulated(g, sh, *waits):
            tokens, scaled = {}, {}
            for j in range(DT + 1):
                if j < DT:
                    scaled[j] = k.dve(lambda e: e.scalar_tensor_tensor(tmp[j % 2][:], x[:, j, :], gcol[:, g + j:g + j + 1],
                                                                       rstd[:], ALU.mult, ALU.mult),
                                      "rstd", f"tmp{j % 2}", *waits)
                if j > 0:
                    n = j - 1
                    tokens[n] = hilo(lambda: ahi[:, n, :], lambda: alo[:, n, :], tmp[n % 2][:], scaled[n],
                                     shift=mod[:, sh + n:sh + n + 1], mark=f"tmp{n % 2}")
            return tokens

        def down(scale, gain):
            clear_sum()

            def body(i):
                for c in range(2):
                    banks = (2 * c, 2 * c + 1)
                    for part in range(3):
                        n = min(8, FT - 8 * part)
                        product([(kt * 2 + m, bank(banks[m]), P, hhi[:, 8 * part + kt, :], hlo[:, 8 * part + kt, :],
                                  part + kt == 0, 8 * part + kt == FT - 1, 0)
                                 for kt in range(n) for m in range(2)],
                                [f"bank{b}" for b in banks] + (["hidden"] if part == 2 else []),
                                then=(lambda t: residual(scale, gain)(i * 4 + 2 * c, banks, t)) if part == 2 else None)
                    k.mark(f"a{c}", last("dve"))
            k.loop(2, body, late=(("pe", "bank2"), ("pe", "bank3")))

        def down_inputs():
            return ["a0"] * 6 + ["a1"] * 2

        def last(engine):
            return Token(engine, k.count[engine], tuple(k.loops))

        def used():
            return count("use", k.count["use"])

        def plain_pair(i, tokens=None, after_first=None):
            tg = unit_of((0, 1), tokens, then=after_first)
            ts = []
            for m in range(2):
                t = k.dve(lambda e: e.tensor_tensor(tmp[m][:], bank(m), rstd[:], ALU.mult), tg, f"tmp{m}", "rstd", mark=f"bank{m}")
                ts.append(k.act(lambda e: e.activation(tmp[m][:], tmp[m][:], ACT.Silu), t))
                ts[m] = k.pool(lambda e: e.tensor_tensor(tmp[m][:], tmp[m][:], rstd[:], ALU.mult), ts[m])
            tv = unit_of((2, 3))
            for m in range(2):
                t = k.dve(lambda e: e.tensor_tensor(tmp[m][:], tmp[m][:], bank(2 + m), ALU.mult), tv, ts[m],
                          mark=f"bank{2 + m}")
                hilo(lambda: one(hhi, i * 2 + m), lambda: one(hlo, i * 2 + m), tmp[m][:], t, mark=f"tmp{m}")

        def conv_pair(i, tokens=None, after_first=None):
            def conv(b, dst, off, t, name):
                j = i * 2 + off
                t = k.act(lambda e: e.activation(dst[:], bank(b), ACT.Identity, bias=dyn(cols, j + COL["b_conv"]),
                                                 scale=dyn(cols, j + COL["w_conv2"])), t, name)
                for d, w in ((1, "w_conv1"), (2, "w_conv0")):
                    t = k.dve(lambda e: e.scalar_tensor_tensor(dst[:, d:], bank(b, n=S - d), dyn(cols, j + COL[w]), dst[:, d:],
                                                               ALU.mult, ALU.add), t)
                k.mark(f"bank{b}", t)
                return t
            tg = unit_of((0, 1), tokens)
            ts = []
            for m in range(2):
                t = conv(m, tmp[m], m, tg, f"tmp{m}")
                ts.append(k.act(lambda e: e.activation(tmp[m][:], tmp[m][:], ACT.Silu), t))
            tv = unit_of((2, 3))
            for m in range(2):
                t = conv(2 + m, tmp[2 + m], FT + m, tv, f"tmp{2 + m}")
                t = k.dve(lambda e: e.tensor_tensor(tmp[m][:], tmp[m][:], tmp[2 + m][:], ALU.mult), t, ts[m],
                          mark=f"tmp{2 + m}")
                hilo(lambda: one(hhi, i * 2 + m), lambda: one(hlo, i * 2 + m), tmp[m][:], t, mark=f"tmp{m}")

        def feed_forward(pair_of, tokens, scale, gain, after_first=None, then=None):
            pair_of(0, tokens, after_first)
            free = then() if then else ()

            def body(i):
                pair_of(i + 1)
                for e in ("act", "dve"):
                    k.wait(e, *free)
            k.loop(HALF - 1, body)
            k.mark("hidden", last("act"), last("dve"))
            k.mark("ahi_read", used())
            for e in ("act", "dve"):
                k.wait(e, "lc")
            down(scale, gain)

        def head_norm(tile, rows, ones_name, gain, t_in, s, table):
            r, y = (w[0:rows, :] for w in slots[s])
            t = k.act(lambda e: e.activation(r, tile, ACT.Square), f"sq{s}", t_in)
            yield
            t = k.pe(lambda e: e.matmul(bank(s, rows), C(ones_name)[0:rows, 0:rows], r, start=True, stop=True), t, f"bank{s}")
            yield
            t = k.act(lambda e: e.activation(r, bank(s, rows), ACT.Sqrt, bias=EPS[0:rows]), t)
            yield
            t = k.dve(lambda e: e.reciprocal(r, r), t)
            t = k.dve(lambda e: e.scalar_tensor_tensor(tile if table is None else y, tile, gain, r, ALU.mult, ALU.mult), t)
            if table is not None:
                cos, sin, perm = table
                yield
                t = k.pe(lambda e: e.matmul(bank(s, rows), C(perm)[0:rows, 0:rows], y, start=True, stop=True), t)
                yield
                t2 = k.dve(lambda e: e.tensor_tensor(r, bank(s, rows), sin[0:rows, :], ALU.mult), t)
                t1 = k.pool(lambda e: e.tensor_tensor(y, y, cos[0:rows, :], ALU.mult), t)
                yield
                t = k.pool(lambda e: e.tensor_tensor(tile, y, r, ALU.add), t1, t2)
            for name in (f"sq{s}", f"bank{s}"):
                k.mark(name, t)
            yield

        QAT = {3: (0, 0, 0), 2: (1, 0, 512), 0: (1, 384, 896), 1: (2, 0, 1024)}
        KAT = {0: (0, 0, 0), 1: (1, 0, 512), 3: (1, 384, 896), 2: (2, 0, 1024)}
        PACKED = 1280

        def scores_steps(q, key, d, lo, strip, scale, E, stat, slot, ready, t_strip=()):
            done = {}
            for i in (3, 2, 0, 1):
                b, off, _ = QAT[i]
                done[i] = k.pe(lambda e: e.matmul(ps[:, b, off:off + P * (i + 1)], q[lo:lo + d, P * i:P * (i + 1)],
                                                  key[lo:lo + d, 0:P * (i + 1)], start=True, stop=True),
                               *ready, f"bank{b}")
            done[2] = done[0]
            for i in (3, 2, 0, 1):
                b, off, at = QAT[i]
                tm = k.dve(lambda e: e.tensor_tensor_reduce(
                    out=E[:, at:at + P * (i + 1)], in0=ps[:, b, off:off + P * (i + 1)],
                    in1=strip[:, S - P * (i + 1):S], scale=scale, scalar=-3e38, op0=ALU.add, op1=ALU.max,
                    accum_out=stat[:, i:i + 1]), done[i], f"E{slot}", *t_strip, mark=f"bank{b}", apart=True)
            t = k.dve(lambda e: e.tensor_scalar(stat[:, 4:8], stat[:, 0:4], -1.0, None, ALU.mult), tm)
            yield
            for i in (3, 2, 0, 1):
                at = QAT[i][2]
                te = k.act(lambda e: e.activation(E[:, at:at + P * (i + 1)], E[:, at:at + P * (i + 1)], ACT.Exp,
                                                  bias=stat[:, 4 + i:5 + i], accum_out=stat[:, 8 + i:9 + i]), t)
            yield k.dve(lambda e: e.reciprocal(stat[:, 12:16], stat[:, 8:12]), te)

        def mix_values(E, t_e, PT, vtok, dv, lo, t_v):
            tp = []
            for b, w, at in ((0, 512, 0), (1, 512, 512), (2, 256, 1024)):
                tb = (3, 4, 3)[b]

                def make(e):
                    for j in range(4):
                        if KAT[j][0] == b:
                            for i in range(j, 4):
                                src = QAT[i][2] + P * j
                                to = KAT[j][1] + P * (i - j)
                                ins = e.transpose(ps[:, tb, to:to + P], E[:, src:src + P], C("ident"))
                    return ins
                tt = k.pe(make, *t_e, f"bank{tb}")
                tp.append(k.act(lambda e: e.activation(PT[:, at:at + w], ps[:, tb, 0:w], ACT.Copy), tt, "PT",
                                mark=f"bank{tb}"))
            yield tt

            def make(e):
                for j in range(4):
                    at = KAT[j][2]
                    ins = e.matmul(ps[lo:lo + dv, 5, P * j:S], vtok[:, j, :], PT[:, at:at + S - P * j],
                                   start=(j == 0), stop=(j == 3))
                return ins
            t = k.pe(make, tp[-1], *t_v, "bank5")
            k.mark("PT", t)
            yield t

        def weave(*plans):
            turn, live = 0, list(plans)
            while live:
                for plan in list(live):
                    if plan[0] <= turn and next(plan[1], "end") == "end":
                        live.remove(plan)
                turn += 1

        z1 = region("z1", 0, [P, 19, S])
        qt = region("qt", 19, [P, 8, S])
        kvt = region("kvt", 27, [P, 8, S])
        tables = [region(f"table{n}", 35 + n, [P, S]) for n in range(4)]
        t_strip = k.dma("act", "d_strip", strip_causal[:], strip_in[0])
        t_strip2 = k.dma("act", "d_strip2", strip_dil[:], strip_in[1])
        t_c = k.act(lambda e: e.activation(small[:, 8:16], cols[:, COL["c"]:COL["c"] + 8], ACT.Silu), t_cols)

        def ada_steps(j, rows, turned, from_stream=True):
            for m in range(2):
                if from_stream:
                    r, loaded, v = take()
                    w = raw[r]
                    if not k.dry:
                        L = k.loops[-1]
                        ada_at.extend(v + n * L.per["take"] for n in range(L.n))
                else:
                    w, loaded = early[:, 2 * j + m], t_early[2 * j + m]

                def make(e):
                    for kt in range(DT):
                        ins = e.matmul(ps[0:1, rows[m], 0:2 * P], small[:, 8 + kt:9 + kt], w[:, 2 * kt:2 * kt + 2, :],
                                       start=(kt == 0), stop=(kt == DT - 1))
                    return ins
                t = k.pe(make, loaded, t_c, f"bank{rows[m]}", sem=f"free{r}" if from_stream else None)
                k.dve(lambda e: e.tensor_copy(ada_row[:, m, :], ps[0:1, rows[m], 0:2 * P]), t, "ada_row", mark=f"bank{rows[m]}")
                yield

            def make(e):
                for n in range(4):
                    ins = e.matmul(ps[:, turned, n:n + 1], ada_row[0:1, n // 2, P * (n % 2):P * (n % 2) + P], ONE,
                                   start=True, stop=True)
                return ins
            t = k.pe(make, last("dve"), f"bank{turned}", mark="ada_row")
            k.dve(lambda e: e.tensor_tensor(dyn(mod, j * 4, 4), ps[:, turned, 0:4], dyn(cols, j * 4 + COL["b_ada"], 4), ALU.add),
                  t, mark=f"bank{turned}")
            yield

        angles = [region("angle_dil", 42, [P, S]), region("angle_mla", 43, [P, S])]
        for j in range(ADA_EARLY // 2):
            for _ in ada_steps(j, (0, 1) if j % 2 == 0 else (3, 4), 2, from_stream=False):
                pass
            if j == 1:
                clear_sum()
                for n in range(DT):
                    t = k.act(lambda e: e.activation(sq[n % 2][:], x[:, n, :], ACT.Square), t_x, f"sq{n % 2}")
                    t = k.dve(lambda e: e.tensor_tensor(rstd[:], rstd[:], sq[n % 2][:], ALU.add), t, "sum", mark="sum")
                    k.mark(f"sq{n % 2}", t)
            if j == 2:
                root()
                t = k.dve(lambda e: e.tensor_copy(tmp[2][0:1, :], pos_i[:]), t_pos)
                t_p = k.pe(lambda e: e.matmul(bank(6), C("ones")[0:1, :], tmp[2][0:1, :], start=True, stop=True), t, t_const)
                for f, a in zip(("freq_dil", "freq_mla"), angles):
                    t_angle = k.dve(lambda e: e.tensor_scalar(a[:], bank(6), col(f), None, ALU.mult), t_p, t_cols, mark="bank6")

        def scaled_gain(n, g, c):
            t = k.dve(lambda e: e.tensor_scalar(gcol[:, 8 * n:8 * n + 8], mod[:, c:c + 8], 1.0, None, ALU.add), last("dve"))
            return k.dve(lambda e: e.tensor_tensor(gcol[:, 8 * n:8 * n + 8], gcol[:, 8 * n:8 * n + 8],
                                                   cols[:, COL[g]:COL[g] + 8], ALU.mult), t)
        t_g = scaled_gain(0, "g_mix", 8)
        for _ in range(2):
            split()

        tokens = modulated(0, 0, t_g)
        for e in ("act", "dve"):
            k.wait(e, last("pe"))

        q_parts = [(hlo[:, 5 + j, :], hlo[:, 9 + j, :]) for j in range(4)]
        kv_parts = [(hhi[:, j, :], hhi[:, 2 + j, :]) for j in range(2)]
        rms_q, rms_kv = region("rms_q", 39, [P, S]), region("rms_kv", 42, [P, S])

        def latent(j, b, t, parts, gain, out, stat_bank):
            n = len(parts)
            hi, lo = parts[j]
            th = k.act(lambda e: e.activation(hi, bank(b), ACT.Copy, scale=col(gain, j)), t)
            tq = k.act(lambda e: e.activation(sq[j % 2][:], bank(b), ACT.Square), f"sq{j % 2}")
            tl = k.dve(lambda e: e.scalar_tensor_tensor(lo, bank(b), col(gain, j), hi.bitcast(F32), ALU.mult, ALU.subtract), th, tq)
            k.mark(f"bank{b}", tq, tl)

            def add_up():
                t = k.pe(lambda e: e.matmul(bank(stat_bank), C("ones"), sq[j % 2][:], start=(j == 0), stop=(j == n - 1)),
                         tq, mark=f"sq{j % 2}")
                if j == n - 1:
                    t = k.act(lambda e: e.activation(out[:], bank(stat_bank), ACT.Sqrt, bias=EPS, scale=1.0 / (n * P)), t)
                    k.mark(f"bank{stat_bank}", k.dve(lambda e: e.reciprocal(out[:], out[:]), t))
            return add_up, tl

        t = unit_of((4, 5), tokens)
        a_lat = [latent(j, 4 + j, t, q_parts, "g_q_lat", rms_q, 3) for j in range(2)]
        t_second = unit_of((6, 7))

        TWO_PI = 2 * math.pi
        C1 = 6.28125
        C2 = float(np.round((TWO_PI - C1) * 2 ** 22) / 2 ** 22)
        C3 = TWO_PI - C1 - C2
        MAGIC = 1.5 * 2 ** 23
        m, turns = tmp[3][:], tmp[2][:]
        for n, angle in enumerate(angles):
            a, (cos, sin) = angle[:], tables[2 * n:2 * n + 2]
            td = k.dve(lambda e: e.tensor_scalar(m, a, 1.0 / TWO_PI, MAGIC, ALU.mult, ALU.add), t_angle)
            td = k.dve(lambda e: e.tensor_scalar(m, m, -MAGIC, None, ALU.add), td)
            for c in (C1, C2, C3):
                td = k.dve(lambda e: e.scalar_tensor_tensor(a, m, -c, a, ALU.mult, ALU.add), td)
            td = k.dve(lambda e: e.tensor_scalar(a, a, 3.1415925, -3.1415925, ALU.min, ALU.max), td)
            k.act(lambda e: e.activation(sin[:], a, ACT.Sin), td)
            ta = k.act(lambda e: e.activation(turns, a, ACT.Abs), td, "angle")
            t_tab = k.act(lambda e: e.activation(cos[:], turns, ACT.Sin, bias=HALF_PI, scale=-1.0), ta, mark="angle")
        for add_up, _ in a_lat:
            add_up()
        a_lat = [latent(2 + j, 6 + j, t_second, q_parts, "g_q_lat", rms_q, 3) for j in range(2)]
        t = unit_of((4, 5))
        for add_up, _ in a_lat:
            add_up()
        t_q_lat = a_lat[1][1]
        kv_lat = [latent(j, 4 + j, t, kv_parts, "g_kv_lat", rms_kv, 2) for j in range(2)]

        done = {}

        def tiles(jobs, evac, first=()):
            for n, (tile, rows, blocks) in enumerate(jobs):
                b = 4 + tile % 4
                for c in range(0, len(blocks), 4):
                    t = product([(blk, bank(b, rows), rows, hi, lo, c + q == 0, c + q == len(blocks) - 1, 0)
                                 for q, (blk, hi, lo) in enumerate(blocks[c:c + 4])],
                                [f"bank{b}", *first], last_part=n == len(jobs) - 1 and c + 4 >= len(blocks))
                    if c + 4 < len(blocks):
                        yield
                evac(tile, b, t)
                yield

        def products():
            for u in range(U_QB):
                heads = tiles([(4 * u + h, 96, [(kt * 4 + h, *q_parts[kt]) for kt in range(4)]) for h in range(4)],
                              q_out, (t_q_lat,))
                if u == 0:
                    next(heads)
                    yield
                    for add_up, _ in kv_lat:
                        add_up()
                yield from heads
            yield from tiles([(h, P, [(kt * 8 + h, *kv_parts[kt]) for kt in range(2)]) for h in range(8)],
                             kv_out, (kv_lat[1][1],))
            inputs = [(ahi[:, kt, :], alo[:, kt, :]) for kt in range(DT)]
            for first in (6, 8, 10, 12, 18, 14, 16):
                if first == 18:
                    yield from tiles([(18, 96, [(kt * 2, *inputs[kt]) for kt in range(DT)])], z_out)
                else:
                    yield from tiles([(first + m, P, [(kt * 2 + m, *inputs[kt]) for kt in range(DT)]) for m in range(2)], z_out)

        def q_out(h, b, t):
            done["q", h] = k.dve(lambda e: e.tensor_tensor(qt[0:96, h, :], bank(b, 96), rms_q[0:96, :], ALU.mult), t,
                                 mark=f"bank{b}")

        def kv_out(h, b, t):
            done["kv", h] = k.dve(lambda e: e.tensor_tensor(kvt[:, h, :], bank(b), rms_kv[:], ALU.mult), t, mark=f"bank{b}")

        def z_out(j, b, t):
            rows = 96 if j == 18 else P
            done["z", j] = k.act(lambda e: e.activation(z1[0:rows, j, :], bank(b, rows), ACT.Copy), t, mark=f"bank{b}")

        rot_q = (tables[2], tables[3], "permq")
        rot_d = (tables[0], tables[1], "perm64")
        slots = [(sq[0], tmp[0]), (sq[1], tmp[1]), (rstd, tmp[2]), (region("slot3", 43, [P, S]), tmp[3])]
        jobs = [(("q", h), qt[0:96, h, :], 96, "blkq", "g_q", rot_q) for h in range(8)]
        jobs += [(("kv", h), kvt[0:64, h, :], 64, "blk64", "g_k", None) for h in range(8)]
        for j in range(4):
            jobs += [(("z", 6 + j), z1[:, 6 + j, :], P, "blk64", "g_dq", rot_d)]
        for j in range(4):
            jobs += [(("z", 10 + j), z1[:, 10 + j, :], P, "blk64", "g_dk", rot_d)]
        jobs += [(("z", 18), z1[0:96, 18, :], 96, "blkq", "g_k", rot_q)]

        def head_norms(s):
            for key, tile, rows, ones_name, gain, table in jobs[s::4]:
                while key not in done:
                    yield
                yield from head_norm(tile, rows, ones_name, col(gain)[0:rows], done[key], s, table)
        k.mark("sq2", *tokens.values())
        for e in ("pool", "act", "dve"):
            k.wait(e, t_tab)
        lo_engine[0] = "pool"
        weave((0, products()), *((1 + s, head_norms(s)) for s in range(4)))
        lo_engine[0] = "dve"
        t_prep = (last("dve"), last("act"), last("pe"), last("pool"))

        E = [region(f"E{s}", 2.5 * s, [P, PACKED]) for s in range(2)]
        PT = region("PT", 35, [P, PACKED])
        vtok = region("vtok", 5, [P, 4, P])
        qs = [region("qs0", 37.5, [P, S]), region("qs1", 38.5, [P, S])]
        ks = [region("ks0", 42, [P, S]), region("ks1", 43, [P, S])]
        stat = [place(f"stat{s}", [P, 16]) for s in range(2)]

        for e in ("act", "dve", "pool", "pe"):
            k.wait(e, *t_prep)
        for s in range(2):
            t_kpe = k.dve(lambda e: e.tensor_copy(ks[s][64:96, :], z1[64:96, 18, :]))

        def attend_heads(heads, strip, scale, i, dst, j_ada):
            def attend(s, q, key, d, lo, t_qk, V, olo):
                for t in scores_steps(q, key, d, lo, strip, scale, E[s], stat[s], s, t_qk, (t_strip, t_strip2)):
                    if t is None:
                        k.mark(f"QK{s}", last("pe"))
                        yield
                for b in (3, 2, 0, 1):
                    at = QAT[b][2]
                    t2 = k.dve(lambda e: e.tensor_scalar(E[s][:, at:at + P * (b + 1)], E[s][:, at:at + P * (b + 1)],
                                                         stat[s][:, 12 + b:13 + b], None, ALU.mult), t)
                t_v, v = V(s)
                yield
                two = mix_values(E[s], (t2,), PT, v, 64, olo, (t_v,))
                k.mark(f"E{s}", next(two))
                yield
                t_o = next(two)
                k.mark("vtok", t_o)
                o = ps[olo:olo + 64, 5, :]
                hilo(lambda: one(ahi, dst(i), 64, olo), lambda: one(alo, dst(i), 64, olo), o, t_o, mark="bank5")
            weave(*((s, attend(s, *head)) for s, head in enumerate(heads)), (1, ada_steps(i + j_ada, (6, 7), 6)))

        def mla(i):
            heads = []
            for s in range(2):
                t1 = k.pool(lambda e: e.tensor_copy(qs[s][0:96, :], one(qt, i * 2 + s, 96)), f"QK{s}")
                t2 = k.pool(lambda e: e.tensor_copy(ks[s][0:64, :], one(kvt, i * 2 + s, 64)))
                t3 = k.pool(lambda e: e.tensor_copy(sq[s][:], one(kvt, i * 2 + s)), f"V{s}")

                def values(s, t3=t3):
                    def make(e):
                        for j in range(4):
                            ins = e.transpose(ps[:, 4, P * j:P * (j + 1)], sq[s][:, P * j:P * (j + 1)], C("ident"))
                        return ins
                    t = k.pe(make, t3, "bank4", mark=f"V{s}")
                    t = k.act(lambda e: e.activation(vtok[:, :, 64 * s:64 * s + 64],
                                                     ps[:, 4, :].rearrange("p (j d) -> p j d", j=4)[:, :, 64:128], ACT.Copy),
                              t, "vtok", mark="bank4")
                    return t, vtok[:, :, 64 * s:64 * s + 64]
                heads.append((qs[s], ks[s], 96, 0, (t2, t_kpe), values, 64 * s))
            attend_heads(heads, strip_causal, (96.0) ** -0.5, i, lambda i: i, ADA_EARLY // 2)
        k.loop(4, mla)

        def dil(i):
            t1 = k.pool(lambda e: e.tensor_copy(qs[0][:], one(z1, i + 6)), "QK0", "QK1")
            t2 = k.pool(lambda e: e.tensor_copy(ks[0][:], one(z1, i + 10)))
            t3 = k.pool(lambda e: e.tensor_copy(sq[0][:], one(z1, i + 14)), "V0")

            def values(s):
                if s == 0:
                    def make(e):
                        for j in range(4):
                            ins = e.transpose(ps[:, 4, P * j:P * (j + 1)], sq[0][:, P * j:P * (j + 1)], C("ident"))
                        return ins
                    t = k.pe(make, t3, "bank4", mark="V0")
                    values.t = k.act(lambda e: e.activation(vtok[:], ps[:, 4, :].rearrange("p (j d) -> p j d", j=4), ACT.Copy),
                                     t, "vtok", mark="bank4")
                return values.t, vtok[:, :, 64 * s:64 * s + 64]
            heads = [(qs[0], ks[0], 64, 64 * s, (t2,), values, 64 * s) for s in range(2)]
            attend_heads(heads, strip_dil, 64.0 ** -0.5, i, lambda i: i + 4, ADA_EARLY // 2 + 4)
        k.loop(4, dil)
        tok_mix = [last("dve")] * DT
        t_g = scaled_gain(1, "g_ffn", 32)
        for e in ("pe", "act", "dve"):
            k.wait(e, last("dve"), last("act"), last("pe"))

        rel = region("rel", 6, [32, 8])
        onehot = region("onehot", 7, [P, 2 * 640])
        dist = region("dist", 10, [8, 640])
        hankel = region("hankel", 12, [P, 8, S])
        flip = region("flip", 20, [P, P])
        flipped = region("flipped", 34, [P, 8, S])
        t_rel = k.dma("act", "d_rel", rel[:], rel_in)
        t_hot = k.dma("act", "d_hot", onehot[:], bucket_in[:, 0:1280])
        t_flip = k.dma("act", "d_flip", flip[:], bucket_in[:, 1280:1280 + P])
        t_strips, t_flipped = [], []

        def by_distance():
            def make(e):
                e.matmul(ps[0:8, 4, :], rel[:], onehot[0:32, 0:512], start=True, stop=True)
                return e.matmul(ps[0:8, 5, 0:128], rel[:], onehot[0:32, 512:640], start=True, stop=True)
            t = k.pe(make, t_rel, t_hot, "bank4", "bank5")
            k.dve(lambda e: e.scalar_tensor_tensor(dist[:, 0:512], ps[0:8, 4, :], 8.0, onehot[0:8, 640:1152], ALU.mult, ALU.add),
                  t, t_hot)
            t = k.dve(lambda e: e.scalar_tensor_tensor(dist[:, 512:640], ps[0:8, 5, 0:128], 8.0, onehot[0:8, 1152:1280],
                                                       ALU.mult, ALU.add))
            k.mark("bank4", t)
            k.mark("bank5", t)
            t = k.dma("pool", "d_scratch", scratch, dist[:], t)
            t_strips.append(k.dma("pool", "d_hankel", hankel[:],
                                  bass.AP(tensor=scratch.tensor, offset=0, ap=[[1, P], [640, 8], [1, S]]), t))

        def flips(heads):
            for h in heads:
                b = 4 + h % 4
                t = k.pe(lambda e: e.matmul(bank(b), flip[:], hankel[:, h, :], start=True, stop=True), t_strips[0], t_flip,
                         f"bank{b}")
                t_flipped.append(k.dve(lambda e: e.tensor_copy(flipped[:, h, :], bank(b)), t, mark=f"bank{b}"))

        def strips_out():
            flips(range(4, 8))
            t_strips[:] = [k.dma("pool", "d_strips", strips_dram.rearrange("h p n -> p h n"), flipped[:], t_flipped[-1])]
            return t_strips

        clear_sum()
        wide(tok_mix, U_O, residual(lambda j: dyn(mod, j + 16)), by_distance, urgent=True)
        t_x, t_used = last("dve"), used()
        flips(range(4))
        root()
        tokens = modulated(8, 24, t_x, t_used)
        feed_forward(conv_pair, tokens, lambda j: dyn(mod, j + 40), lambda j: dyn(cols, j + COL["ffn1_0"]),
                     then=strips_out)
        k.wait("pool", *t_strips)

        def skip():
            product([(0, bank(6), P, ahi[:, 0, :], alo[:, 0, :], True, True, 0)], ["bank6"])
            k.mark("bank6", used())
        for _ in range(U_PAD):
            skip()

        z2 = region("z2", 0, [P, FT, S])
        EE = [[region(f"EE{h}{m}", 22 + 5 * h + 2.5 * m, [P, PACKED]) for m in range(2)] for h in range(2)]
        PT2 = region("PTT", 32, [P, PACKED])
        vtok2 = region("vtok2", 34.5, [P, 4, P])
        strip2 = [[region(f"strip{h}{m}", 35.5 + 2 * h + m, [P, S]) for m in range(2)] for h in range(2)]
        W = [region(f"W{n}", 39.5 + n, [P, S]) for n in range(4)] + [tmp[3]]
        stat4 = [stat, [place(f"stat{s}", [P, 16]) for s in range(2, 4)]]
        bd = place("bd", [P, 4, P])

        def head(h):
            slot = h % 2
            E0, E1 = EE[slot]
            st = []
            for m in range(2):
                t_s = k.dma("pool", f"d_st{slot}{m}", strip2[slot][m][:], strips_dram[2 * h + m], f"strip{slot}{m}")
                E, stat = EE[slot][m], stat4[slot][m]
                t_r = None
                for part in scores_steps(z2[:, h, :], z2[:, 4 + h, :], 64, 64 * m, strip2[slot][m], 0.125, E, stat,
                                         f"{slot}{m}", (), (t_s,)):
                    t_r = part
                    yield
                k.mark(f"strip{slot}{m}", t_r)
                st.append(t_r)
                if m == 0:
                    def make(e):
                        for j in range(4):
                            ins = e.transpose(ps[:, 4, P * j:P * (j + 1)], z2[:, 8 + h, P * j:P * (j + 1)], C("ident"))
                        return ins
                    t = k.pe(make, "bank4")
                    t_v = k.act(lambda e: e.activation(vtok2[:], ps[:, 4, :].rearrange("p (j d) -> p j d", j=4), ACT.Copy),
                                t, "vtok", mark="bank4")
            stat0, stat1 = stat4[slot]
            t = k.dve(lambda e: e.tensor_scalar(stat1[:, 12:16], stat1[:, 12:16], small[:, 21:22], None, ALU.mult), st[1])
            for i in (3, 2, 0, 1):
                at, w = QAT[i][2], P * (i + 1)
                t1 = k.dve(lambda e: e.tensor_scalar(E1[:, at:at + w], E1[:, at:at + w], stat1[:, 12 + i:13 + i],
                                                     None, ALU.mult), t)
            for i in (3, 2, 0, 1):
                at, w = QAT[i][2], P * (i + 1)
                t2 = k.dve(lambda e: e.scalar_tensor_tensor(E0[:, at:at + w], E0[:, at:at + w], stat0[:, 12 + i:13 + i],
                                                            E1[:, at:at + w], ALU.mult, ALU.add), t1)
            k.mark(f"E{slot}1", t2)
            yield
            two = mix_values(E0, (t2,), PT2, vtok2, P, 0, (t_v,))
            k.mark(f"E{slot}0", next(two))
            yield
            t_o = next(two)
            k.mark("vtok", t_o)
            t = k.act(lambda e: e.activation(sq[0][:], bank(5), ACT.Square), t_o, "sq0")
            yield
            t = k.pe(lambda e: e.matmul(bank(4), C("ones"), sq[0][:], start=True, stop=True), t, "bank4")
            t = k.act(lambda e: e.activation(sq[0][:], bank(4), ACT.Sqrt, bias=SUB_EPS, scale=1.0 / P), t, mark="bank4")
            t = k.dve(lambda e: e.reciprocal(sq[0][:], sq[0][:]), t)
            mixed[h] = k.dve(lambda e: e.scalar_tensor_tensor(z2[:, h, :], bank(5), small[:, 22:23], sq[0][:],
                                                              ALU.mult, ALU.mult), t, mark="bank5")
            k.mark("sq0", mixed[h])
            yield
            split_mixed(h)

        def shifted(dst, src, taps, *waits, bias=None):
            if bias is not None:
                t = k.act(lambda e: e.activation(dst, src, ACT.Identity, bias=bias, scale=taps[0]), *waits)
            else:
                t = k.act(lambda e: e.activation(dst, src, ACT.Copy, scale=taps[0]), *waits)
            for d in range(1, len(taps)):
                t = k.dve(lambda e: e.scalar_tensor_tensor(dst[:, d:], src[:, 0:S - d], taps[d], dst[:, d:],
                                                           ALU.mult, ALU.add), t)
            return t

        def decay():
            n2 = slice(LCOL["lambda"], LCOL["lambda"] + 2)
            sc = [small[:, 4:6], small[:, 6:8]] + [small[:, 24 + 2 * n:26 + 2 * n] for n in range(4)]
            t = k.act(lambda e: e.activation(sc[0], lc[:, n2], ACT.Abs), "decay")
            t = k.act(lambda e: e.activation(sc[0], sc[0], ACT.Exp, scale=-1.0), t)
            t = k.dve(lambda e: e.tensor_scalar(sc[1], sc[0], 1.0, None, ALU.add), t)
            t1 = k.act(lambda e: e.activation(sc[2], sc[1], ACT.Ln), t)
            t = k.dve(lambda e: e.tensor_scalar(sc[3], sc[1], -1.0, None, ALU.add), t)
            t = k.dve(lambda e: e.tensor_scalar(sc[4], sc[3], 0.0, None, ALU.is_equal), t)
            t = k.dve(lambda e: e.tensor_tensor(sc[3], sc[3], sc[4], ALU.add), t)
            t = k.dve(lambda e: e.reciprocal(sc[3], sc[3]), t)
            t = k.dve(lambda e: e.tensor_tensor(sc[2], sc[2], sc[4], ALU.add), t, t1)
            t = k.dve(lambda e: e.tensor_tensor(sc[2], sc[2], sc[3], ALU.mult), t)
            t = k.dve(lambda e: e.tensor_tensor(sc[2], sc[2], sc[0], ALU.mult), t)
            t = k.dve(lambda e: e.tensor_scalar(sc[5], lc[:, n2], 0.0, None, ALU.min), t)
            t = k.dve(lambda e: e.tensor_tensor(sc[2], sc[2], sc[5], ALU.subtract), t)
            return k.dve(lambda e: e.tensor_scalar(sc[2], sc[2], -8.0, None, ALU.mult), t)

        def recurrence(f, t_sp, t_x, t_bd):
            nsp = small[:, 24 + f:25 + f]
            xr, r, g, a, th = (w[:] for w in W)
            t_xr = shifted(xr, z2[:, 12 + f, :], [lcol("lru_w", 2 * n + f) for n in (3, 2, 1, 0)], t_x, "W",
                           bias=lcol("lru_b", f))
            yield
            t_g1 = k.pe(lambda e: e.matmul(bank(3), bd[:, f, :], xr, start=True, stop=True), t_xr, "bank3", t_bd)
            t_r = k.act(lambda e: e.activation(r, bank(3), ACT.Sigmoid, bias=lcol("ba", f)), t_g1, mark="bank3")
            t_g2 = k.pe(lambda e: e.matmul(bank(4), bd[:, 2 + f, :], xr, start=True, stop=True), "bank4")
            t_i = k.act(lambda e: e.activation(g, bank(4), ACT.Sigmoid, bias=lcol("bx", f)), t_g2, mark="bank4")
            yield
            t_a = k.act(lambda e: e.activation(a, r, ACT.Exp, scale=nsp), t_r, t_sp)
            t_t = k.act(lambda e: e.activation(th, r, ACT.Tanh, scale=nsp), t_r)
            t1 = k.pool(lambda e: e.tensor_tensor(g, g, xr, ALU.mult), t_i)
            yield
            t = k.dve(lambda e: e.tensor_scalar(r, th, -1.0, None, ALU.add), t_t, t_a)
            t = k.dve(lambda e: e.reciprocal(r, r), t)
            t = k.dve(lambda e: e.scalar_tensor_tensor(th, th, 2.0, r, ALU.mult, ALU.mult), t)
            t = k.dve(lambda e: e.tensor_scalar(th, th, 2.0 ** -116, None, ALU.max), t)
            t = k.act(lambda e: e.activation(th, th, ACT.Sqrt), t)
            yield
            t = k.dve(lambda e: e.tensor_tensor(g, g, th, ALU.mult), t, t1)
            rec[f] = k.dve(lambda e: e.tensor_tensor_scan(z2[:, 12 + f, :], a, g, 0.0, ALU.mult, ALU.add), t, mark="W")

        def short_conv(f, t_x):
            p = z2[:, 18 + f, :]
            t = k.pool(lambda e: e.tensor_tensor(p, z2[:, 16 + f, :], p, ALU.mult), t_x)
            t = shifted(tmp[1][:], p, [lcol("sc_w", 2 * n + f) for n in (2, 1, 0)], t, "tmp1")
            yield
            mixed[4 + f] = k.dve(lambda e: e.tensor_tensor(z2[:, 14 + f, :], tmp[1][:], z2[:, 14 + f, :], ALU.mult), t,
                                 mark="tmp1")

        def gated(f, t_x):
            t = k.act(lambda e: e.activation(tmp[2][:], z2[:, 20 + f, :], ACT.Gelu_apprx_tanh), t_x, "tmp2")
            mixed[6 + f] = k.dve(lambda e: e.tensor_tensor(z2[:, 12 + f, :], tmp[2][:], z2[:, 12 + f, :], ALU.mult), t, rec[f],
                                 mark="tmp2")

        mixed, rec = {}, {}
        MIXED_AT = (0, 1, 2, 3, 14, 15, 12, 13)

        def mixed_parts(n):
            hi, lo = (4 + n, 8 + n) if n < 4 else (2 * n + 8, 2 * n + 9) if n < 6 else (n + 14, n + 16)
            return tuple(hhi[:, t, :] if t < FT else hlo[:, t - FT, :] for t in (hi, lo))

        def split_mixed(n):
            src = z2[:, MIXED_AT[n], :]
            hi, lo = mixed_parts(n)
            mixed[n] = hilo(lambda: hi, lambda: lo, src, mixed[n], *([] if n < 4 else [mixed[4], mixed[5]] if n < 6 else [mixed[6], mixed[7], "E00"]))

        def layer(l):
            t_lc = k.dma("pool", "d_lc", lc[:], lambda: layer_in[bass.ds(l, 1)].rearrange("a p n -> (a p) n"),
                         last("act"), last("dve"), last("pe"))
            t_bd = k.dma("pool", "d_bd", bd[:], lambda: lru_in[bass.ds(l, 1)].rearrange("a p b n -> (a p) b n"))
            k.mark("lc", t_lc)
            feed_forward(plain_pair, down_inputs(), lambda j: 0.5, lambda j: dyn(lc, j + LCOL["mix"]), root)

            for n in range(2):
                t = k.dve(lambda e: e.tensor_tensor(small[0:64, 16 + n:17 + n], lc[0:64, LCOL["lam"] + 2 * n:LCOL["lam"] + 2 * n + 1],
                                                    lc[0:64, LCOL["lam"] + 2 * n + 1:LCOL["lam"] + 2 * n + 2], ALU.mult), t_lc)
            t_l = t
            wide(down_inputs(), 6, into_scaled(z2), root)
            t_q = last("dve")
            t = k.pe(lambda e: e.matmul(ps[:, 5, 0:2], C("ones")[0:64, :], small[0:64, 16:18], start=True, stop=True), t_l, "bank5")
            t = k.act(lambda e: e.activation(small[:, 18:20], ps[:, 5, 0:2], ACT.Exp), t, mark="bank5")
            t = k.dve(lambda e: e.tensor_tensor(small[:, 20:21], small[:, 18:19], small[:, 19:20], ALU.subtract), t)
            t = k.dve(lambda e: e.tensor_tensor(small[:, 20:21], small[:, 20:21], lcol("lam_init"), ALU.add), t)
            t = k.dve(lambda e: e.tensor_scalar(small[:, 21:22], small[:, 20:21], -1.0, None, ALU.mult), t)
            k.dve(lambda e: e.tensor_tensor(small[:, 22:23], lcol("subln"), lcol("sub_scale"), ALU.mult))
            t_sp = decay()
            k.mark("decay", t_sp)
            ready = {}

            def projection():
                for u in range(6, 11):
                    for m in range(2):
                        quarter_of(2 * m, (6, 7))
                        yield
                        t = quarter_of(2 * m + 1, (6, 7))
                        ready[2 * u + m] = k.dve(lambda e: e.tensor_tensor(z2[:, 2 * u + m, :], bank(6 + m), rstd[:], ALU.mult),
                                                 t, mark=f"bank{6 + m}")
                        yield
                skip()
                k.mark("ahi_read", used())

            def mixers():
                for f in range(2):
                    yield from recurrence(f, t_sp, ready[12 + f], t_bd)
                    yield
                yield
                for f in range(2):
                    yield from short_conv(f, ready[18 + f])

            def finish():
                for f in range(2):
                    gated(f, ready[20 + f])
                for n in (4, 5, 6, 7):
                    yield
                    split_mixed(n)
            rest = projection()
            for _ in range(4):
                next(rest)
            for e in ("pe", "act", "dve", "pool"):
                k.wait(e, last("dve"), last("act"), t_q)
            lo_engine[0] = "pool"
            weave((0, rest), (0, head(0)), (4, head(1)), (8, head(2)), (12, head(3)), (6, mixers()), (20, finish()))

            lo_engine[0] = "dve"

            clear_sum()
            wide(mixed, U_O, residual(lambda j: 1.0, lambda j: lcol("ffn2", j)), parts=mixed_parts, urgent=True,
                 order=(0, 1, 2, 4, 5, 6, 7, 3))
            feed_forward(plain_pair, down_inputs(), lambda j: 0.5, lambda j: dyn(lc, j + LCOL["next"]), root)
        k.loop(LAYERS, layer)

        root()
        for j in range(0, DT, 2):
            for n in (j, j + 1):
                t = k.dve(lambda e: e.scalar_tensor_tensor(x[:, n, :], x[:, n, :], col("final", n), rstd[:], ALU.mult, ALU.mult),
                          "rstd", last("act"))
            k.dma("sp", f"d_out{j}", y_out[:, j:j + 2, :], x[:, j:j + 2, :], t)
        for j in range(0, DT, 2):
            nc.sync.wait_ge(k.sem(f"d_out{j}"), 16)
        for s in range(2):
            nc.sync.wait_ge(k.sem(f"ld{s}"), 16 * (U_ALL // 2))
    return sorted(ada_at)


def blocks_of(w, order):
    out = np.zeros((len(order), P, P), w.dtype)
    for n, b in enumerate(order):
        if b is not None:
            kt, c, width = b
            out[n, :, :width] = w[kt * P:(kt + 1) * P, c:c + width]
    return out


def wide_order(n, first=0):
    return [(kt, first + 256 * u + P * m, P) for u in range(n) for kt in range(DT) for m in range(2)]


def down_order():
    order = []
    for pair in range(4):
        for part in range(3):
            blocks = [(8 * part + kt, 256 * pair + P * m, P) for kt in range(min(8, FT - 8 * part)) for m in range(2)]
            order += blocks + [None] * (UB - len(blocks))
    return order


def ada_units(v, first, end):
    order = wide_order(end - first, 256 * first)
    return np.ascontiguousarray(blocks_of(v["w_ada"][0], order).reshape(-1, UB, P, P).transpose(0, 2, 1, 3))


def stream_of(v, ada_at):
    parts = []
    w = v["w_in"][0]
    parts.append(blocks_of(w, wide_order(3)))
    parts.append(blocks_of(v["w_q_b"][0], [(kt, 96 * (4 * u + h), 96) for u in range(2) for kt in range(4) for h in range(4)]))
    parts.append(blocks_of(v["w_kv_b"][0], [(kt, P * h, P) for kt in range(2) for h in range(8)]))
    order = wide_order(4, 800)
    for kt in range(DT):
        order += [(kt, 704, 96), None]
    parts.append(blocks_of(w, order + wide_order(2, 1824)))
    parts.append(blocks_of(v["w_o"][0], wide_order(4)))

    def pairs(a, b, off):
        for j in range(HALF):
            order = [(kt, 256 * j + P * m, P) for kt in range(DT) for m in range(2)]
            parts.append(blocks_of(a, order))
            parts.append(blocks_of(b, [(kt, c + off, w) for kt, c, w in order]))
    pairs(v["w_up"][0], v["w_up"][0], FF)
    parts.append(blocks_of(v["w_down"][0], down_order()))
    parts.append(np.zeros((U_PAD * UB, P, P), np.float32))
    tiles = list(range(12)) + [18, 19] + list(range(12, 18)) + [20, 21]
    in2 = [(kt, P * tiles[2 * u + m], P) for u in range(11) for kt in range(DT) for m in range(2)]
    for l in range(LAYERS):
        for n in (1, 2):
            if n == 2:
                parts.append(blocks_of(v["w_in_2"][l], in2 + [None] * UB))
                parts.append(blocks_of(v["w_out_2"][l], wide_order(4)))
            pairs(v[f"ffn{n}_gate_2"][l], v[f"ffn{n}_up_2"][l], 0)
            parts.append(blocks_of(v[f"ffn{n}_down_2"][l], down_order()))
    parts.append(np.zeros((2 * UB, P, P), np.float32))
    rest = np.concatenate(parts).reshape(-1, UB, P, P)
    s = np.empty((U_ALL, P, UB, P), np.float32)
    s[ada_at] = ada_units(v, ADA_EARLY, U_ADA)
    s[np.setdiff1d(np.arange(U_ALL), ada_at)] = rest.transpose(0, 2, 1, 3)
    return s


def columns_of(plan, n, vectors):
    out = np.zeros((P, n), np.float32)
    for name, a in vectors.items():
        a = np.asarray(a).reshape(-1)
        w = -(-a.size // P)
        full = np.zeros(w * P, a.dtype)
        full[:a.size] = a
        out[:, plan[name]:plan[name] + w] = full.reshape(w, P).T
    return out


def constants():
    ident = np.eye(P)
    ones = np.ones((P, P))
    blk64 = np.kron(np.eye(2), np.ones((64, 64)) / 64)
    blkq = np.zeros((P, P))
    blkq[:64, :64] = 1 / 64
    blkq[64:96, 64:96] = 1 / 32
    def swap(m, at, half):
        for j in range(half):
            m[at + half + j, at + j] = -1
            m[at + j, at + half + j] = 1
    perm64, permq = np.zeros((P, P)), np.zeros((P, P))
    swap(perm64, 0, 32)
    swap(perm64, 64, 32)
    swap(permq, 64, 16)
    const = np.concatenate([ident, ones, blk64, blkq, perm64, permq], 1).astype(np.float32)
    dist = np.arange(P)[:, None] - np.arange(S)[None] + 384
    causal = np.where(dist >= 0, 0.0, NEG)
    times = ((dist >= 0) & (dist <= 128)).astype(int) + ((dist >= 0) & (dist % 4 == 0)) + ((dist >= 0) & (dist % 16 == 0))
    dil = np.where(times > 0, 8.0 * np.log(np.maximum(times, 1)), NEG)
    strips = np.stack([causal, dil]).astype(np.float32)
    d = 511 - np.arange(640)
    n = np.maximum(d, 0)
    nf = np.maximum(n, 1).astype(np.float32)
    large = 16 + (np.log(nf / np.float32(16)) / np.float32(math.log(8)) * np.float32(16)).astype(np.int32)
    bucket = np.where(n < 16, n, np.minimum(large, 31))
    table = np.zeros((P, 1280 + P), np.float32)
    table[:32, :640] = bucket[None] == np.arange(32)[:, None]
    table[:8, 640:1280] = np.where(d >= 0, 0.0, NEG)[None]
    table[:, 1280:] = np.eye(P)[::-1]
    return const, strips, table


def kernel(**inputs):
    import concourse.bacc as _bacc
    from concourse.bass_utils import run_bass_kernel_spmd as _run

    v = {name: np.asarray(a) for name, a in inputs.items()}
    const, strips, table = constants()
    freq = {d: (10000.0 ** (-2.0 * np.arange(d // 2) / d)).astype(np.float32) for d in (32, 64)}
    freq_mla = np.zeros(P, np.float32)
    freq_mla[64:96] = np.tile(freq[32], 2)
    cols = columns_of(COL, NCOL, {
        "c": v["c"], "b_ada": v["b_ada"], "g_mix": v["g_mix_norm"], "g_q_lat": v["g_q_lat"], "g_kv_lat": v["g_kv_lat"],
        "g_q": np.concatenate([v["g_mla_q_nope"][0], v["g_mla_q_pe"][0]]),
        "g_k": np.concatenate([v["g_mla_k_nope"][0], v["g_mla_k_pe"][0]]),
        "g_dq": np.tile(v["g_dil_q"][0], 2), "g_dk": np.tile(v["g_dil_k"][0], 2), "g_ffn": v["g_ffn_norm"],
        "w_conv0": v["w_conv"][0, 0], "w_conv1": v["w_conv"][0, 1], "w_conv2": v["w_conv"][0, 2], "b_conv": v["b_conv"],
        "final": v["final_norm_2"], "ffn1_0": v["ffn1_norm_2"][0], "freq_dil": np.tile(freq[64], 4), "freq_mla": freq_mla})
    layers = []
    lru = np.zeros((LAYERS, P, 4, P), np.float32)
    for l in range(LAYERS):
        lam = np.zeros((4, P), np.float32)
        for n, name in enumerate(("lam_q1_2", "lam_k1_2", "lam_q2_2", "lam_k2_2")):
            lam[n, :64] = v[name][l]
        lam_init = 0.8 - 0.6 * math.exp(-0.3 * l)
        layers.append(columns_of(LCOL, NLCOL, {
            "ffn1": v["ffn1_norm_2"][l], "mix": v["mix_norm_2"][l], "ffn2": v["ffn2_norm_2"][l],
            "next": v["ffn1_norm_2"][l + 1] if l + 1 < LAYERS else v["final_norm_2"],
            "subln": v["subln_gain_2"][l], "sc_w": v["sc_conv_w_2"][l], "lru_w": v["lru_conv_w_2"][l],
            "lru_b": v["lru_conv_b_2"][l], "lambda": v["lru_lambda_2"][l], "ba": v["lru_ba_2"][l],
            "bx": v["lru_bx_2"][l], "lam": lam, "lam_init": np.full(P, lam_init), "sub_scale": np.full(P, 1.0 - lam_init)}))
        for n, name in enumerate(("lru_wa_2", "lru_wx_2")):
            for b in range(4):
                at = 64 * (b % 2)
                lru[l, at:at + 64, 2 * n + b // 2, at:at + 64] = v[name][l, b]
    arrays = {
        "wstream": np.zeros((1,), np.float32),
        "ada_in": ada_units(v, 0, ADA_EARLY),
        "x_in": np.ascontiguousarray(v["x"][0].T.reshape(DT, P, S).transpose(1, 0, 2)),
        "pos_in": v["positions"],
        "cols_in": cols,
        "layer_in": np.stack(layers),
        "const_in": const,
        "strip_in": strips,
        "bucket_in": table,
        "rel_in": v["rel_bias_2"],
        "lru_in": lru,
    }
    nc = _bacc.Bacc("TRN2", target_bir_lowering=False, num_devices=1)
    shapes = {name: a.shape for name, a in arrays.items()}
    shapes["wstream"] = (U_ALL, P, UB, P)
    args = [nc.dram_tensor(name, shapes[name], mybir.dt.from_np(a.dtype), kind="ExternalInput").ap() for name, a in arrays.items()]
    args.append(nc.dram_tensor("y_out", (P, DT, S), F32, kind="ExternalOutput").ap())
    arrays["wstream"] = stream_of(v, build(nc, *args))
    r = _run(nc, [arrays], core_ids=[0])
    y = r.results[0]["y_out"]
    return np.ascontiguousarray(y.transpose(1, 0, 2).reshape(D, S).T)[None]
```
